# Optimizing a Trainium2 kernel written in Bass

```python
import jax, jax.numpy as jnp
from jax import lax
import numpy as np

D_MODEL = 1024
BATCH = 1
SEQ = 256
DEPTH = 1
DEC_BATCH = 8
DEC_SEQ = 1
PAST_LEN = 2048
PAGE_SIZE = 128

N_BRANCH = 4
BR_WIDTH = D_MODEL // 2
N_GROUPS = 4
GROUP_CH = BR_WIDTH // N_GROUPS
CHUNK = 128
CONV_B_WIDTH = 3
POOL_WINDOWS = (2, 4, 8, 16)
POOL_STATE = max(POOL_WINDOWS) - 1
CONF_WIDTH = 31
N_EXPERTS = 64
TOP_K = 8
N_EXPERT_GROUPS = 8
TOPK_GROUPS = 4
D_EXPERT = D_MODEL // 4
D_SHARED = D_EXPERT
ROUTED_SCALE = 2.5
EPS = 1e-6

A_COLS = 2 * BR_WIDTH
B_COLS = 3 * BR_WIDTH
C_COLS = BR_WIDTH
D_COLS = 2 * BR_WIDTH
G_COLS = N_BRANCH * D_MODEL
IN_COLS = A_COLS + B_COLS + C_COLS + D_COLS + G_COLS
IN_SPLITS = (A_COLS, A_COLS + B_COLS, A_COLS + B_COLS + C_COLS, A_COLS + B_COLS + C_COLS + D_COLS)

kernel_name = "hybrid_gated_conv_pool_chunkmlp_moe_decoder_step"

def rmsnorm(x, g):
    x32 = x.astype(jnp.float32)
    y = x32 * lax.rsqrt(jnp.mean(x32 * x32, axis=-1, keepdims=True) + EPS)
    return (y * g.astype(jnp.float32)).astype(x.dtype)

def layernorm(x, g, b):
    x32 = x.astype(jnp.float32)
    mu = jnp.mean(x32, axis=-1, keepdims=True)
    xc = x32 - mu
    var = jnp.mean(xc * xc, axis=-1, keepdims=True)
    return (xc * lax.rsqrt(var + EPS) * g.astype(jnp.float32) + b.astype(jnp.float32)).astype(x.dtype)

def causal_depthwise_conv(x, prev, w):
    xp = jnp.concatenate([prev.astype(x.dtype), x], axis=1)
    y = lax.conv_general_dilated(xp, w[:, None, :].astype(x.dtype), (1,), 'VALID',
                                 dimension_numbers=('NWC', 'WIO', 'NWC'),
                                 feature_group_count=x.shape[-1])
    return y, xp[:, -(w.shape[0] - 1):]

def chunk_spatial_gate(v, w_s, b_s):
    bsz, t, c = v.shape
    n_chunks = -(-t // CHUNK)
    pad = n_chunks * CHUNK - t
    vp = jnp.pad(v, ((0, 0), (0, pad), (0, 0))).reshape(bsz, n_chunks, CHUNK, N_GROUPS, GROUP_CH)
    mask = jnp.tril(jnp.ones((CHUNK, CHUNK), dtype=bool))
    w = jnp.where(mask[None], w_s, 0).astype(v.dtype)
    s = jnp.einsum('gpq,bnqgc->bnpgc', w, vp) + jnp.transpose(b_s)[None, None, :, :, None].astype(v.dtype)
    return s.reshape(bsz, n_chunks * CHUNK, c)[:, :t]

def multi_scale_pool(p, prev, start_pos):
    bsz, t, c = p.shape
    xp = jnp.concatenate([prev.astype(p.dtype), p], axis=1)
    cs = jnp.pad(jnp.cumsum(xp.astype(jnp.float32), axis=1), ((0, 0), (1, 0), (0, 0)))
    end = cs[:, POOL_STATE + 1:]
    pos = start_pos + jnp.arange(t)
    outs = []
    for g, win in enumerate(POOL_WINDOWS):
        sl = slice(g * GROUP_CH, (g + 1) * GROUP_CH)
        s0 = POOL_STATE + 1 - win
        wsum = end[:, :, sl] - cs[:, s0:s0 + t, sl]
        cnt = jnp.minimum(win, pos + 1).astype(jnp.float32)[None, :, None]
        outs.append(wsum / cnt)
    mean = jnp.concatenate(outs, axis=-1)
    return (mean - p.astype(jnp.float32)).astype(p.dtype), xp[:, -POOL_STATE:]

def token_mixer(h, conv_prev, pool_prev, conf_prev, start_pos, w_in, sgu_ln_g, sgu_ln_b, sgu_w, sgu_b,
                conv_w, pool_w, pool_scale, conf_w, conf_b, conf_ln_g, conf_ln_b, w_branch, w_out):
    bsz, t, _ = h.shape
    z = h @ w_in
    za, zb, zc, zd, zg = jnp.split(z, IN_SPLITS, axis=-1)
    u, v = jnp.split(jax.nn.gelu(za, approximate=False), 2, axis=-1)
    v = layernorm(v, sgu_ln_g, sgu_ln_b)
    ya = u * chunk_spatial_gate(v, sgu_w, sgu_b)
    gate_b, gate_c, hb = jnp.split(zb, 3, axis=-1)
    conv_out, conv_state = causal_depthwise_conv(gate_c * hb, conv_prev, conv_w)
    yb = gate_b * conv_out
    pooled, pool_state = multi_scale_pool(zc, pool_prev, start_pos)
    yc = jnp.einsum('btgc,gcd->btgd', pooled.reshape(bsz, t, N_GROUPS, GROUP_CH), pool_w)
    yc = yc.reshape(bsz, t, BR_WIDTH) * pool_scale
    a, b = jnp.split(zd, 2, axis=-1)
    glu = a * jax.nn.sigmoid(b)
    dconv, conf_state = causal_depthwise_conv(glu, conf_prev, conf_w)
    yd = jax.nn.silu(layernorm(dconv + conf_b, conf_ln_g, conf_ln_b))
    branches = jnp.stack([ya, yb, yc, yd], axis=2)
    proj = jnp.einsum('btkc,kcd->btkd', branches, w_branch)
    gates = jax.nn.sigmoid(zg.reshape(bsz, t, N_BRANCH, D_MODEL))
    merged = jnp.sum(gates * proj, axis=2)
    return merged @ w_out, (conv_state, pool_state, conf_state, v)

def moe_ffn(h, router_w, router_bias, e_gate, e_up, e_down, s_gate, s_up, s_down):
    n = h.shape[0]
    scores = jax.nn.sigmoid((h @ router_w).astype(jnp.float32))
    biased = scores + router_bias.astype(jnp.float32)
    grp = biased.reshape(n, N_EXPERT_GROUPS, N_EXPERTS // N_EXPERT_GROUPS)
    grp_score = jnp.sum(lax.top_k(grp, 2)[0], axis=-1)
    _, grp_idx = lax.top_k(grp_score, TOPK_GROUPS)
    grp_mask = jnp.sum(jax.nn.one_hot(grp_idx, N_EXPERT_GROUPS, dtype=jnp.float32), axis=1) > 0
    expert_mask = jnp.repeat(grp_mask, N_EXPERTS // N_EXPERT_GROUPS, axis=1)
    _, idx = lax.top_k(jnp.where(expert_mask, biased, -jnp.inf), TOP_K)
    w = jnp.take_along_axis(scores, idx, axis=1)
    w = w / jnp.sum(w, axis=-1, keepdims=True) * ROUTED_SCALE
    gates = jnp.zeros((n, N_EXPERTS), jnp.float32).at[jnp.arange(n)[:, None], idx].set(w)
    hg = jnp.einsum('nd,edf->nef', h, e_gate)
    hu = jnp.einsum('nd,edf->nef', h, e_up)
    act = jax.nn.silu(hg) * hu * gates[:, :, None].astype(h.dtype)
    routed = jnp.einsum('nef,efd->nd', act, e_down)
    shared = (jax.nn.silu(h @ s_gate) * (h @ s_up)) @ s_down
    return routed + shared

def decoder_layer(x, c, conv_prev, pool_prev, conf_prev, start_pos, per_sequence_moe,
                  ada_w, ada_b, norm1_g, norm2_g, w_in, sgu_ln_g, sgu_ln_b, sgu_w, sgu_b,
                  conv_w, pool_w, pool_scale, conf_w, conf_b, conf_ln_g, conf_ln_b,
                  w_branch, w_out, router_w, router_bias, e_gate, e_up, e_down,
                  s_gate, s_up, s_down):
    mod = (jax.nn.silu(c) @ ada_w + ada_b)[:, None, :]
    shift1, scale1, gate1, shift2, scale2, gate2 = jnp.split(mod, 6, axis=-1)
    h = rmsnorm(x, norm1_g) * (1 + scale1) + shift1
    mix, new_states = token_mixer(h, conv_prev, pool_prev, conf_prev, start_pos, w_in, sgu_ln_g, sgu_ln_b,
                                  sgu_w, sgu_b, conv_w, pool_w, pool_scale, conf_w, conf_b,
                                  conf_ln_g, conf_ln_b, w_branch, w_out)
    x = x + gate1 * mix
    h = rmsnorm(x, norm2_g) * (1 + scale2) + shift2
    moe = lambda tok: moe_ffn(tok, router_w, router_bias, e_gate, e_up, e_down, s_gate, s_up, s_down)
    if per_sequence_moe:
        f = lax.map(moe, h)
    else:
        f = moe(h.reshape(-1, D_MODEL)).reshape(h.shape)
    x = x + gate2 * f
    return x, new_states

def setup_inputs(seed: int = 0) -> dict:
    key = jax.random.key(seed)
    ks = iter(jax.random.split(key, 48))
    f32 = jnp.float32

    def nrm(shape, scale):
        return jax.random.normal(next(ks), shape, f32) * scale

    def gain(shape):
        return 1.0 + nrm(shape, 0.05)

    L = DEPTH
    return {
        "x_prompt": nrm((BATCH, SEQ, D_MODEL), 1.0),
        "x_sample": nrm((DEC_BATCH, DEC_SEQ, D_MODEL), 1.0),
        "state_conv": nrm((L, DEC_BATCH, CONV_B_WIDTH - 1, BR_WIDTH), 1.0),
        "state_pool": nrm((L, DEC_BATCH, POOL_STATE, BR_WIDTH), 1.0),
        "state_conf": nrm((L, DEC_BATCH, CONF_WIDTH - 1, BR_WIDTH), 0.5),
        "c_prompt": nrm((BATCH, D_MODEL), 1.0),
        "c_sample": nrm((DEC_BATCH, D_MODEL), 1.0),
        "ada_w": nrm((L, D_MODEL, 6 * D_MODEL), 0.5 * D_MODEL ** -0.5),
        "ada_b": nrm((L, 6 * D_MODEL), 0.02),
        "norm1_g": gain((L, D_MODEL)),
        "norm2_g": gain((L, D_MODEL)),
        "w_in": nrm((L, D_MODEL, IN_COLS), D_MODEL ** -0.5),
        "sgu_ln_g": gain((L, BR_WIDTH)),
        "sgu_ln_b": nrm((L, BR_WIDTH), 0.02),
        "sgu_w": nrm((L, N_GROUPS, CHUNK, CHUNK), CHUNK ** -0.5),
        "sgu_b": 1.0 + nrm((L, N_GROUPS, CHUNK), 0.02),
        "conv_w": nrm((L, CONV_B_WIDTH, BR_WIDTH), CONV_B_WIDTH ** -0.5),
        "pool_w": nrm((L, N_GROUPS, GROUP_CH, GROUP_CH), GROUP_CH ** -0.5),
        "pool_scale": 1.0 + nrm((L, BR_WIDTH), 0.1),
        "conf_w": nrm((L, CONF_WIDTH, BR_WIDTH), CONF_WIDTH ** -0.5),
        "conf_b": nrm((L, BR_WIDTH), 0.02),
        "conf_ln_g": gain((L, BR_WIDTH)),
        "conf_ln_b": nrm((L, BR_WIDTH), 0.02),
        "w_branch": nrm((L, N_BRANCH, BR_WIDTH, D_MODEL), BR_WIDTH ** -0.5),
        "w_out": nrm((L, D_MODEL, D_MODEL), D_MODEL ** -0.5),
        "router_w": nrm((L, D_MODEL, N_EXPERTS), D_MODEL ** -0.5),
        "router_bias": nrm((L, N_EXPERTS), 0.01),
        "e_gate": nrm((L, N_EXPERTS, D_MODEL, D_EXPERT), D_MODEL ** -0.5),
        "e_up": nrm((L, N_EXPERTS, D_MODEL, D_EXPERT), D_MODEL ** -0.5),
        "e_down": nrm((L, N_EXPERTS, D_EXPERT, D_MODEL), D_EXPERT ** -0.5),
        "s_gate": nrm((L, D_MODEL, D_SHARED), D_MODEL ** -0.5),
        "s_up": nrm((L, D_MODEL, D_SHARED), D_MODEL ** -0.5),
        "s_down": nrm((L, D_SHARED, D_MODEL), D_SHARED ** -0.5),
        "final_g": gain((D_MODEL,)),
    }

def reference(x_prompt, x_sample, state_conv, state_pool, state_conf, c_prompt, c_sample,
              ada_w, ada_b, norm1_g, norm2_g, w_in, sgu_ln_g, sgu_ln_b, sgu_w, sgu_b,
              conv_w, pool_w, pool_scale, conf_w, conf_b, conf_ln_g, conf_ln_b,
              w_branch, w_out, router_w, router_bias, e_gate, e_up, e_down,
              s_gate, s_up, s_down, final_g):
    bp = x_prompt.shape[0]
    dt = x_prompt.dtype
    yp, ys = x_prompt, x_sample
    conv_p, pool_p, conf_p = [], [], []
    conv_s, pool_s, conf_s, chunk_v_s = [], [], [], []
    for l in range(DEPTH):
        lw = (ada_w[l], ada_b[l], norm1_g[l], norm2_g[l], w_in[l], sgu_ln_g[l], sgu_ln_b[l], sgu_w[l], sgu_b[l],
              conv_w[l], pool_w[l], pool_scale[l], conf_w[l], conf_b[l], conf_ln_g[l], conf_ln_b[l],
              w_branch[l], w_out[l], router_w[l], router_bias[l], e_gate[l], e_up[l], e_down[l],
              s_gate[l], s_up[l], s_down[l])
        yp, (cp, pp, fp, _) = decoder_layer(
            yp, c_prompt,
            jnp.zeros((bp, CONV_B_WIDTH - 1, BR_WIDTH), dt),
            jnp.zeros((bp, POOL_STATE, BR_WIDTH), dt),
            jnp.zeros((bp, CONF_WIDTH - 1, BR_WIDTH), dt),
            0, True, *lw)
        ys, (cs, ps, fs, vs) = decoder_layer(
            ys, c_sample, state_conv[l], state_pool[l], state_conf[l], PAST_LEN, False, *lw)
        conv_p.append(cp); pool_p.append(pp); conf_p.append(fp)
        conv_s.append(cs); pool_s.append(ps); conf_s.append(fs); chunk_v_s.append(vs)
    y_prompt = rmsnorm(yp, final_g)
    y_sample = rmsnorm(ys, final_g)
    return (y_prompt, y_sample,
            jnp.stack(conv_p), jnp.stack(pool_p), jnp.stack(conf_p),
            jnp.stack(conv_s), jnp.stack(pool_s), jnp.stack(conf_s), jnp.stack(chunk_v_s))


_drawn_inputs = setup_inputs


def setup_inputs(seed=0):
    import zlib

    import numpy as np

    out = dict(_drawn_inputs(seed))
    spreads = {}
    factors = {'sgu_ln_b': 2.867,
     'sgu_b': 73.274,
     'conf_b': 4.214,
     'conf_ln_g': 18.982,
     'conf_ln_b': 38.515,
     'pool_scale': 10.096,
     'norm2_g': 3.296,
     'router_bias': 3.559}
    for name, (base, spread) in spreads.items():
        noise = np.random.default_rng([zlib.crc32(name.encode()), seed]).standard_normal(out[name].shape)
        drawn = base * np.exp(spread * noise) if base else spread * noise
        out[name] = __import__('jax').numpy.asarray(drawn.astype(out[name].dtype))
    for name, factor in factors.items():
        out[name] = (out[name] * factor).astype(out[name].dtype)
    return out
```

```python
from contextlib import ExitStack

import numpy as np

import concourse.bass as bass
from concourse import mybir

F32 = mybir.dt.float32
I32 = mybir.dt.int32
ALU = mybir.AluOpType
ACT = mybir.ActivationFunctionType
AX = mybir.AxisListType

P = 128
D = 1024
KT = D // P
BR = D // 2
CT = BR // P
SEQ = 256
NS = 8
TOK = SEQ + NS
TILES = [(0, P), (P, P), (2 * P, NS)]
NC_ROWS = NS + 1
HC, HP, HF = 2, 15, 30
NE = 64
NG = 8
TOPG = 4
FE = D // 4
EPS = 1e-6
ROUTED_SCALE = 2.5
BLK = 512
RING = 3
NBANK = 8

R_CONFW, R_CONVW, R_CONFB, R_CLNG, R_CLNB, R_PSC, R_N1G = 0, 31, 34, 35, 36, 37, 38
NPROW = 40

BLOCKS = ([("ada", j) for j in range(4)]
          + [("win", j) for j in (1, 7, 6, 3, 4, 5, 2, 0)]
          + [("ada", j) for j in range(4, 12)]
          + [x for k in (2, 1, 0, 3) for x in (("win", 8 + 2 * k), ("win", 9 + 2 * k), ("br", k))]
          + [("out", 0), ("out", 1)])
SLOT = {b: i for i, b in enumerate(BLOCKS)}
BR_ORDER = (2, 1, 0, 3)


def jobs_of_mixer():
    out = ["cT", "prow0", "wsT"]
    out += [("hist", n) for n in range(4)]
    for kind, j in BLOCKS:
        if kind == "ada":
            out.append(("ada", j))
            if j == 3:
                out.append("modT")
                out += [("hT", k) for k in range(KT)]
            if j in (5, 7, 9, 11):
                out += [("bc", (j - 4) // 2, h) for h in range(2)]
        elif kind == "win" and j == 1:
            out += [("v", t) for t in range(3)]
        elif kind == "win" and j < 8:
            out += [("z", j, c) for c in range(CT)]
            if j == 6:
                out.append("st_conf")
            if j == 4:
                out.append("st_conv")
            if j == 5:
                out.append("st_pool")
            if j == 0:
                out += [("sg", g) for g in range(CT)]
                out += [("pw", g) for g in range(CT)]
        elif kind == "win":
            k, half = (j - 8) // 2, (j - 8) % 2
            if half == 0:
                out += {0: ["cmean"], 3: ["cvar"]}.get(k, [])
            out += [("zg", k, 4 * half + c) for c in range(CT)]
        elif kind == "br":
            out += [("pr", j, d) for d in range(KT)]
        else:
            out += [("mix", j, t) for t in range(3)]
    out += [("h2T", k) for k in range(KT)]
    out += ["logit", ("sgu", 0), ("sgu", 1), "slot"]
    for t in range(3):
        out += [("saT", t)] + [("sgu", 2)] * (t == 0) + [("sy", t, 0), ("sy", t, 1)]
    return out


JOBS = jobs_of_mixer()
JOB = {name: i for i, name in enumerate(JOBS)}


def bank_of(name):
    return JOB[name] % NBANK, JOB[name] // NBANK


LAST_JOB = {}
for _kind, _j in BLOCKS:
    if _kind == "ada":
        LAST_JOB["ada", _j] = ("ada", _j)
    elif _kind == "br":
        LAST_JOB["br", _j] = ("pr", _j, KT - 1)
    elif _kind == "out":
        LAST_JOB["out", _j] = ("mix", _j, 2)
    elif _j == 1:
        LAST_JOB["win", 1] = ("v", 2)
    elif _j < 8:
        LAST_JOB["win", _j] = ("z", _j, CT - 1)
    else:
        LAST_JOB["win", _j] = ("zg", (_j - 8) // 2, 4 * ((_j - 8) % 2) + CT - 1)

BIG = 4096.0
CAP = P
ROUNDS = -(-TOK // CAP)
UNROLL = 4
NPARAM = 8
SLOTF = 2 * KT * FE + 2 * D


def bass_decoder_step(nc, x_prompt, x_sample, state_conv, state_pool, state_conf, c_prompt, c_sample,
                      ada_w, ada_b, norm1_g, norm2_g, w_in, sgu_ln_g, sgu_ln_b, sgu_w, sgu_b,
                      conv_w, pool_w, pool_scale, conf_w, conf_b, conf_ln_g, conf_ln_b,
                      w_branch, w_out, router_w, router_bias, e_gate, e_up, e_down,
                      s_gate, s_up, s_down, final_g,
                      y_prompt, y_sample, conv_p, pool_p, conf_p, conv_s, pool_s, conf_s, chunk_v_s,
                      h_table, y_table):
    with ExitStack() as ctx:
        def sb(name, shape, dt=F32):
            return ctx.enter_context(nc.sbuf_tensor(name, shape, dt))

        def sem(name):
            return ctx.enter_context(nc.semaphore(name))

        psum = ctx.enter_context(nc.psum_tensor("psum", [P, NBANK, 512], F32))

        wexp = sb("wexp", [P, UNROLL, SLOTF])
        ring = wexp[:, 2:4, :].rearrange("p a n -> p (a n)").rearrange("p (s n) -> p s n", s=RING)
        early = wexp[:, 0:2, :].rearrange("p a n -> p (a n)")
        used = [0]

        def take(n):
            at = used[0]
            used[0] += n
            assert used[0] <= 2 * SLOTF
            return early[:, at:at + n]

        sg = take(KT * TOK).rearrange("p (k t) -> p k t", k=KT)
        ybr = take(4 * CT * TOK).rearrange("p (b c t) -> p b c t", b=4, c=CT)
        tmpT = take(CT * TOK).rearrange("p (c t) -> p c t", c=CT)
        gluP = take(CT * (HF + TOK)).rearrange("p (c t) -> p c t", c=CT)
        zcP = take(CT * (HP + TOK)).rearrange("p (c t) -> p c t", c=CT)
        cgP = take(CT * (HC + TOK)).rearrange("p (c t) -> p c t", c=CT)
        convH = take(CT * NS * HC).rearrange("p (c s h) -> p c s h", c=CT, h=HC)
        poolH = take(CT * NS * HP).rearrange("p (c s h) -> p c s h", c=CT, h=HP)
        confH = take(CT * NS * HF).rearrange("p (c s h) -> p c s h", c=CT, h=HF)

        x_sb = sb("x_sb", [P, 3, D])
        xn = sb("xn", [P, 3, D])
        hT = sb("hT", [P, KT, TOK])
        mod = sb("mod", [NC_ROWS, 4 * D])
        bc = sb("bc", [P, 4, D])
        mT = sb("mT", [P, KT, TOK])
        mid = sb("mid", [P, 5 * D + 64])
        dcv = mid[:, 0:CT * TOK].rearrange("p (c t) -> p c t", c=CT)
        v_sb = mid[:, 1056:2592].rearrange("p (t c) -> p t c", t=3)
        lnv = mid[:, 2592:3616].rearrange("p (a c) -> p a c", a=2)
        sgub = mid[:, 3616:4128].rearrange("p (g q) -> p g q", g=CT)
        poolw = mid[:, 4128:4640].rearrange("p (g q) -> p g q", g=CT)
        wsT = mid[:, 4640:5152].rearrange("p (g q) -> p g q", g=CT)
        crow = mid[0:NC_ROWS, 0:D]
        shared = mid[:, 0:3 * D].rearrange("p (t d) -> p t d", t=3)
        xgT = mid[:, 3 * D:5 * D].rearrange("p (b k c) -> p b k c", b=2, k=KT)
        w00 = sb("w00", [NS, CT])
        wdiag = sb("wdiag", [NS, CT, NS])
        rtw = sb("rtw", [P, KT, NE])
        rtb = sb("rtb", [P, NE])
        cT = sb("cT", [P, KT, NC_ROWS])
        prm = sb("prm", [P, CT, NPROW])
        S1 = sb("S1", [P, KT, NC_ROWS])
        G1 = sb("G1", [P, KT, NC_ROWS])
        ident = sb("ident", [P, P])
        lower = sb("lower", [P, P])
        iota_i = sb("iota_i", [P, P], I32)
        iota_f = sb("iota_f", [P, P])
        ones = sb("ones", [P, P])
        cmean = sb("cmean", [P, P])
        sel8 = sb("sel8", [NC_ROWS, P])
        rc = sb("rc", [P, 16])
        st = sb("st", [P, 3, 8])
        bns = sb("bns", [P, 3, 8])
        sc = sb("sc", [P, 3, NE])
        bsd = sb("bsd", [P, 3, NE])
        msk = sb("msk", [P, 3, NE])
        sel = sb("sel", [P, 3, NE])
        rnk = sb("rnk", [P, 3, NE])
        posm = sb("posm", [P, 3, NE])
        tab = sb("tab", [P, 3, NE, 3])
        cmp2 = sb("cmp2", [P, 3, NG, NG])
        tok8 = sb("tok8", [P, 3])
        epsc = sb("epsc", [P, 1])
        gm = sb("gm", [P, 3, NG, 8])
        gs = sb("gs", [P, 3, NG])
        cmp_ = sb("cmp_", [P, 3, NG, NG])
        trig = sb("trig", [P, NG, NG])
        tokid = sb("tokid", [P, 3])
        valid = sb("valid", [P, 3])
        cnt_f = sb("cnt_f", [P, 1])
        cnt_i = sb("cnt_i", [P, 1], I32)
        lst = sb("lst", [P, 4])
        idx = sb("idx", [P, UNROLL, 3], I32)
        gcol = sb("gcol", [P, UNROLL, 1])
        hist = mT[:, :, :].rearrange("p k t -> p (k t)")[:, 0:4 * BR].rearrange("p (n c) -> p n c", n=4)
        hTf = hT[:, :, :].rearrange("p k t -> p (k t)")
        prow = hTf[0:NPROW, 0:BR]
        wsr = hTf[:, BR:2 * BR].rearrange("p (g q) -> p g q", g=CT)
        st_rows = bc[:, 3, :].rearrange("p (a c) -> p a c", a=2)
        st_conf, st_conv, st_pool = st_rows[:, 0, :], st_rows[:, 1, :], bc[:, 1, 0:BR]
        y_rows = mT[:, :, :].rearrange("p k t -> p (k t)")[:, 0:2 * D].rearrange("p (b d) -> p b d", b=2)
        xg = xn[:, 0:2, :]
        xnf = xn[:, :, :].rearrange("p t d -> p (t d)")
        sums = xnf[:, 0:544].rearrange("p (a n) -> p a n", a=2)
        prod = xnf[:, 544:784].rearrange("p (s h) -> p s h", s=NS)
        stat = xnf[:, 784:784 + 2 * TOK].rearrange("p (a t) -> p a t", a=2)
        silu = hTf[:, 0:512].rearrange("p (b f) -> p b f", b=2)
        act = hTf[:, 512:1024].rearrange("p (b f) -> p b f", b=2)
        actT = hTf[:, 1024:1536].rearrange("p (b j c) -> p b j c", b=2, j=2)
        mTf = mT[:, :, :].rearrange("p k t -> p (k t)")
        sh_act = mTf[:, 0:256]
        sh_actT = mTf[:, 256:512].rearrange("p (j c) -> p j c", j=2)
        sh_silu = mTf[:, 512:768]
        fing = bc[:, 0, :]
        oh = bc[:, 1, 0:6 * P].rearrange("p (b t c) -> p b t c", b=2, t=3)

        bank_full = [sem(f"bank_full{b}") for b in range(NBANK)]
        bank_free = [sem(f"bank_free{b}") for b in range(NBANK)]
        ring_full = [sem(f"ring_full{s}") for s in range(RING)]
        names = """cnt_ready ld_mod2 mrg_ready sh_load dn_done x_xt x_w moe_done fin_ready
                   out_done pool_chain consts ld_stage wg_masked states_done v_ready st_stored h2_ready
                   h2_stored x2_ready ld_fin lst_ready xt_done dma_may_go ys_act ys_dve x_idx
                   x_gat x_y x_sc c_silu x_norm h_ready ws_ready ld_param pooled_ready
                   g2_rows dconv_ready sq_ready ya_ready sel_ready oh_ready list_done xgt_act xgt_dve
                   act_ready gu_done actT_ready tact_done x_oh x_list x_xgt x_gu x_act
                   x_tact x_actT x_dn act_chain ld_c ld_x x_sq v_mean v_std
                   dn_ready yd_ready x2_sq sh_silu_ready silu_ready x_silu fin_red fin_sq dve_chain
                   ld_mod sg_used""".split()
        S = {n: sem(n) for n in names}
        fin_ld = [sem(f"fin_ld{t}") for t in range(3)]
        gathered = [sem(f"gathered{b}") for b in range(2)]
        scattered = [sem(f"scattered{b}") for b in range(2)]
        gu_full = [sem(f"gu_full{s}") for s in range(UNROLL)]
        down_full = [sem(f"down_full{s}") for s in range(UNROLL)]

        def col(c, r, n=P):
            return prm[0:n, c, r:r + 1]

        def await_full(eng, name):
            b, before = bank_of(name)
            eng.wait_ge(bank_full[b], before + 1)
            return psum[:, b, :]

        def free(ins, name):
            return ins.then_inc(bank_free[bank_of(name)[0]], 1)

        def await_freed(eng, name):
            b, before = bank_of(name)
            eng.wait_ge(bank_free[b], before + 1)

        def need(eng, sem_, value):
            if not isinstance(value, int) or value > 0:
                eng.wait_ge(sem_, value)

        def block_source(kind, j):
            if kind == "ada":
                return ada_w[0, :, j * BLK:(j + 1) * BLK].rearrange("(k p) n -> p k n", p=P)
            if kind == "win":
                return w_in[0, :, j * BLK:(j + 1) * BLK].rearrange("(k p) n -> p k n", p=P)
            if kind == "br":
                return w_branch[0, j].rearrange("(k p) n -> p k n", p=P)
            return w_out[0, :, j * BLK:(j + 1) * BLK].rearrange("(k p) n -> p k n", p=P)

        def ring_view(kind, j):
            k = CT if kind == "br" else KT
            return ring[:, SLOT[kind, j] % RING, :].rearrange("p (k n) -> p k n", k=k)

        w_gu = [wexp[:, s, 0:4096].rearrange("p (a k f) -> p k a f", a=2, k=KT) for s in range(UNROLL)]
        w_dn = [wexp[:, s, 4096:6144].rearrange("p (j n) -> p j n", j=2) for s in range(UNROLL)]
        gate_v = e_gate[0].rearrange("e (p k) f -> e p (k f)", k=KT)
        up_v = e_up[0].rearrange("e (p k) f -> e p (k f)", k=KT)
        down_v = e_down[0].rearrange("e (p j) n -> e p (j n)", j=2)
        ytab_v = y_table.rearrange("(t r) d -> t r d", r=8)
        fin_y = wexp[:, :, :].rearrange("p s n -> p (s n)").rearrange("p (t r d) -> p t r d", t=3, r=8)

        def extra_passes(eng, step):
            eng.wait_ge(S["cnt_ready"], 1)
            longest = eng.value_load(cnt_i[0:1, 0:1], min_val=0, max_val=TOK)
            with eng.If(longest > CAP):
                for r in range(1, ROUNDS):
                    with eng.Fori(0, NE) as e:
                        step(r, e, NE * (r - 1) + e)

        block = ctx.enter_context(nc.Block())

        @block.sync
        def _(sp):
            for i, (kind, j) in enumerate(BLOCKS):
                if i >= RING:
                    await_full(sp, LAST_JOB[BLOCKS[i - RING]])
                sp.dma_start(ring_view(kind, j), block_source(kind, j)).then_inc(ring_full[i % RING], 16)
                if BLOCKS[i] == ("ada", 5):
                    await_full(sp, "modT")
                    sp.dma_start(mod[:, :], ada_b[0:1, 2 * D:].to_broadcast([NC_ROWS, 4 * D])).then_inc(S["ld_mod2"], 16)
            sp.wait_ge(S["mrg_ready"], KT)
            sp.dma_start(wexp[:, 1, 0:2048], s_gate[0].rearrange("(p k) f -> p (k f)", k=KT)).then_inc(S["sh_load"], 16)
            sp.dma_start(wexp[:, 1, 2048:4096], s_up[0].rearrange("(p k) f -> p (k f)", k=KT)).then_inc(S["sh_load"], 16)
            sp.dma_start(wexp[:, 1, 4096:6144], s_down[0].rearrange("(p j) n -> p (j n)", j=2)).then_inc(S["sh_load"], 16)

            def load_expert(e, s):
                sp.dma_start(wexp[:, s, 0:2048], gate_v[e]).then_inc(gu_full[s], 16)
                sp.dma_start(wexp[:, s, 2048:4096], up_v[e]).then_inc(gu_full[s], 16)
                sp.dma_start(wexp[:, s, 4096:6144], down_v[e]).then_inc(down_full[s], 16)

            load_expert(0, 0)
            await_full(sp, ("mix", 1, 2))
            load_expert(2, 2)
            await_full(sp, ("sy", 2, 1))
            load_expert(1, 1)
            load_expert(3, 3)
            with sp.Fori(1, NE // UNROLL) as i:
                for s in range(UNROLL):
                    sp.wait_ge(S["dn_done"], UNROLL * i + (s - 3))
                    for w, base, f, n in ((e_gate, 0, gu_full[s], 2048), (e_up, 2048, gu_full[s], 2048),
                                          (e_down, 4096, down_full[s], 2048)):
                        view = {0: gate_v, 2048: up_v, 4096: down_v}[base]
                        sp.dma_start(wexp[:, s, base:base + n], view[bass.ds(UNROLL * i + s, 1)].rearrange("e p n -> (e p) n")).then_inc(f, 16)

            def extra(r, e, n):
                sp.wait_ge(S["x_xt"], n + 1)
                for at, view in ((0, gate_v), (2048, up_v), (4096, down_v)):
                    sp.dma_start(wexp[:, 0, at:at + 2048], view[bass.ds(e, 1)].rearrange("e p n -> (e p) n")).then_inc(S["x_w"], 16)

            sp.wait_ge(S["dn_done"], NE)
            extra_passes(sp, extra)
            sp.wait_ge(S["moe_done"], 1)
            for t, (t0, n) in enumerate(TILES):
                sp.dma_start(fin_y[0:n, t], ytab_v[t0:t0 + n]).then_inc(fin_ld[t], 16)
            for t, (t0, n) in enumerate(TILES):
                sp.wait_ge(S["fin_ready"], t + 1)
                dst = y_sample[:, 0, :] if t == 2 else y_prompt[0, t0:t0 + n, :]
                sp.dma_start(dst, x_sb[0:n, t, :]).then_inc(S["out_done"], 16)
            sp.wait_ge(S["out_done"], 3 * 16)

        @block.gpsimd
        def _(pool):
            n_chain = [0]

            def link(ins):
                n_chain[0] += 1
                ins.then_inc(S["pool_chain"], 1)
                pool.wait_ge(S["pool_chain"], n_chain[0])

            g = nc.gpsimd
            g.memset(ident[:], 0.0)
            g.memset(sel8[:], 0.0)
            g.memset(ones[:], 1.0)
            g.memset(cmean[:], 1.0 / BR)
            g.memset(lower[:], 1.0)
            g.memset(trig[:], 1.0)
            link(g.memset(valid[:], 1.0))
            g.affine_select(out=ident[:], in_=ident[:], compare_op=ALU.not_equal, fill=1.0, base=0,
                            pattern=[[-1, P]], channel_multiplier=1).then_inc(S["consts"], 1)
            g.affine_select(out=sel8[:], in_=sel8[:], compare_op=ALU.not_equal, fill=1.0, base=-NS,
                            pattern=[[0, P]], channel_multiplier=1)
            g.affine_select(out=lower[:], in_=lower[:], compare_op=ALU.is_ge, fill=0.0, base=-1,
                            pattern=[[1, P]], channel_multiplier=-1)
            g.affine_select(out=trig[:], in_=trig[:], compare_op=ALU.is_ge, fill=0.0, base=-1,
                            pattern=[[1, NG], [-1, NG]], channel_multiplier=0)
            g.affine_select(out=valid[:], in_=valid[:], compare_op=ALU.is_ge, fill=0.0, base=TOK - 1,
                            pattern=[[-P, 3]], channel_multiplier=-1)
            g.iota(iota_i[:], pattern=[[1, P]], base=0, channel_multiplier=0)
            g.iota(idx[:, 0, :], pattern=[[P, 3]], base=0, channel_multiplier=1)
            g.memset(gluP[:, :, 0:HF], 0.0)
            g.memset(zcP[:, :, 0:HP], 0.0)
            g.memset(cgP[:, :, 0:HC], 0.0)
            g.memset(st[:], 1.0)
            g.memset(bns[:], 1.0)
            g.memset(epsc[:], EPS)
            g.memset(sc[:], 0.0).then_inc(S["consts"], 1)
            pool.wait_ge(S["ld_stage"], 12 * 16)
            g.affine_select(out=wsr, in_=wsr, compare_op=ALU.is_ge, fill=0.0, base=0,
                            pattern=[[0, CT], [-1, P]], channel_multiplier=1).then_inc(S["wg_masked"], 1)
            with nc.allow_non_contiguous_dma(reason="history rows"):
                g.dma_start(conv_s[0, :, 0:HC - 1, :], state_conv[0, :, 1:HC, :]).then_inc(S["states_done"], 16)
                g.dma_start(pool_s[0, :, 0:HP - 1, :], state_pool[0, :, 1:HP, :]).then_inc(S["states_done"], 16)
                g.dma_start(conf_s[0, :, 0:HF - 1, :], state_conf[0, :, 1:HF, :]).then_inc(S["states_done"], 16)
            pool.wait_ge(S["v_ready"], 1)
            g.dma_start(chunk_v_s[0, :, 0, :], v_sb[0:NS, 2, :]).then_inc(S["states_done"], 16)
            for name, rows, h, prompt, sample in (("st_conf", st_conf, HF, conf_p, conf_s), ("st_conv", st_conv, HC, conv_p, conv_s),
                                                  ("st_pool", st_pool, HP, pool_p, pool_s)):
                await_freed(pool, name)
                g.dma_start(prompt[0, 0], rows[0:h, :]).then_inc(S["st_stored"], 16)
                g.dma_start(sample[0, :, h - 1, :], rows[h:h + NS, :]).then_inc(S["st_stored"], 16)
            pool.wait_ge(S["h2_ready"], 1)
            g.dma_start(h_table[0:SEQ].rearrange("(t p) d -> p t d", p=P), xn[:, 0:2, :]).then_inc(S["h2_stored"], 16)
            g.dma_start(h_table[SEQ:TOK], xn[0:NS, 2, :]).then_inc(S["h2_stored"], 16)
            pool.wait_ge(S["x2_ready"], 6)
            g.dma_start(fing, final_g.rearrange("(a d) -> a d", a=1).to_broadcast([P, D])).then_inc(S["ld_fin"], 16)
            pool.wait_ge(S["h2_stored"], 32)

            last_token, last_result = pool.alloc_register("last_token"), pool.alloc_register("last_result")
            pool.reg_mov(last_token, TOK - 1)
            pool.reg_mov(last_result, 8 * TOK - 1)

            def gather(i, j):
                e = UNROLL * i + j
                pool.wait_ge(S["lst_ready"], e + 1)
                need(pool, S["xt_done"], e - 1)
                if isinstance(e, int) and e == 0:
                    await_full(pool, ("h2T", KT - 1))
                pool.sem_inc(S["dma_may_go"], 1)
                g.indirect_dma_start(out=xg[:, j % 2, :], out_offset=None, in_=h_table,
                                     in_offset=bass.IndirectOffsetOnAxis(ap=idx[:, j % 4, 0:1].bitcast(mybir.dt.uint32), axis=0),
                                     bounds_check=last_token, oob_is_err=False).then_inc(gathered[j % 2], 16)

            def scatter(i, j):
                e = UNROLL * i + j
                pool.wait_ge(S["ys_act"], e + 1)
                pool.wait_ge(S["ys_dve"], e + 1)
                pool.sem_inc(S["dma_may_go"], 1)
                g.indirect_dma_start(out=y_table, out_offset=bass.IndirectOffsetOnAxis(ap=idx[:, j % 4, 2:3].bitcast(mybir.dt.uint32), axis=0),
                                     in_=y_rows[:, j % 2, :], in_offset=None,
                                     bounds_check=last_result, oob_is_err=False).then_inc(scattered[j % 2], 16)

            gather(0, 0)
            gather(0, 1)

            def body(i, first=False, last=False):
                for j in range(UNROLL):
                    if not (first and j == 0):
                        scatter(i if j else i - 1, (j - 1) % UNROLL)
                    if not (last and j >= 2):
                        gather(i if j < 2 else i + 1, (j + 2) % UNROLL)

            body(0, first=True)
            with pool.Fori(1, NE // UNROLL - 1) as i:
                body(i)
            body(NE // UNROLL - 1, last=True)
            scatter(NE // UNROLL - 1, UNROLL - 1)
            pool.wait_ge(scattered[0], 16 * (NE // 2))
            pool.wait_ge(scattered[1], 16 * (NE // 2))

            def extra(r, e, n):
                pool.wait_ge(S["x_idx"], n + 1)
                pool.sem_inc(S["dma_may_go"], 1)
                g.indirect_dma_start(out=xg[:, 0, :], out_offset=None, in_=h_table,
                                     in_offset=bass.IndirectOffsetOnAxis(ap=idx[:, 0, 0:1].bitcast(mybir.dt.uint32), axis=0),
                                     bounds_check=last_token, oob_is_err=False).then_inc(S["x_gat"], 16)
                pool.wait_ge(S["x_y"], n + 1)
                pool.sem_inc(S["dma_may_go"], 1)
                g.indirect_dma_start(out=y_table, out_offset=bass.IndirectOffsetOnAxis(ap=idx[:, 0, 2:3].bitcast(mybir.dt.uint32), axis=0),
                                     in_=y_rows[:, 0, :], in_offset=None,
                                     bounds_check=last_result, oob_is_err=False).then_inc(S["x_sc"], 16)
                pool.wait_ge(S["x_sc"], 16 * n + 16)

            extra_passes(pool, extra)
            pool.sem_inc(S["moe_done"], 1)
            pool.wait_ge(S["states_done"], 4 * 16)
            pool.wait_ge(S["st_stored"], 6 * 16)

        @block.tensor
        def _(pe):
            mm = nc.tensor.matmul

            def claim(name):
                b, before = bank_of(name)
                need(pe, bank_free[b], before)
                return psum[:, b, :]

            def full(ins, name):
                ins.then_inc(bank_full[bank_of(name)[0]], 1)

            def weights(kind, j):
                i = SLOT[kind, j]
                pe.wait_ge(ring_full[i % RING], 16 * (i // RING + 1))
                return ring_view(kind, j)

            def turn(out, src, rows):
                return nc.tensor.transpose(out, src, ident[0:rows, 0:rows])

            pe.wait_ge(S["consts"], 2)
            pe.wait_ge(S["c_silu"], 1)
            out = claim("cT")
            for k in range(KT):
                last = turn(out[:, k * NC_ROWS:(k + 1) * NC_ROWS], crow[:, k * P:(k + 1) * P], NC_ROWS)
            full(last, "cT")
            pe.wait_ge(S["ld_stage"], 12 * 16)
            out = claim("prow0")
            for c in range(CT):
                last = turn(out[:, c * NPROW:(c + 1) * NPROW], prow[:, c * P:(c + 1) * P], NPROW)
            full(last, "prow0")
            pe.wait_ge(S["wg_masked"], 1)
            out = claim("wsT")
            for c in range(CT):
                last = turn(out[:, c * P:(c + 1) * P], wsr[:, c, :], P)
            full(last, "wsT")
            for n, rows in enumerate((NS * HC, NS * HP, 4 * HF, 4 * HF)):
                out = claim(("hist", n))
                for c in range(CT):
                    last = turn(out[:, c * rows:(c + 1) * rows], hist[0:rows, n, c * P:(c + 1) * P], rows)
                full(last, ("hist", n))

            def ada(j):
                w = weights("ada", j)
                out = claim(("ada", j))
                await_freed(pe, "cT")
                for k in range(KT):
                    last = mm(out[0:NC_ROWS, :], cT[:, k, :], w[:, k, :], start=(k == 0), stop=(k == KT - 1))
                full(last, ("ada", j))

            for j in range(4):
                ada(j)
            out = claim("modT")
            await_freed(pe, ("ada", 3))
            for k in range(2 * KT):
                last = turn(out[:, k * NC_ROWS:(k + 1) * NC_ROWS], mod[:, k * P:(k + 1) * P], NC_ROWS)
            full(last, "modT")
            pe.wait_ge(S["x_norm"], 3)
            for k in range(KT):
                out = claim(("hT", k))
                for t, (t0, n) in enumerate(TILES):
                    last = turn(out[:, t0:t0 + n], xn[0:n, t, k * P:(k + 1) * P], n)
                full(last, ("hT", k))

            w = weights("win", 1)
            pe.wait_ge(S["h_ready"], KT)
            for t, (t0, n) in enumerate(TILES):
                out = claim(("v", t))
                for k in range(KT):
                    last = mm(out[0:n, :], hT[:, k, t0:t0 + n], w[:, k, :], start=(k == 0), stop=(k == KT - 1))
                full(last, ("v", t))

            def columns(j, names):
                w = weights("win", j)
                for c, name in enumerate(names):
                    out = claim(name)
                    for k in range(KT):
                        last = mm(out[:, 0:TOK], w[:, k, c * P:(c + 1) * P], hT[:, k, :], start=(k == 0), stop=(k == KT - 1))
                    full(last, name)

            def state(name, made_of, src, at, n):
                await_freed(pe, made_of)
                out = claim(name)
                for c in range(CT):
                    last = turn(out[0:n, c * P:(c + 1) * P], src[:, c, at:at + n], P)
                full(last, name)

            for j in (7, 6, 3, 4, 5, 2, 0):
                columns(j, [("z", j, c) for c in range(CT)])
                if j == 6:
                    state("st_conf", ("z", 6, CT - 1), gluP, SEQ, HF + NS)
                if j == 4:
                    state("st_conv", ("z", 4, CT - 1), cgP, SEQ, HC + NS)
                if j == 5:
                    state("st_pool", ("z", 5, CT - 1), zcP, SEQ, HP + NS)
            pe.wait_ge(S["v_ready"], 1)
            pe.wait_ge(S["ws_ready"], 1)
            for c in range(CT):
                out = claim(("sg", c))
                for t in range(2):
                    mm(out[:, t * P:(t + 1) * P], v_sb[:, t, c * P:(c + 1) * P], wsT[:, c, :], start=True, stop=True)
                last = mm(out[:, SEQ:TOK], v_sb[0:NS, 2, c * P:(c + 1) * P], wdiag[:, c, :], start=True, stop=True)
                full(last, ("sg", c))
            pe.wait_ge(S["ld_param"], NPARAM * 16)
            pe.wait_ge(S["pooled_ready"], CT)
            for c in range(CT):
                out = claim(("pw", c))
                full(mm(out[:, 0:TOK], poolw[:, c, :], ybr[:, 2, c, :], start=True, stop=True), ("pw", c))
            for j in range(4, 12):
                ada(j)
                if j % 2:
                    i = (j - 5) // 2
                    await_freed(pe, ("ada", j))
                    if i == 2:
                        pe.wait_ge(S["g2_rows"], 1)
                    for h in range(2):
                        out = claim(("bc", i, h))
                        at = i * D + h * BLK
                        full(mm(out, sel8[:, :], mod[:, at:at + BLK], start=True, stop=True), ("bc", i, h))
            for n, k in enumerate(BR_ORDER):
                if k == 0:
                    pe.wait_ge(S["dconv_ready"], 1)
                    out = claim("cmean")
                    for c in range(CT):
                        last = mm(out[:, 0:TOK], cmean[:, :], dcv[:, c, :], start=(c == 0), stop=(c == CT - 1))
                    full(last, "cmean")
                if k == 3:
                    pe.wait_ge(S["sq_ready"], 1)
                    out = claim("cvar")
                    for c in range(CT):
                        last = mm(out[:, 0:TOK], cmean[:, :], tmpT[:, c, :], start=(c == 0), stop=(c == CT - 1))
                    full(last, "cvar")
                for half in range(2):
                    columns(8 + 2 * k + half, [("zg", k, 4 * half + c) for c in range(CT)])
                w = weights("br", k)
                if k == 2:
                    await_freed(pe, ("pw", CT - 1))
                elif k == 1:
                    await_freed(pe, ("z", 2, CT - 1))
                else:
                    pe.wait_ge(S["ya_ready" if k == 0 else "yd_ready"], CT)
                for d in range(KT):
                    out = claim(("pr", k, d))
                    for c in range(CT):
                        last = mm(out[:, 0:TOK], w[:, c, d * P:(d + 1) * P], ybr[:, k, c, :], start=(c == 0), stop=(c == CT - 1))
                    full(last, ("pr", k, d))
            pe.wait_ge(S["mrg_ready"], KT)
            for j in range(2):
                w = weights("out", j)
                for t, (t0, n) in enumerate(TILES):
                    out = claim(("mix", j, t))
                    for k in range(KT):
                        last = mm(out[0:n, :], mT[:, k, t0:t0 + n], w[:, k, :], start=(k == 0), stop=(k == KT - 1))
                    full(last, ("mix", j, t))
            pe.wait_ge(S["h2_ready"], 1)
            for k in range(KT):
                out = claim(("h2T", k))
                for t, (t0, n) in enumerate(TILES):
                    last = turn(out[:, t0:t0 + n], xn[0:n, t, k:D:KT], n)
                full(last, ("h2T", k))
            await_freed(pe, ("h2T", KT - 1))
            out = claim("logit")
            for t, (t0, n) in enumerate(TILES):
                for k in range(KT):
                    last = mm(out[0:n, t * NE:(t + 1) * NE], hT[:, k, t0:t0 + n], rtw[:, k, :], start=(k == 0), stop=(k == KT - 1))
            full(last, "logit")

            def shared_up(t):
                t0, n = TILES[t]
                out = claim(("sgu", t))
                for k in range(KT):
                    last = mm(out[0:n, :], hT[:, k, t0:t0 + n], w_gu[1][:, k], start=(k == 0), stop=(k == KT - 1))
                full(last, ("sgu", t))

            pe.wait_ge(S["sh_load"], 48)
            shared_up(0)
            shared_up(1)
            pe.wait_ge(S["sel_ready"], 1)
            out = claim("slot")
            for t in range(3):
                for u in range(t):
                    mm(out[:, t * NE:(t + 1) * NE], ones[:, :], sel[:, u, :], start=(u == 0), stop=False)
                mm(out[:, t * NE:(t + 1) * NE], lower[:, :], sel[:, t, :], start=(t == 0), stop=True)
            for t in range(3):
                last = mm(out[:, 3 * NE:4 * NE], ones[:, :], sel[:, t, :], start=(t == 0), stop=(t == 2))
            full(last, "slot")
            for t, (t0, n) in enumerate(TILES):
                out = claim(("saT", t))
                await_freed(pe, ("sgu", t))
                for h in range(2):
                    last = turn(out[:, h * P:h * P + n], sh_act[0:n, h:FE:2], n)
                full(last, ("saT", t))
                if t == 0:
                    shared_up(2)
                await_freed(pe, ("saT", t))
                for h in range(2):
                    out = claim(("sy", t, h))
                    for f in range(2):
                        last = mm(out[0:n, :], sh_actT[:, f, 0:n], w_dn[1][:, f, h * BLK:(h + 1) * BLK], start=(f == 0), stop=(f == 1))
                    full(last, ("sy", t, h))

            for b in range(NBANK):
                uses = len([1 for name in JOBS if bank_of(name)[0] == b])
                pe.wait_ge(bank_free[b], uses)

            def token_list(i, j):
                e = UNROLL * i + j
                pe.wait_ge(S["oh_ready"], e + 1)
                need(pe, S["lst_ready"], e)
                for t in range(3):
                    rhs = tab[:, t, :, :].rearrange("p e c -> p (e c)")
                    rhs = rhs[:, 3 * e:3 * e + 3] if isinstance(e, int) else rhs[:, bass.ds(3 * e, 3)]
                    last = mm(psum[:, 7, 0:3], oh[:, j % 2, t, :], rhs, start=(t == 0), stop=(t == 2))
                last.then_inc(S["list_done"], 1)

            def turn_rows(i, j):
                e = UNROLL * i + j
                pe.wait_ge(gathered[j % 2], 16 * (2 * i + j // 2 + 1))
                need(pe, S["xgt_act"], e)
                need(pe, S["xgt_dve"], e)
                for k in range(KT):
                    last = turn(psum[:, 5 + k // 4, (k % 4) * P:(k % 4 + 1) * P], xg[:, j % 2, k:D:KT], P)
                last.then_inc(S["xt_done"], 1)

            def up(i, j, ks):
                e = UNROLL * i + j
                if ks[0] == 0:
                    pe.wait_ge(gu_full[j], 32 * (i + 1))
                    pe.wait_ge(S["xgt_act"], e + 1)
                    pe.wait_ge(S["xgt_dve"], e + 1)
                    need(pe, S["act_ready"], e - 1)
                for k in ks:
                    last = mm(psum[:, j % 2, :], xgT[:, j % 2, k, :], w_gu[j][:, k], start=(k == 0), stop=(k == KT - 1))
                if ks[-1] == KT - 1:
                    last.then_inc(S["gu_done"], 1)

            def turn_act(i, j):
                e = UNROLL * i + j
                pe.wait_ge(S["act_ready"], e + 1)
                need(pe, S["actT_ready"], e)
                for h in range(2):
                    last = turn(psum[:, 2, h * P:(h + 1) * P], act[:, j % 2, h:FE:2], P)
                last.then_inc(S["tact_done"], 1)

            def down(i, j):
                e = UNROLL * i + j
                pe.wait_ge(S["actT_ready"], e + 1)
                pe.wait_ge(down_full[j], 16 * (i + 1))
                need(pe, S["ys_act"], e)
                need(pe, S["ys_dve"], e)
                for h in range(2):
                    for f in range(2):
                        last = mm(psum[:, 3 + h, :], actT[:, j % 2, f, :], w_dn[j][:, f, h * BLK:(h + 1) * BLK],
                                  start=(f == 0), stop=(f == 1))
                last.then_inc(S["dn_done"], 1)

            def body(i, first=False, last=False):
                for j in range(UNROLL):
                    prev = not (first and j == 0)
                    pi, pj = (i if j else i - 1), (j - 1) % UNROLL
                    up(i, j, range(0, 4))
                    if prev:
                        turn_act(pi, pj)
                    up(i, j, range(4, KT))
                    if prev:
                        down(pi, pj)
                    if not (last and j == UNROLL - 1):
                        turn_rows(i if j < 3 else i + 1, (j + 1) % UNROLL)
                    if not (last and j >= 2):
                        token_list(i if j < 2 else i + 1, (j + 2) % UNROLL)

            token_list(0, 0)
            token_list(0, 1)
            turn_rows(0, 0)
            body(0, first=True)
            with pe.Fori(1, NE // UNROLL - 1) as i:
                body(i)
            body(NE // UNROLL - 1, last=True)
            turn_act(NE // UNROLL - 1, UNROLL - 1)
            down(NE // UNROLL - 1, UNROLL - 1)


            def extra(r, e, n):
                pe.wait_ge(S["x_oh"], n + 1)
                for t in range(3):
                    rhs = tab[:, t, :, :].rearrange("p e c -> p (e c)")[:, bass.ds(3 * e, 3)]
                    last = mm(psum[:, 7, 0:3], oh[:, 0, t, :], rhs, start=(t == 0), stop=(t == 2))
                last.then_inc(S["x_list"], 1)
                pe.wait_ge(S["x_gat"], 16 * n + 16)
                for k in range(KT):
                    last = turn(psum[:, 5 + k // 4, (k % 4) * P:(k % 4 + 1) * P], xg[:, 0, k:D:KT], P)
                last.then_inc(S["x_xt"], 1)
                pe.wait_ge(S["x_xgt"], n + 1)
                pe.wait_ge(S["x_w"], 48 * n + 48)
                for k in range(KT):
                    last = mm(psum[:, 0, :], xgT[:, 0, k, :], w_gu[0][:, k], start=(k == 0), stop=(k == KT - 1))
                last.then_inc(S["x_gu"], 1)
                pe.wait_ge(S["x_act"], n + 1)
                for h in range(2):
                    last = turn(psum[:, 2, h * P:(h + 1) * P], act[:, 0, h:FE:2], P)
                last.then_inc(S["x_tact"], 1)
                pe.wait_ge(S["x_actT"], n + 1)
                for h in range(2):
                    for f in range(2):
                        last = mm(psum[:, 3 + h, :], actT[:, 0, f, :], w_dn[0][:, f, h * BLK:(h + 1) * BLK], start=(f == 0), stop=(f == 1))
                last.then_inc(S["x_dn"], 1)

            extra_passes(pe, extra)

        @block.scalar
        def _(ac):
            n_chain = [0]

            def link(ins):
                n_chain[0] += 1
                ins.then_inc(S["act_chain"], 1)
                ac.wait_ge(S["act_chain"], n_chain[0])

            def load(dst, src, name):
                ac.dma_start(dst, src).then_inc(S[name], 16)

            F = nc.scalar.activation
            load(crow[0:NS], c_sample, "ld_c")
            load(crow[NS:NC_ROWS], c_prompt, "ld_c")
            load(x_sb[:, 0:2, :], x_prompt[0].rearrange("(t p) d -> p t d", p=P), "ld_x")
            load(x_sb[0:NS, 2, :], x_sample[:, 0, :], "ld_x")
            load(mod[:, 0:2 * D], ada_b[0:1, 0:2 * D].to_broadcast([NC_ROWS, 2 * D]), "ld_mod")
            load(prow[R_CONFW:R_CONFW + 31], conf_w[0], "ld_stage")
            load(prow[R_CONVW:R_CONVW + 3], conv_w[0], "ld_stage")
            for r, p in ((R_CONFB, conf_b), (R_CLNG, conf_ln_g), (R_CLNB, conf_ln_b), (R_PSC, pool_scale)):
                load(prow[r:r + 1], p, "ld_stage")
            load(prow[R_N1G:R_N1G + 2], norm1_g.rearrange("a (r c) -> (a r) c", r=2), "ld_stage")
            load(wsr, sgu_w[0].rearrange("g p q -> p g q"), "ld_stage")
            load(hist[0:NS * HC, 0, :], state_conv[0].rearrange("s h c -> (s h) c"), "ld_stage")
            load(hist[0:NS * HP, 1, :], state_pool[0].rearrange("s h c -> (s h) c"), "ld_stage")
            for a in range(2):
                load(hist[0:4 * HF, 2 + a, :], state_conf[0, 4 * a:4 * a + 4].rearrange("s h c -> (s h) c"), "ld_stage")
            load(lnv[:, 0, :], sgu_ln_g.to_broadcast([P, BR]), "ld_param")
            load(lnv[:, 1, :], sgu_ln_b.to_broadcast([P, BR]), "ld_param")
            load(sgub, sgu_b[0:1].rearrange("a g q -> a (g q)").to_broadcast([P, BR]).rearrange("p (g q) -> p g q", g=CT), "ld_param")
            with nc.allow_non_contiguous_dma(reason="one weight per group"):
                load(w00[:], sgu_w[0, :, 0, 0:1].rearrange("g a -> a g").to_broadcast([NS, CT]), "ld_param")
            load(poolw, pool_w[0].rearrange("g c d -> c g d"), "ld_param")
            load(rtw[:], router_w[0].rearrange("(p k) e -> p k e", k=KT), "ld_param")
            load(rtb[:], router_bias.to_broadcast([P, NE]), "ld_param")
            load(bc[0:NC_ROWS, 2, :], norm2_g.to_broadcast([NC_ROWS, D]), "ld_param")

            ac.wait_ge(S["ld_c"], 32)
            F(crow[:, :], crow[:, :], ACT.Silu).then_inc(S["c_silu"], 1)

            def row_norm(src_sem, value, done):
                ac.wait_ge(src_sem, value)
                for t, (t0, n) in enumerate(TILES):
                    last = F(xn[0:n, t, :], x_sb[0:n, t, :], ACT.Square, accum_out=st[0:n, t, 0:1])
                link(last)
                F(st[:, :, 1], st[:, :, 0], ACT.Sqrt, scale=1.0 / D, bias=epsc[:, 0:1]).then_inc(done, 1)

            ac.wait_ge(S["consts"], 2)
            row_norm(S["ld_x"], 32, S["x_sq"])
            for t, (t0, n) in enumerate(TILES):
                b = await_full(ac, ("v", t))
                free(F(v_sb[0:n, t, :], b[0:n, :], ACT.Gelu), ("v", t))
            ac.wait_ge(S["v_mean"], 1)
            F(st[:, :, 6], st[:, :, 5], ACT.Sqrt, bias=epsc[:, 0:1]).then_inc(S["v_std"], 1)

            def z_out(j, func, dst, reader):
                for c in range(CT):
                    b = await_full(ac, ("z", j, c))
                    if reader:
                        await_freed(ac, ("z", reader, c))
                    free(F(dst(c), b[:, 0:TOK], func), ("z", j, c))

            def state_rows(name, rows, n):
                b = await_full(ac, name)
                free(F(rows[0:n, :], b[0:n, :], ACT.Copy), name)

            z_out(7, ACT.Sigmoid, lambda c: tmpT[:, c, :], None)
            state_rows("st_conf", st_conf, HF + NS)
            z_out(3, ACT.Copy, lambda c: tmpT[:, c, :], 6)
            state_rows("st_conv", st_conv, HC + NS)
            for c in range(CT):
                b = await_full(ac, ("z", 5, c))
                free(F(zcP[:, c, HP:], b[:, 0:TOK], ACT.Copy), ("z", 5, c))
            state_rows("st_pool", st_pool, HP + NS)
            z_out(0, ACT.Gelu, lambda c: tmpT[:, c, :], 4)

            def spread_out(i):
                for h in range(2):
                    b = await_full(ac, ("bc", i, h))
                    if i in (1, 3):
                        ac.wait_ge(S["st_stored"], 6 * 16)
                    free(F(bc[:, i, h * BLK:(h + 1) * BLK], b[:, :], ACT.Copy), ("bc", i, h))

            for i in range(4):
                spread_out(i)
            for n, k in enumerate(BR_ORDER):
                if k == 0:
                    await_freed(ac, "cmean")
                    F(tmpT[:, :, :], dcv[:, :, :], ACT.Square).then_inc(S["sq_ready"], 1)
                if k == 3:
                    b = await_full(ac, "cvar")
                    free(F(stat[:, 0, :], b[:, 0:TOK], ACT.Sqrt, bias=epsc[:, 0:1]), "cvar")
                    ac.wait_ge(S["dn_ready"], 1)
                    for c in range(CT):
                        F(ybr[:, 3, c, :], dcv[:, c, :], ACT.Silu, scale=col(c, R_CLNG), bias=col(c, R_CLNB)).then_inc(S["yd_ready"], 1)
                for d in range(KT):
                    b = await_full(ac, ("zg", k, d))
                    if n:
                        await_freed(ac, ("pr", BR_ORDER[n - 1], d))
                    free(F(sg[:, d, :], b[:, 0:TOK], ACT.Sigmoid), ("zg", k, d))
            row_norm(S["x2_ready"], 6, S["x2_sq"])
            for k in range(KT):
                b = await_full(ac, ("h2T", k))
                free(F(hT[:, k, :], b[:, 0:TOK], ACT.Copy), ("h2T", k))
            b = await_full(ac, "logit")
            for t, (t0, n) in enumerate(TILES):
                last = F(sc[0:n, t, :], b[0:n, t * NE:(t + 1) * NE], ACT.Sigmoid)
            free(last, "logit")

            for t, (t0, n) in enumerate(TILES):
                b = await_full(ac, ("sgu", t))
                if t:
                    await_freed(ac, ("sgu", t - 1))
                F(sh_silu[0:n, :], b[0:n, 0:FE], ACT.Silu).then_inc(S["sh_silu_ready"], 1)
                b = await_full(ac, ("saT", t))
                if t:
                    await_full(ac, ("sy", t - 1, 1))
                free(F(sh_actT[:, :, 0:n], b[:, 0:2 * P].rearrange("p (h c) -> p h c", h=2)[:, :, 0:n], ACT.Copy), ("saT", t))
                for h in range(2):
                    b = await_full(ac, ("sy", t, h))
                    free(F(shared[0:n, t, h * BLK:(h + 1) * BLK], b[0:n, :], ACT.Copy), ("sy", t, h))

            def rows_out(i, j):
                e = UNROLL * i + j
                ac.wait_ge(S["xt_done"], e + 1)
                need(ac, S["gu_done"], e - 1)
                F(xgT[:, j % 2, 0:4, :], psum[:, 5, :].rearrange("p (k c) -> p k c", k=4), ACT.Copy).then_inc(S["xgt_act"], 1)

            def act_turned(i, j):
                e = UNROLL * i + j
                ac.wait_ge(S["tact_done"], e + 1)
                need(ac, S["dn_done"], e - 1)
                F(actT[:, j % 2], psum[:, 2, 0:2 * P].rearrange("p (h c) -> p h c", h=2), ACT.Copy).then_inc(S["actT_ready"], 1)

            def y_out(i, j):
                e = UNROLL * i + j
                ac.wait_ge(S["dn_done"], e + 1)
                need(ac, scattered[j % 2], 16 * (2 * i + j // 2))
                F(y_rows[:, j % 2, 0:BLK], psum[:, 3, :], ACT.Copy).then_inc(S["ys_act"], 1)

            def body(i, first=False, last=False):
                for j in range(UNROLL):
                    prev = not (first and j == 0)
                    pi, pj = (i if j else i - 1), (j - 1) % UNROLL
                    e = UNROLL * i + j
                    if prev:
                        act_turned(pi, pj)
                    ac.wait_ge(S["gu_done"], e + 1)
                    need(ac, S["act_ready"], e - 1)
                    F(silu[:, j % 2, :], psum[:, j % 2, 0:FE], ACT.Silu).then_inc(S["silu_ready"], 1)
                    if prev:
                        y_out(pi, pj)
                    if not (last and j == UNROLL - 1):
                        rows_out(i if j < 3 else i + 1, (j + 1) % UNROLL)

            rows_out(0, 0)
            body(0, first=True)
            with ac.Fori(1, NE // UNROLL - 1) as i:
                body(i)
            body(NE // UNROLL - 1, last=True)
            act_turned(NE // UNROLL - 1, UNROLL - 1)
            y_out(NE // UNROLL - 1, UNROLL - 1)

            def extra(r, e, n):
                ac.wait_ge(S["x_gu"], n + 1)
                F(silu[:, 0, :], psum[:, 0, 0:FE], ACT.Silu).then_inc(S["x_silu"], 1)
                ac.wait_ge(S["x_tact"], n + 1)
                F(actT[:, 0], psum[:, 2, 0:2 * P].rearrange("p (h c) -> p h c", h=2), ACT.Copy).then_inc(S["x_actT"], 1)

            extra_passes(ac, extra)
            for t, (t0, n) in enumerate(TILES):
                ac.wait_ge(S["fin_red"], t + 1)
                link(F(xn[0:n, t, :], x_sb[0:n, t, :], ACT.Square, accum_out=st[0:n, t, 0:1]))
                F(st[0:n, t, 1:2], st[0:n, t, 0:1], ACT.Sqrt, scale=1.0 / D, bias=epsc[0:n, 0:1]).then_inc(S["fin_sq"], 1)

        @block.vector
        def _(ve):
            n_chain = [0]
            V = nc.vector

            def mark(ins):
                n_chain[0] += 1
                ins.then_inc(S["dve_chain"], 1)
                return n_chain[0]

            def link(ins):
                ve.wait_ge(S["dve_chain"], mark(ins))

            ve.wait_ge(S["consts"], 2)
            V.tensor_copy(tokid[:], idx[:, 0, :])
            link(V.tensor_copy(iota_f[:], iota_i[:]))
            link(V.tensor_scalar(rc[:], iota_f[:, 0:16], 1.0, None, ALU.add))
            V.reciprocal(rc[:], rc[:])
            ve.wait_ge(S["x_sq"], 1)
            link(V.reciprocal(st[:, :, 2], st[:, :, 1]))
            for t, (t0, n) in enumerate(TILES):
                V.tensor_scalar(xn[0:n, t, :], x_sb[0:n, t, :], st[0:n, t, 2:3], None, ALU.mult).then_inc(S["x_norm"], 1)
            b = await_full(ve, "cT")
            free(V.tensor_copy(cT[:].rearrange("p k r -> p (k r)"), b[:, 0:KT * NC_ROWS]), "cT")
            b = await_full(ve, "prow0")
            free(V.tensor_copy(prm[:].rearrange("p c r -> p (c r)"), b[:, 0:CT * NPROW]), "prow0")
            b = await_full(ve, "wsT")
            free(V.tensor_copy(wsT.rearrange("p g q -> p (g q)"), b[:, :]), "wsT")
            ve.wait_ge(S["ld_param"], NPARAM * 16)
            for c in range(CT):
                last = V.tensor_scalar(wdiag[:, c, :], ident[0:NS, 0:NS], w00[:, c:c + 1], None, ALU.mult)
            last.then_inc(S["ws_ready"], 1)
            for n, (dst, rows) in enumerate(((convH.rearrange("p c s h -> p c (s h)"), NS * HC),
                                             (poolH.rearrange("p c s h -> p c (s h)"), NS * HP),
                                             (confH[:, :, 0:4, :].rearrange("p c s h -> p c (s h)"), 4 * HF),
                                             (confH[:, :, 4:8, :].rearrange("p c s h -> p c (s h)"), 4 * HF))):
                b = await_full(ve, ("hist", n))
                free(V.tensor_copy(dst, b[:, 0:CT * rows].rearrange("p (c r) -> p c r", c=CT)), ("hist", n))

            def ada_out(j):
                b = await_full(ve, ("ada", j))
                at = (j % 4 if j < 4 else j - 4) * BLK
                ins = V.tensor_tensor(mod[:, at:at + BLK], b[0:NC_ROWS, :], mod[:, at:at + BLK], ALU.add)
                return ins

            ve.wait_ge(S["ld_mod"], 16)
            for j in range(4):
                free(ada_out(j), ("ada", j))
            b = await_full(ve, "modT")
            V.tensor_copy(S1[:].rearrange("p k r -> p (k r)"), b[:, 0:KT * NC_ROWS])
            free(V.tensor_scalar(G1[:].rearrange("p k r -> p (k r)"), b[:, KT * NC_ROWS:2 * KT * NC_ROWS], 1.0, None, ALU.add), "modT")
            await_freed(ve, "modT")
            await_freed(ve, "prow0")
            link(V.tensor_tensor(G1[:].rearrange("p (a c) r -> p a c r", a=2), G1[:].rearrange("p (a c) r -> p a c r", a=2),
                                 prm[:, :, R_N1G:R_N1G + 2].rearrange("p c a -> p a c").unsqueeze(3).to_broadcast([P, 2, CT, NC_ROWS]),
                                 ALU.mult))
            for k in range(KT):
                b = await_full(ve, ("hT", k))
                V.tensor_scalar(hT[:, k, 0:SEQ], b[:, 0:SEQ], G1[:, k, NS:NC_ROWS], S1[:, k, NS:NC_ROWS], ALU.mult, ALU.add)
                free(V.tensor_tensor(hT[:, k, SEQ:TOK], b[:, SEQ:TOK], G1[:, k, 0:NS], ALU.mult), ("hT", k))
                await_freed(ve, ("hT", k))
                V.tensor_tensor(hT[:, k, SEQ:TOK], hT[:, k, SEQ:TOK], S1[:, k, 0:NS], ALU.add).then_inc(S["h_ready"], 1)
            for t, (t0, n) in enumerate(TILES):
                await_freed(ve, ("v", t))
                link(V.bn_stats(bns[0:n, t, 0:6], v_sb[0:n, t, :]))
                last = V.bn_aggr(st[0:n, t, 4:6], bns[0:n, t, 0:6])
            last.then_inc(S["v_mean"], 1)
            ve.wait_ge(S["v_std"], 1)
            link(V.reciprocal(st[:, :, 7], st[:, :, 6]))
            for t, (t0, n) in enumerate(TILES):
                link(V.tensor_scalar(v_sb[0:n, t, :], v_sb[0:n, t, :], st[0:n, t, 4:5], st[0:n, t, 7:8], ALU.subtract, ALU.mult))
                link(V.tensor_tensor(v_sb[0:n, t, :], v_sb[0:n, t, :], lnv[0:n, 0, :], ALU.mult))
                last = V.tensor_tensor(v_sb[0:n, t, :], v_sb[0:n, t, :], lnv[0:n, 1, :], ALU.add)
            last.then_inc(S["v_ready"], 1)

            for c in range(CT):
                b = await_full(ve, ("z", 6, c))
                await_freed(ve, ("z", 7, c))
                free(V.tensor_tensor(gluP[:, c, HF:], b[:, 0:TOK], tmpT[:, c, :], ALU.mult), ("z", 6, c))
            for c in range(CT):
                b = await_full(ve, ("z", 4, c))
                await_freed(ve, ("z", 3, c))
                free(V.tensor_tensor(cgP[:, c, HC:], b[:, 0:TOK], tmpT[:, c, :], ALU.mult), ("z", 4, c))

            await_freed(ve, ("z", 4, CT - 1))
            taps = [0] * CT
            for h in range(HC + 1):
                for c in range(CT):
                    w = col(c, R_CONVW + h)
                    past = convH[:, c, :, h] if h < HC else cgP[:, c, HC + SEQ:]
                    if h == 0:
                        V.tensor_scalar(ybr[:, 1, c, 0:SEQ], cgP[:, c, 0:SEQ], w, None, ALU.mult)
                        taps[c] = mark(V.tensor_scalar(ybr[:, 1, c, SEQ:], past, w, None, ALU.mult))
                    else:
                        ve.wait_ge(S["dve_chain"], taps[c])
                        V.scalar_tensor_tensor(ybr[:, 1, c, 0:SEQ], cgP[:, c, h:h + SEQ], w, ybr[:, 1, c, 0:SEQ], ALU.mult, ALU.add)
                        taps[c] = mark(V.scalar_tensor_tensor(ybr[:, 1, c, SEQ:], past, w, ybr[:, 1, c, SEQ:], ALU.mult, ALU.add))

            for c in range(CT):
                win = 2 << c
                await_freed(ve, ("z", 5, c))
                src = zcP[:, c, :]
                for r in range(c + 1):
                    d = 1 << r
                    dst = sums[:, r % 2, :]
                    link(V.tensor_tensor(dst[:, 2 * d - 1:HP + SEQ], src[:, 2 * d - 1:HP + SEQ], src[:, d - 1:HP + SEQ - d], ALU.add))
                    src = dst
                own = zcP[:, c, HP:HP + SEQ]
                V.scalar_tensor_tensor(ybr[:, 2, c, win - 1:SEQ], src[:, HP + win - 1:HP + SEQ], 1.0 / win, own[:, win - 1:], ALU.mult, ALU.subtract)
                link(V.tensor_tensor(src[:, HP:HP + win - 1], src[:, HP:HP + win - 1], rc[:, 0:win - 1], ALU.mult))
                V.tensor_tensor(ybr[:, 2, c, 0:win - 1], src[:, HP:HP + win - 1], own[:, 0:win - 1], ALU.subtract)
                new = zcP[:, c, HP + SEQ:]
                part = prod[:, :, 0]
                if win > 2:
                    link(V.tensor_reduce(part, poolH[:, c, :, HP - win + 1:HP], AX.X, ALU.add))
                else:
                    link(V.tensor_copy(part, poolH[:, c, :, HP - 1]))
                link(V.tensor_tensor(part, part, new, ALU.add))
                V.scalar_tensor_tensor(ybr[:, 2, c, SEQ:], part, 1.0 / win, new, ALU.mult, ALU.subtract).then_inc(S["pooled_ready"], 1)

            for c in range(CT):
                b = await_full(ve, ("z", 2, c))
                free(V.tensor_tensor(ybr[:, 1, c, :], b[:, 0:TOK], ybr[:, 1, c, :], ALU.mult), ("z", 2, c))
            for c in range(CT):
                b = await_full(ve, ("sg", c))
                V.tensor_tensor(ybr[:, 0, c, 0:SEQ].rearrange("p (t q) -> p t q", t=2), b[:, 0:SEQ].rearrange("p (t q) -> p t q", t=2),
                                sgub[:, c:c + 1, :].to_broadcast([P, 2, P]), ALU.add)
                free(V.tensor_scalar(ybr[:, 0, c, SEQ:], b[:, SEQ:TOK], sgub[:, c, 0:1], None, ALU.add), ("sg", c))
                await_freed(ve, ("sg", c))
                await_freed(ve, ("z", 0, c))
                V.tensor_tensor(ybr[:, 0, c, :], ybr[:, 0, c, :], tmpT[:, c, :], ALU.mult).then_inc(S["ya_ready"], 1)
            for c in range(CT):
                b = await_full(ve, ("pw", c))
                free(V.tensor_scalar(ybr[:, 2, c, :], b[:, 0:TOK], col(c, R_PSC), None, ALU.mult), ("pw", c))

            taps = [0] * CT

            def conf_taps(h0, h1):
                for h in range(h0, h1):
                    for c in range(CT):
                        w = col(c, R_CONFW + h)
                        if h == 0:
                            taps[c] = mark(V.tensor_scalar(dcv[:, c, 0:SEQ], gluP[:, c, 0:SEQ], w, col(c, R_CONFB), ALU.mult, ALU.add))
                        else:
                            ve.wait_ge(S["dve_chain"], taps[c])
                            taps[c] = mark(V.scalar_tensor_tensor(dcv[:, c, 0:SEQ], gluP[:, c, h:h + SEQ], w, dcv[:, c, 0:SEQ], ALU.mult, ALU.add))

            for j in range(4, 12):
                if j == 4:
                    ve.wait_ge(S["ld_mod2"], 16)
                free(ada_out(j), ("ada", j))
                if j == 9:
                    await_freed(ve, ("ada", 9))
                    V.scalar_tensor_tensor(mod[:, 2 * D:3 * D], mod[:, 2 * D:3 * D], 1.0, bc[0:NC_ROWS, 2, :], ALU.add, ALU.mult).then_inc(S["g2_rows"], 1)
                conf_taps(4 * (j - 4), min(4 * (j - 3), HF + 1))
            for c in range(CT):
                w = prm[:, c, R_CONFW:R_CONFW + HF].unsqueeze(1).to_broadcast([P, NS, HF])
                link(V.tensor_tensor(prod, confH[:, c, :, :], w, ALU.mult))
                link(V.tensor_reduce(dcv[:, c, SEQ:], prod, AX.X, ALU.add))
                link(V.scalar_tensor_tensor(dcv[:, c, SEQ:], gluP[:, c, HF + SEQ:], col(c, R_CONFW + HF), dcv[:, c, SEQ:], ALU.mult, ALU.add))
                last = V.tensor_scalar(dcv[:, c, SEQ:], dcv[:, c, SEQ:], col(c, R_CONFB), None, ALU.add)
            last.then_inc(S["dconv_ready"], 1)

            for n, k in enumerate(BR_ORDER):
                if k == 0:
                    b = await_full(ve, "cmean")
                    ve.wait_ge(S["dconv_ready"], 1)
                    free(V.tensor_tensor(dcv[:, :, :], dcv[:, :, :], b[:, 0:TOK].unsqueeze(1).to_broadcast([P, CT, TOK]), ALU.subtract), "cmean")
                if k == 3:
                    await_freed(ve, "cvar")
                    link(V.reciprocal(stat[:, 1, :], stat[:, 0, :]))
                    V.tensor_tensor(dcv[:, :, :], dcv[:, :, :], stat[:, 1:2, :].to_broadcast([P, CT, TOK]), ALU.mult).then_inc(S["dn_ready"], 1)
                for d in range(KT):
                    b = await_full(ve, ("pr", k, d))
                    await_freed(ve, ("zg", k, d))
                    if n == 0:
                        free(V.tensor_tensor(mT[:, d, :], b[:, 0:TOK], sg[:, d, :], ALU.mult), ("pr", k, d))
                    else:
                        free(V.tensor_tensor(sg[:, d, :], b[:, 0:TOK], sg[:, d, :], ALU.mult), ("pr", k, d))
                        await_freed(ve, ("pr", k, d))
                        ins = V.tensor_tensor(mT[:, d, :], mT[:, d, :], sg[:, d, :], ALU.add)
                        if n == 3:
                            ins.then_inc(S["mrg_ready"], 1)
                        else:
                            ins.then_inc(S["sg_used"], 1)
                if 0 < n < 3:
                    ve.wait_ge(S["sg_used"], n * KT)

            def rows_of(i, t, n, a, b):
                return mod[0:n, i * D + a:i * D + b] if t == 2 else bc[0:n, i, a:b]

            for j in range(2):
                for t, (t0, n) in enumerate(TILES):
                    b = await_full(ve, ("mix", j, t))
                    if j == t == 0:
                        await_freed(ve, ("bc", 0, 1))
                    a = slice(j * BLK, (j + 1) * BLK)
                    free(V.tensor_tensor(xn[0:n, t, a], b[0:n, :], rows_of(0, t, n, a.start, a.stop), ALU.mult), ("mix", j, t))
                    await_freed(ve, ("mix", j, t))
                    V.tensor_tensor(x_sb[0:n, t, a], x_sb[0:n, t, a], xn[0:n, t, a], ALU.add).then_inc(S["x2_ready"], 1)
            ve.wait_ge(S["x2_sq"], 1)
            link(V.reciprocal(st[:, :, 2], st[:, :, 1]))
            await_freed(ve, ("bc", 2, 1))
            for t, (t0, n) in enumerate(TILES):
                link(V.scalar_tensor_tensor(xn[0:n, t, :], x_sb[0:n, t, :], st[0:n, t, 2:3], rows_of(2, t, n, 0, D), ALU.mult, ALU.mult))
                last = V.tensor_tensor(xn[0:n, t, :], xn[0:n, t, :], rows_of(1, t, n, 0, D), ALU.add)
            last.then_inc(S["h2_ready"], 1)

            await_freed(ve, "logit")
            link(V.tensor_tensor(bsd[:], sc[:], rtb[:].unsqueeze(1).to_broadcast([P, 3, NE]), ALU.add))
            for t in range(3):
                for q in range(NG):
                    last = V.max(gm[:, t, q, :], bsd[:, t, q * 8:(q + 1) * 8])
            link(last)
            link(V.tensor_tensor(gs[:], gm[:, :, :, 0], gm[:, :, :, 1], ALU.add))
            for t in range(3):
                mine = gs[:, t, :].unsqueeze(2).to_broadcast([P, NG, NG])
                other = gs[:, t, :].unsqueeze(1).to_broadcast([P, NG, NG])
                V.tensor_tensor(cmp_[:, t], other, mine, ALU.is_gt)
                last = V.tensor_tensor(cmp2[:, t], other, mine, ALU.is_equal)
            link(last)
            link(V.tensor_tensor(cmp2[:], cmp2[:], trig[:].unsqueeze(1).to_broadcast([P, 3, NG, NG]), ALU.mult))
            link(V.tensor_tensor(cmp_[:], cmp_[:], cmp2[:], ALU.add))
            link(V.tensor_reduce(gs[:], cmp_[:], AX.X, ALU.add))
            link(V.tensor_scalar(gs[:], gs[:], float(TOPG), None, ALU.is_lt))
            link(V.tensor_scalar(gm[:, :, :, 0], gs[:], -1.0, 1e30, ALU.add, ALU.mult))
            sel_g = gs[:].unsqueeze(3).to_broadcast([P, 3, NG, 8])
            pen_g = gm[:, :, :, 0:1].to_broadcast([P, 3, NG, 8])
            link(V.tensor_tensor(msk[:].rearrange("p t (g e) -> p t g e", g=NG), bsd[:].rearrange("p t (g e) -> p t g e", g=NG), sel_g, ALU.mult))
            link(V.tensor_tensor(msk[:].rearrange("p t (g e) -> p t g e", g=NG), msk[:].rearrange("p t (g e) -> p t g e", g=NG), pen_g, ALU.add))
            for t in range(3):
                last = V.max(gm[:, t, 0, :], msk[:, t, :])
            link(last)
            for t in range(3):
                last = V.match_replace(sel[:, t, :], gm[:, t, 0, :], msk[:, t, :], -3e30)
            link(last)
            link(V.tensor_tensor(sel[:], sel[:], msk[:], ALU.not_equal))
            V.tensor_tensor(sel[:], sel[:], valid[:].unsqueeze(2).to_broadcast([P, 3, NE]), ALU.mult).then_inc(S["sel_ready"], 1)
            ve.wait_ge(S["sel_ready"], 1)

            def shared_act(t):
                t0, n = TILES[t]
                b = await_full(ve, ("sgu", t))
                ve.wait_ge(S["sh_silu_ready"], t + 1)
                if t:
                    await_full(ve, ("saT", t - 1))
                free(V.tensor_tensor(sh_act[0:n, :], b[0:n, FE:2 * FE], sh_silu[0:n, :], ALU.mult), ("sgu", t))

            shared_act(0)
            link(V.tensor_tensor(msk[:], sc[:], sel[:], ALU.mult))
            link(V.tensor_reduce(st[:, :, 3], msk[:], AX.X, ALU.add))
            link(V.tensor_scalar(st[:, :, 3], st[:, :, 3], 1e-38, None, ALU.max))
            link(V.reciprocal(st[:, :, 3], st[:, :, 3]))
            for t in range(3):
                V.tensor_scalar(tab[:, t, :, 1], msk[:, t, :], st[:, t, 3:4], ROUTED_SCALE, ALU.mult, ALU.mult)
                last = V.tensor_tensor_scan(rnk[:, t, :], ones[:, 0:NE], sel[:, t, :], 0.0, ALU.mult, ALU.add)
            link(last)
            link(V.tensor_tensor(rnk[:], rnk[:], sel[:], ALU.subtract))
            for t in range(3):
                V.tensor_scalar(tab[:, t, :, 0], sel[:, t, :], 0.0, tokid[:, t:t + 1], ALU.mult, ALU.add)
            link(V.tensor_scalar(tok8[:], tokid[:], 8.0, -BIG, ALU.mult, ALU.add))
            for t in range(3):
                last = V.tensor_scalar(tab[:, t, :, 2], rnk[:, t, :], tok8[:, t:t + 1], None, ALU.add)
            link(last)
            V.tensor_scalar(tab[:, :, :, 0], tab[:, :, :, 0], -BIG, None, ALU.add)
            b = await_full(ve, "slot")
            link(V.tensor_scalar(posm[:], sel[:], -1.0, 1e6, ALU.add, ALU.mult))
            V.tensor_reduce(cnt_f[:], b[:, 3 * NE:4 * NE], AX.X, ALU.max)
            free(V.tensor_tensor(posm[:].rearrange("p t e -> p (t e)"), b[:, 0:3 * NE], posm[:].rearrange("p t e -> p (t e)"), ALU.add), "slot")
            await_freed(ve, "slot")
            V.tensor_copy(cnt_i[:], cnt_f[:]).then_inc(S["cnt_ready"], 1)

            def one_hot(i, j):
                e = UNROLL * i + j
                need(ve, S["list_done"], e - 1)
                for t in range(3):
                    p = posm[:, t, e:e + 1] if isinstance(e, int) else posm[:, t, bass.ds(e, 1)]
                    last = V.tensor_scalar(oh[:, j % 2, t, :], iota_f[:], p, None, ALU.is_equal)
                last.then_inc(S["oh_ready"], 1)

            def list_out(i, j):
                e = UNROLL * i + j
                ve.wait_ge(S["list_done"], e + 1)
                need(ve, scattered[j % 2], 16 * (2 * i + j // 2 - 1))
                V.tensor_scalar(idx[:, j, :], psum[:, 7, 0:3], BIG, None, ALU.add)
                V.tensor_copy(gcol[:, j, :], psum[:, 7, 1:2]).then_inc(S["lst_ready"], 1)

            def rows_out(i, j):
                e = UNROLL * i + j
                ve.wait_ge(S["xt_done"], e + 1)
                need(ve, S["gu_done"], e - 1)
                V.tensor_copy(xgT[:, j % 2, 4:8, :], psum[:, 6, :].rearrange("p (k c) -> p k c", k=4)).then_inc(S["xgt_dve"], 1)

            def gated(i, j):
                e = UNROLL * i + j
                ve.wait_ge(S["silu_ready"], e + 1)
                need(ve, S["tact_done"], e - 1)
                V.scalar_tensor_tensor(act[:, j % 2, :], psum[:, j % 2, FE:2 * FE], gcol[:, j, :], silu[:, j % 2, :],
                                       ALU.mult, ALU.mult).then_inc(S["act_ready"], 1)

            def y_out(i, j):
                e = UNROLL * i + j
                ve.wait_ge(S["dn_done"], e + 1)
                need(ve, scattered[j % 2], 16 * (2 * i + j // 2))
                V.tensor_copy(y_rows[:, j % 2, BLK:2 * BLK], psum[:, 4, :]).then_inc(S["ys_dve"], 1)

            def body(i, first=False, last=False):
                for j in range(UNROLL):
                    prev = not (first and j == 0)
                    pi, pj = (i if j else i - 1), (j - 1) % UNROLL
                    if not (last and j >= 2):
                        one_hot(i if j < 2 else i + 1, (j + 2) % UNROLL)
                    gated(i, j)
                    if prev:
                        y_out(pi, pj)
                    if not (last and j == UNROLL - 1):
                        rows_out(i if j < 3 else i + 1, (j + 1) % UNROLL)
                    if not (last and j >= 2):
                        list_out(i if j < 2 else i + 1, (j + 2) % UNROLL)

            one_hot(0, 0)
            one_hot(0, 1)
            shared_act(1)
            shared_act(2)
            list_out(0, 0)
            list_out(0, 1)
            rows_out(0, 0)
            body(0, first=True)
            with ve.Fori(1, NE // UNROLL - 1) as i:
                body(i)
            body(NE // UNROLL - 1, last=True)
            y_out(NE // UNROLL - 1, UNROLL - 1)

            def extra(r, e, n):
                for t in range(3):
                    last = V.tensor_scalar(oh[:, 0, t, :], iota_f[:], posm[:, t, bass.ds(e, 1)], float(-CAP * r), ALU.subtract, ALU.is_equal)
                last.then_inc(S["x_oh"], 1)
                ve.wait_ge(S["x_list"], n + 1)
                V.tensor_scalar(idx[:, 0, :], psum[:, 7, 0:3], BIG, None, ALU.add)
                V.tensor_copy(gcol[:, 0, :], psum[:, 7, 1:2]).then_inc(S["x_idx"], 1)
                ve.wait_ge(S["x_xt"], n + 1)
                V.tensor_copy(xgT[:, 0, :, :], psum[:, 5:7, :].rearrange("p b (k c) -> p (b k) c", k=4)).then_inc(S["x_xgt"], 1)
                ve.wait_ge(S["x_silu"], n + 1)
                V.scalar_tensor_tensor(act[:, 0, :], psum[:, 0, FE:2 * FE], gcol[:, 0, :], silu[:, 0, :], ALU.mult, ALU.mult).then_inc(S["x_act"], 1)
                ve.wait_ge(S["x_dn"], n + 1)
                V.tensor_copy(y_rows[:, 0, :].rearrange("p (b n) -> p b n", b=2), psum[:, 3:5, :]).then_inc(S["x_y"], 1)
                ve.wait_ge(S["x_sc"], 16 * n + 16)

            extra_passes(ve, extra)
            await_freed(ve, ("bc", 3, 1))
            for t, (t0, n) in enumerate(TILES):
                ve.wait_ge(fin_ld[t], 16)
                link(V.tensor_reduce(xn[0:n, t, :], fin_y[0:n, t].rearrange("p r d -> p d r"), AX.X, ALU.add))
                link(V.tensor_tensor(xn[0:n, t, :], xn[0:n, t, :], shared[0:n, t, :], ALU.add))
                link(V.tensor_tensor(xn[0:n, t, :], xn[0:n, t, :], rows_of(3, t, n, 0, D), ALU.mult))
                V.tensor_tensor(x_sb[0:n, t, :], x_sb[0:n, t, :], xn[0:n, t, :], ALU.add).then_inc(S["fin_red"], 1)
            ve.wait_ge(S["ld_fin"], 16)
            for t, (t0, n) in enumerate(TILES):
                ve.wait_ge(S["fin_sq"], t + 1)
                link(V.reciprocal(st[0:n, t, 2:3], st[0:n, t, 1:2]))
                V.scalar_tensor_tensor(x_sb[0:n, t, :], x_sb[0:n, t, :], st[0:n, t, 2:3], fing[0:n, :], ALU.mult, ALU.mult).then_inc(S["fin_ready"], 1)


_INS = ["x_prompt", "x_sample", "state_conv", "state_pool", "state_conf", "c_prompt", "c_sample",
        "ada_w", "ada_b", "norm1_g", "norm2_g", "w_in", "sgu_ln_g", "sgu_ln_b", "sgu_w", "sgu_b",
        "conv_w", "pool_w", "pool_scale", "conf_w", "conf_b", "conf_ln_g", "conf_ln_b",
        "w_branch", "w_out", "router_w", "router_bias", "e_gate", "e_up", "e_down",
        "s_gate", "s_up", "s_down", "final_g"]
_OUTS = [(1, SEQ, D), (NS, 1, D), (1, 1, HC, BR), (1, 1, HP, BR), (1, 1, HF, BR),
         (1, NS, HC, BR), (1, NS, HP, BR), (1, NS, HF, BR), (1, NS, 1, BR)]


def kernel(**inputs):
    import concourse.bacc as _bacc
    from concourse.bass_utils import run_bass_kernel_spmd as _run

    nc = _bacc.Bacc("TRN2", target_bir_lowering=False, num_devices=1)
    arrays, args = {}, []
    for name in _INS:
        a = np.ascontiguousarray(inputs[name])
        arrays[f"in_{name}"] = a
        args.append(nc.dram_tensor(f"in_{name}", a.shape, F32, kind="ExternalInput").ap())
    for i, shape in enumerate(_OUTS):
        args.append(nc.dram_tensor(f"out_{i}", shape, F32, kind="ExternalOutput").ap())
    args.append(nc.dram_tensor("h_table", (TOK, D), F32, kind="Internal").ap())
    args.append(nc.dram_tensor("y_table", (TOK * 8, D), F32, kind="Internal").ap())
    bass_decoder_step(nc, *args)
    r = _run(nc, [arrays], core_ids=[0])
    return tuple(r.results[0][f"out_{i}"] for i in range(len(_OUTS)))
```

```python
from contextlib import ExitStack

import numpy as np

import concourse.bass as bass
from concourse import mybir

F32 = mybir.dt.float32
I32 = mybir.dt.int32
ALU = mybir.AluOpType
ACT = mybir.ActivationFunctionType
AX = mybir.AxisListType

P = 128
D = 1024
KT = D // P
BR = D // 2
CT = BR // P
SEQ = 256
NS = 8
TOK = SEQ + NS
TILES = [(0, P), (P, P), (2 * P, NS)]
NC_ROWS = NS + 1
HC, HP, HF = 2, 15, 30
NE = 64
NG = 8
TOPG = 4
FE = D // 4
EPS = 1e-6
ROUTED_SCALE = 2.5
BLK = 512
RING = 3
NBANK = 8

R_CONFW, R_CONVW, R_CONFB, R_CLNG, R_CLNB, R_PSC, R_N1G = 0, 31, 34, 35, 36, 37, 38
NPROW = 40

BLOCKS = ([("ada", j) for j in range(4)]
          + [("win", j) for j in (1, 7, 6, 3, 4, 5, 2, 0)]
          + [("ada", j) for j in range(4, 12)]
          + [x for k in (2, 1, 0, 3) for x in (("win", 8 + 2 * k), ("win", 9 + 2 * k), ("br", k))]
          + [("out", 0), ("out", 1)])
SLOT = {b: i for i, b in enumerate(BLOCKS)}
BR_ORDER = (2, 1, 0, 3)
MIX_ORDER = (2, 0, 1)
LIST_BANK = 7


def jobs_of_mixer():
    out = ["cT", "prow0", "wsT"]
    out += [("hist", n) for n in range(4)]
    for kind, j in BLOCKS:
        if kind == "ada":
            out.append(("ada", j))
            if j == 3:
                out.append("modT")
                out += [("hT", k) for k in range(KT)]
            if j in (5, 7, 9, 11):
                out += [("bc", (j - 4) // 2, h) for h in range(2)]
        elif kind == "win" and j == 1:
            out += [("v", t) for t in range(3)]
        elif kind == "win" and j < 8:
            out += [("z", j, c) for c in range(CT)]
            if j == 6:
                out.append("st_conf")
            if j == 4:
                out.append("st_conv")
            if j == 5:
                out.append("st_pool")
            if j == 0:
                out += [("sg", g) for g in range(CT)]
                out += [("pw", g) for g in range(CT)]
        elif kind == "win":
            k, half = (j - 8) // 2, (j - 8) % 2
            if half == 0:
                out += {0: ["cmean"], 3: ["cvar"]}.get(k, [])
            out += [("zg", k, 4 * half + c) for c in range(CT)]
        elif kind == "br":
            out += [("pr", j, d) for d in range(KT)]
    for n, t in enumerate(MIX_ORDER):
        out += [("mix", t, 0), ("mix", t, 1)]
        if n:
            out += [("h2T", MIX_ORDER[n - 1], h) for h in range(2)]
    out += [("h2T", MIX_ORDER[-1], h) for h in range(2)]
    out += ["logit"] + [(part, j) for j in range(2) for part in ("shared_gate", "shared_up")]
    out += ["slot", "lists"]
    out += [("sy", t, h) for t in range(3) for h in range(2)]
    return out


JOBS = jobs_of_mixer()
JOB = {name: i for i, name in enumerate(JOBS)}
FIRST_BANK = (LIST_BANK - JOB["lists"]) % NBANK


def bank_of(name):
    return (JOB[name] + FIRST_BANK) % NBANK, JOB[name] // NBANK


LAST_JOB = {}
for _kind, _j in BLOCKS:
    if _kind == "ada":
        LAST_JOB["ada", _j] = ("ada", _j)
    elif _kind == "br":
        LAST_JOB["br", _j] = ("pr", _j, KT - 1)
    elif _kind == "out":
        LAST_JOB["out", _j] = ("mix", MIX_ORDER[-1], _j)
    elif _j == 1:
        LAST_JOB["win", 1] = ("v", 2)
    elif _j < 8:
        LAST_JOB["win", _j] = ("z", _j, CT - 1)
    else:
        LAST_JOB["win", _j] = ("zg", (_j - 8) // 2, 4 * ((_j - 8) % 2) + CT - 1)

BIG = 4096.0
CAP = P
ROUNDS = -(-TOK // CAP)
UNROLL = 4
NPARAM = 8
SLOTF = 2 * KT * FE + 2 * D


def bass_decoder_step(nc, x_prompt, x_sample, state_conv, state_pool, state_conf, c_prompt, c_sample,
                      ada_w, ada_b, norm1_g, norm2_g, w_in, sgu_ln_g, sgu_ln_b, sgu_w, sgu_b,
                      conv_w, pool_w, pool_scale, conf_w, conf_b, conf_ln_g, conf_ln_b,
                      w_branch, w_out, router_w, router_bias, e_gate, e_up, e_down,
                      s_gate, s_up, s_down, final_g,
                      y_prompt, y_sample, conv_p, pool_p, conf_p, conv_s, pool_s, conf_s, chunk_v_s,
                      h_table, y_even, y_odd):
    with ExitStack() as ctx:
        def sb(name, shape, dt=F32):
            return ctx.enter_context(nc.sbuf_tensor(name, shape, dt))

        def sem(name):
            return ctx.enter_context(nc.semaphore(name))

        psum = ctx.enter_context(nc.psum_tensor("psum", [P, NBANK, 512], F32))

        wexp = sb("wexp", [P, UNROLL, SLOTF])
        ring = wexp[:, 2:4, :].rearrange("p a n -> p (a n)").rearrange("p (s n) -> p s n", s=RING)
        early = wexp[:, 0:2, :].rearrange("p a n -> p (a n)")
        used = [0]

        def take(n):
            at = used[0]
            used[0] += n
            assert used[0] <= 2 * SLOTF
            return early[:, at:at + n]

        sg = take(KT * TOK).rearrange("p (k t) -> p k t", k=KT)
        ybr = take(4 * CT * TOK).rearrange("p (b c t) -> p b c t", b=4, c=CT)
        tmpT = take(CT * TOK).rearrange("p (c t) -> p c t", c=CT)
        gluP = take(CT * (HF + TOK)).rearrange("p (c t) -> p c t", c=CT)
        zcP = take(CT * (HP + TOK)).rearrange("p (c t) -> p c t", c=CT)
        cgP = take(CT * (HC + TOK)).rearrange("p (c t) -> p c t", c=CT)
        convH = take(CT * NS * HC).rearrange("p (c s h) -> p c s h", c=CT, h=HC)
        poolH = take(CT * NS * HP).rearrange("p (c s h) -> p c s h", c=CT, h=HP)
        confH = take(CT * NS * HF).rearrange("p (c s h) -> p c s h", c=CT, h=HF)

        x_sb = sb("x_sb", [P, 3, D])
        xn = sb("xn", [P, 3, D])
        hT = sb("hT", [P, KT, TOK])
        mod = sb("mod", [NC_ROWS, 4 * D])
        bc = sb("bc", [P, 4, D])
        mT = sb("mT", [P, KT, TOK])
        mid = sb("mid", [P, 5 * D + 64])
        dcv = mid[:, 0:CT * TOK].rearrange("p (c t) -> p c t", c=CT)
        v_sb = mid[:, 1056:2592].rearrange("p (t c) -> p t c", t=3)
        lnv = mid[:, 2592:3616].rearrange("p (a c) -> p a c", a=2)
        sgub = mid[:, 3616:4128].rearrange("p (g q) -> p g q", g=CT)
        poolw = mid[:, 4128:4640].rearrange("p (g q) -> p g q", g=CT)
        wsT = mid[:, 4640:5152].rearrange("p (g q) -> p g q", g=CT)
        crow = mid[0:NC_ROWS, 0:D]
        shared = mid[:, 0:3 * D].rearrange("p (t d) -> p t d", t=3)
        xgT = mid[:, 3 * D:5 * D].rearrange("p (b k c) -> p b k c", b=2, k=KT)
        w00 = sb("w00", [NS, CT])
        wdiag = sb("wdiag", [NS, CT, NS])
        rtw = sb("rtw", [P, KT, NE])
        rtb = sb("rtb", [P, NE])
        cT = sb("cT", [P, KT, NC_ROWS])
        prm = sb("prm", [P, CT, NPROW])
        S1 = sb("S1", [P, KT, NC_ROWS])
        G1 = sb("G1", [P, KT, NC_ROWS])
        ident = sb("ident", [P, P])
        lower = sb("lower", [P, P])
        iota_i = sb("iota_i", [P, P], I32)
        iota_f = sb("iota_f", [P, P])
        ones = sb("ones", [P, P])
        cmean = sb("cmean", [P, P])
        sel8 = sb("sel8", [NC_ROWS, P])
        rc = sb("rc", [P, 16])
        st = sb("st", [P, 3, 8])
        bns = sb("bns", [P, 3, 8])
        sc = sb("sc", [P, 3, NE])
        bsd = sb("bsd", [P, 3, NE])
        msk = sb("msk", [P, 3, NE])
        sel = sb("sel", [P, 3, NE])
        posm = sb("posm", [P, 3, NE])
        tab = sb("tab", [P, 3, NE, 2])
        cmp2 = sb("cmp2", [P, 3, NG, NG])
        epsc = sb("epsc", [P, 1])
        gm = sb("gm", [P, 3, NG, 8])
        gs = sb("gs", [P, 3, NG])
        cmp_ = sb("cmp_", [P, 3, NG, NG])
        trig = sb("trig", [P, NG, NG])
        tokid = sb("tokid", [P, 3])
        valid = sb("valid", [P, 3])
        cnt_f = sb("cnt_f", [P, 1])
        cnt_i = sb("cnt_i", [P, 1], I32)
        lst = sb("lst", [P, 4])
        tokid_i = sb("tokid_i", [P, 3], I32)
        idx = sb("idx", [P, UNROLL, 1], I32)
        scatter_row = sb("scatter_row", [P, UNROLL, 1], I32)
        gcol = sb("gcol", [P, UNROLL, 1])
        hist = mT[:, :, :].rearrange("p k t -> p (k t)")[:, 0:4 * BR].rearrange("p (n c) -> p n c", n=4)
        hTf = hT[:, :, :].rearrange("p k t -> p (k t)")
        prow = hTf[0:NPROW, 0:BR]
        wsr = hTf[:, BR:2 * BR].rearrange("p (g q) -> p g q", g=CT)
        st_rows = bc[:, 3, :].rearrange("p (a c) -> p a c", a=2)
        st_conf, st_conv, st_pool = st_rows[:, 0, :], st_rows[:, 1, :], bc[:, 1, 0:BR]
        y_rows = mT[:, :, :].rearrange("p k t -> p (k t)")[:, 0:2 * D].rearrange("p (b d) -> p b d", b=2)
        xg = [xn[:, 0, :], xn[:, 1, :], xn[:, 2, :], bc[:, 2, :]]
        xnf = xn[:, :, :].rearrange("p t d -> p (t d)")
        sums = xnf[:, 0:544].rearrange("p (a n) -> p a n", a=2)
        prod = xnf[:, 544:784].rearrange("p (s h) -> p s h", s=NS)
        stat = xnf[:, 784:784 + 2 * TOK].rearrange("p (a t) -> p a t", a=2)
        silu = hTf[:, 0:512].rearrange("p (b f) -> p b f", b=2)
        act = hTf[:, 512:1024].rearrange("p (b f) -> p b f", b=2)
        actT = hTf[:, 1024:1536].rearrange("p (b j c) -> p b j c", b=2, j=2)
        mTf = mT[:, :, :].rearrange("p k t -> p (k t)")
        sh_silu = mTf[:, 0:2 * TOK].rearrange("p (j t) -> p j t", j=2)
        sh_actT = mTf[:, 2 * TOK:4 * TOK].rearrange("p (j t) -> p j t", j=2)
        fing = bc[:, 0, :]
        oh = bc[:, 1, 0:6 * P].rearrange("p (b t c) -> p b t c", b=2, t=3)

        bank_full = [sem(f"bank_full{b}") for b in range(NBANK)]
        bank_free = [sem(f"bank_free{b}") for b in range(NBANK)]
        ring_full = [sem(f"ring_full{s}") for s in range(RING)]
        names = """cnt_ready ld_mod2 mrg_ready sh_load dn_done x_xt x_w moe_done fin_ready
                   out_done pool_chain consts ld_stage wg_masked states_done v_ready tables_zero st_stored
                   h2_ready h2_stored x2_ready ld_fin lst_ready xt_done dma_may_go scatter_row_ready ys_act
                   ys_dve x_idx x_gat x_y x_sc fin_sum c_silu x_norm h_ready
                   ws_ready ld_param pooled_ready g2_rows dconv_ready sq_ready ya_ready sel_ready oh_ready
                   list_done xgt_act xgt_dve act_ready gu_done actT_ready tact_done x_oh x_list
                   x_xgt x_gu x_act x_tact x_actT x_dn act_chain ld_c ld_x
                   x_sq v_mean v_std dn_ready yd_ready x2_sq silu_ready x_silu fin_red
                   fin_sq dve_chain ld_mod sg_used""".split()
        S = {n: sem(n) for n in names}
        fin_ld = [sem(f"fin_ld{t}") for t in range(3)]
        gathered = [sem(f"gathered{b}") for b in range(UNROLL)]
        scattered = [sem(f"scattered{b}") for b in range(2)]
        gu_full = [sem(f"gu_full{s}") for s in range(UNROLL)]
        down_full = [sem(f"down_full{s}") for s in range(UNROLL)]

        def col(c, r, n=P):
            return prm[0:n, c, r:r + 1]

        def await_full(eng, name):
            b, before = bank_of(name)
            eng.wait_ge(bank_full[b], before + 1)
            return psum[:, b, :]

        def free(ins, name):
            return ins.then_inc(bank_free[bank_of(name)[0]], 1)

        def await_freed(eng, name):
            b, before = bank_of(name)
            eng.wait_ge(bank_free[b], before + 1)

        def need(eng, sem_, value):
            if not isinstance(value, int) or value > 0:
                eng.wait_ge(sem_, value)

        def block_source(kind, j):
            if kind == "ada":
                return ada_w[0, :, j * BLK:(j + 1) * BLK].rearrange("(k p) n -> p k n", p=P)
            if kind == "win":
                return w_in[0, :, j * BLK:(j + 1) * BLK].rearrange("(k p) n -> p k n", p=P)
            if kind == "br":
                return w_branch[0, j].rearrange("(k p) n -> p k n", p=P)
            return w_out[0, :, j * BLK:(j + 1) * BLK].rearrange("(k p) n -> p k n", p=P)

        def ring_view(kind, j):
            k = CT if kind == "br" else KT
            return ring[:, SLOT[kind, j] % RING, :].rearrange("p (k n) -> p k n", k=k)

        w_gu = [wexp[:, s, 0:4096].rearrange("p (a k f) -> p k a f", a=2, k=KT) for s in range(UNROLL)]
        w_dn = [wexp[:, s, 4096:6144].rearrange("p (j n) -> p j n", j=2) for s in range(UNROLL)]
        gate_v = e_gate[0].rearrange("e (p k) f -> e p (k f)", k=KT)
        up_v = e_up[0].rearrange("e (p k) f -> e p (k f)", k=KT)
        down_v = e_down[0].rearrange("e (p j) n -> e p (j n)", j=2)
        fin_y = wexp[:, 0:1, :].rearrange("p s n -> p (s n)").rearrange("p (t a d) -> p t a d", t=3, a=2)

        def extra_passes(eng, step):
            eng.wait_ge(S["cnt_ready"], 1)
            longest = eng.value_load(cnt_i[0:1, 0:1], min_val=0, max_val=TOK)
            with eng.If(longest > CAP):
                for r in range(1, ROUNDS):
                    with eng.Fori(0, NE) as e:
                        step(r, e, NE * (r - 1) + e)

        block = ctx.enter_context(nc.Block())

        @block.sync
        def _(sp):
            for i, (kind, j) in enumerate(BLOCKS):
                if i >= RING:
                    await_full(sp, LAST_JOB[BLOCKS[i - RING]])
                sp.dma_start(ring_view(kind, j), block_source(kind, j)).then_inc(ring_full[i % RING], 16)
                if BLOCKS[i] == ("ada", 5):
                    await_full(sp, "modT")
                    sp.dma_start(mod[:, :], ada_b[0:1, 2 * D:].to_broadcast([NC_ROWS, 4 * D])).then_inc(S["ld_mod2"], 16)
            sp.wait_ge(S["mrg_ready"], KT)
            sp.dma_start(wexp[:, 1, 0:2048], s_gate[0].rearrange("(p k) f -> p (k f)", k=KT)).then_inc(S["sh_load"], 16)
            sp.dma_start(wexp[:, 1, 2048:4096], s_up[0].rearrange("(p k) f -> p (k f)", k=KT)).then_inc(S["sh_load"], 16)
            sp.dma_start(wexp[:, 1, 4096:6144], s_down[0].rearrange("(p j) n -> p (j n)", j=2)).then_inc(S["sh_load"], 16)

            def load_expert(e, s):
                sp.dma_start(wexp[:, s, 0:2048], gate_v[e]).then_inc(gu_full[s], 16)
                sp.dma_start(wexp[:, s, 2048:4096], up_v[e]).then_inc(gu_full[s], 16)
                sp.dma_start(wexp[:, s, 4096:6144], down_v[e]).then_inc(down_full[s], 16)

            load_expert(0, 0)
            await_full(sp, ("mix", MIX_ORDER[-1], 1))
            load_expert(2, 2)
            load_expert(3, 3)
            await_full(sp, ("sy", 2, 1))
            load_expert(1, 1)
            with sp.Fori(1, NE // UNROLL) as i:
                for s in range(UNROLL):
                    sp.wait_ge(S["dn_done"], UNROLL * i + (s - 3))
                    for w, base, f, n in ((e_gate, 0, gu_full[s], 2048), (e_up, 2048, gu_full[s], 2048),
                                          (e_down, 4096, down_full[s], 2048)):
                        view = {0: gate_v, 2048: up_v, 4096: down_v}[base]
                        sp.dma_start(wexp[:, s, base:base + n], view[bass.ds(UNROLL * i + s, 1)].rearrange("e p n -> (e p) n")).then_inc(f, 16)

            def extra(r, e, n):
                sp.wait_ge(S["x_xt"], n + 1)
                for at, view in ((0, gate_v), (2048, up_v), (4096, down_v)):
                    sp.dma_start(wexp[:, 0, at:at + 2048], view[bass.ds(e, 1)].rearrange("e p n -> (e p) n")).then_inc(S["x_w"], 16)

            sp.wait_ge(S["dn_done"], NE)
            extra_passes(sp, extra)
            sp.wait_ge(S["moe_done"], 1)
            for t, (t0, n) in enumerate(TILES):
                for a, table in enumerate((y_even, y_odd)):
                    sp.dma_start(fin_y[0:n, t, a], table[t0:t0 + n]).then_inc(fin_ld[t], 16)
            for t, (t0, n) in enumerate(TILES):
                sp.wait_ge(S["fin_ready"], t + 1)
                dst = y_sample[:, 0, :] if t == 2 else y_prompt[0, t0:t0 + n, :]
                sp.dma_start(dst, x_sb[0:n, t, :]).then_inc(S["out_done"], 16)
            sp.wait_ge(S["out_done"], 3 * 16)

        @block.gpsimd
        def _(pool):
            n_chain = [0]

            def link(ins):
                n_chain[0] += 1
                ins.then_inc(S["pool_chain"], 1)
                pool.wait_ge(S["pool_chain"], n_chain[0])

            g = nc.gpsimd
            g.memset(ident[:], 0.0)
            g.memset(xn[:, 2, :], 0.0)
            g.memset(sel8[:], 0.0)
            g.memset(ones[:], 1.0)
            g.memset(cmean[:], 1.0 / BR)
            g.memset(lower[:], 1.0)
            g.memset(trig[:], 1.0)
            link(g.memset(valid[:], 1.0))
            g.affine_select(out=ident[:], in_=ident[:], compare_op=ALU.not_equal, fill=1.0, base=0,
                            pattern=[[-1, P]], channel_multiplier=1).then_inc(S["consts"], 1)
            g.affine_select(out=sel8[:], in_=sel8[:], compare_op=ALU.not_equal, fill=1.0, base=-NS,
                            pattern=[[0, P]], channel_multiplier=1)
            g.affine_select(out=lower[:], in_=lower[:], compare_op=ALU.is_ge, fill=0.0, base=-1,
                            pattern=[[1, P]], channel_multiplier=-1)
            g.affine_select(out=trig[:], in_=trig[:], compare_op=ALU.is_ge, fill=0.0, base=-1,
                            pattern=[[1, NG], [-1, NG]], channel_multiplier=0)
            g.affine_select(out=valid[:], in_=valid[:], compare_op=ALU.is_ge, fill=0.0, base=TOK - 1,
                            pattern=[[-P, 3]], channel_multiplier=-1)
            g.iota(iota_i[:], pattern=[[1, P]], base=0, channel_multiplier=0)
            g.iota(tokid_i[:], pattern=[[P, 3]], base=0, channel_multiplier=1)
            g.memset(gluP[:, :, 0:HF], 0.0)
            g.memset(zcP[:, :, 0:HP], 0.0)
            g.memset(cgP[:, :, 0:HC], 0.0)
            g.memset(st[:], 1.0)
            g.memset(bns[:], 1.0)
            g.memset(epsc[:], EPS)
            g.memset(sc[:], 0.0).then_inc(S["consts"], 1)
            pool.wait_ge(S["ld_stage"], 12 * 16)
            g.affine_select(out=wsr, in_=wsr, compare_op=ALU.is_ge, fill=0.0, base=0,
                            pattern=[[0, CT], [-1, P]], channel_multiplier=1).then_inc(S["wg_masked"], 1)
            with nc.allow_non_contiguous_dma(reason="history rows"):
                g.dma_start(conv_s[0, :, 0:HC - 1, :], state_conv[0, :, 1:HC, :]).then_inc(S["states_done"], 16)
                g.dma_start(pool_s[0, :, 0:HP - 1, :], state_pool[0, :, 1:HP, :]).then_inc(S["states_done"], 16)
                g.dma_start(conf_s[0, :, 0:HF - 1, :], state_conf[0, :, 1:HF, :]).then_inc(S["states_done"], 16)
            pool.wait_ge(S["v_ready"], 1)
            for table in (y_even, y_odd):
                g.dma_start(table[0:2 * (P - NS)].rearrange("(a p) d -> p a d", p=P - NS),
                            xn[NS:P, 2:3, :].to_broadcast([P - NS, 2, D])).then_inc(S["tables_zero"], 16)
                g.dma_start(table[2 * (P - NS):TOK], xn[NS:NS + TOK - 2 * (P - NS), 2, :]).then_inc(S["tables_zero"], 16)
            g.dma_start(chunk_v_s[0, :, 0, :], v_sb[0:NS, 2, :]).then_inc(S["states_done"], 16)
            for name, rows, h, prompt, sample in (("st_conf", st_conf, HF, conf_p, conf_s), ("st_conv", st_conv, HC, conv_p, conv_s),
                                                  ("st_pool", st_pool, HP, pool_p, pool_s)):
                await_freed(pool, name)
                g.dma_start(prompt[0, 0], rows[0:h, :]).then_inc(S["st_stored"], 16)
                g.dma_start(sample[0, :, h - 1, :], rows[h:h + NS, :]).then_inc(S["st_stored"], 16)
            for m, t in enumerate(MIX_ORDER):
                t0, n = TILES[t]
                pool.wait_ge(S["h2_ready"], m + 1)
                g.dma_start(h_table[t0:t0 + n], xn[0:n, t, :]).then_inc(S["h2_stored"], 16)
            pool.wait_ge(S["x2_ready"], 6)
            g.dma_start(fing, final_g.rearrange("(a d) -> a d", a=1).to_broadcast([P, D])).then_inc(S["ld_fin"], 16)
            pool.wait_ge(S["h2_stored"], 3 * 16)
            pool.wait_ge(S["tables_zero"], 4 * 16)

            last_token = pool.alloc_register("last_token")
            pool.reg_mov(last_token, TOK - 1)

            def gather(i, j):
                e = UNROLL * i + j
                pool.wait_ge(S["lst_ready"], e + 1)
                need(pool, S["xt_done"], e - 3)
                pool.sem_inc(S["dma_may_go"], 1)
                g.indirect_dma_start(out=xg[j], out_offset=None, in_=h_table,
                                     in_offset=bass.IndirectOffsetOnAxis(ap=idx[:, j, 0:1].bitcast(mybir.dt.uint32), axis=0),
                                     bounds_check=last_token, oob_is_err=False).then_inc(gathered[j], 16)

            def scatter(i, j):
                e = UNROLL * i + j
                pool.wait_ge(S["scatter_row_ready"], e + 1)
                need(pool, scattered[j % 2], 16 * (2 * i + j // 2))
                pool.wait_ge(S["ys_act"], e + 1)
                pool.wait_ge(S["ys_dve"], e + 1)
                pool.sem_inc(S["dma_may_go"], 1)
                g.indirect_dma_start(out=(y_even, y_odd)[j % 2], out_offset=bass.IndirectOffsetOnAxis(ap=scatter_row[:, j, :].bitcast(mybir.dt.uint32), axis=0),
                                     in_=y_rows[:, j % 2, :], in_offset=None,
                                     bounds_check=last_token, oob_is_err=False, compute_op=ALU.add).then_inc(scattered[j % 2], 16)

            await_full(pool, ("h2T", MIX_ORDER[-1], 1))
            for j in range(UNROLL):
                gather(0, j)

            def body(i, first=False, last=False):
                for j in range(UNROLL):
                    if not (first and j == 0):
                        scatter(i if j else i - 1, (j - 1) % UNROLL)
                    if not last:
                        gather(i + 1, j)

            body(0, first=True)
            with pool.Fori(1, NE // UNROLL - 1) as i:
                body(i)
            body(NE // UNROLL - 1, last=True)
            scatter(NE // UNROLL - 1, UNROLL - 1)
            pool.wait_ge(scattered[0], 16 * (NE // 2))
            pool.wait_ge(scattered[1], 16 * (NE // 2))

            def extra(r, e, n):
                pool.wait_ge(S["x_idx"], n + 1)
                pool.sem_inc(S["dma_may_go"], 1)
                g.indirect_dma_start(out=xg[0], out_offset=None, in_=h_table,
                                     in_offset=bass.IndirectOffsetOnAxis(ap=idx[:, 0, 0:1].bitcast(mybir.dt.uint32), axis=0),
                                     bounds_check=last_token, oob_is_err=False).then_inc(S["x_gat"], 16)
                pool.wait_ge(S["x_y"], n + 1)
                pool.sem_inc(S["dma_may_go"], 1)
                g.indirect_dma_start(out=y_even, out_offset=bass.IndirectOffsetOnAxis(ap=idx[:, 0, 0:1].bitcast(mybir.dt.uint32), axis=0),
                                     in_=y_rows[:, 0, :], in_offset=None,
                                     bounds_check=last_token, oob_is_err=False, compute_op=ALU.add).then_inc(S["x_sc"], 16)
                pool.wait_ge(S["x_sc"], 16 * n + 16)

            extra_passes(pool, extra)
            pool.sem_inc(S["moe_done"], 1)
            for t in (1, 2):
                n = TILES[t][1]
                pool.wait_ge(fin_ld[t], 2 * 16)
                g.tensor_tensor(out=fin_y[0:n, t, 0], in0=fin_y[0:n, t, 0], in1=fin_y[0:n, t, 1], op=ALU.add).then_inc(S["fin_sum"], 1)
            pool.wait_ge(S["states_done"], 4 * 16)
            pool.wait_ge(S["st_stored"], 6 * 16)

        @block.tensor
        def _(pe):
            mm = nc.tensor.matmul

            def claim(name):
                b, before = bank_of(name)
                need(pe, bank_free[b], before)
                return psum[:, b, :]

            def full(ins, name):
                ins.then_inc(bank_full[bank_of(name)[0]], 1)

            def weights(kind, j):
                i = SLOT[kind, j]
                pe.wait_ge(ring_full[i % RING], 16 * (i // RING + 1))
                return ring_view(kind, j)

            def turn(out, src, rows):
                return nc.tensor.transpose(out, src, ident[0:rows, 0:rows])

            pe.wait_ge(S["consts"], 2)
            pe.wait_ge(S["c_silu"], 1)
            out = claim("cT")
            for k in range(KT):
                last = turn(out[:, k * NC_ROWS:(k + 1) * NC_ROWS], crow[:, k * P:(k + 1) * P], NC_ROWS)
            full(last, "cT")
            pe.wait_ge(S["ld_stage"], 12 * 16)
            out = claim("prow0")
            for c in range(CT):
                last = turn(out[:, c * NPROW:(c + 1) * NPROW], prow[:, c * P:(c + 1) * P], NPROW)
            full(last, "prow0")
            pe.wait_ge(S["wg_masked"], 1)
            out = claim("wsT")
            for c in range(CT):
                last = turn(out[:, c * P:(c + 1) * P], wsr[:, c, :], P)
            full(last, "wsT")
            for n, rows in enumerate((NS * HC, NS * HP, 4 * HF, 4 * HF)):
                out = claim(("hist", n))
                for c in range(CT):
                    last = turn(out[:, c * rows:(c + 1) * rows], hist[0:rows, n, c * P:(c + 1) * P], rows)
                full(last, ("hist", n))

            def ada(j):
                w = weights("ada", j)
                out = claim(("ada", j))
                await_freed(pe, "cT")
                for k in range(KT):
                    last = mm(out[0:NC_ROWS, :], cT[:, k, :], w[:, k, :], start=(k == 0), stop=(k == KT - 1))
                full(last, ("ada", j))

            for j in range(4):
                ada(j)
            out = claim("modT")
            await_freed(pe, ("ada", 3))
            for k in range(2 * KT):
                last = turn(out[:, k * NC_ROWS:(k + 1) * NC_ROWS], mod[:, k * P:(k + 1) * P], NC_ROWS)
            full(last, "modT")
            pe.wait_ge(S["x_norm"], 3)
            for k in range(KT):
                out = claim(("hT", k))
                for t, (t0, n) in enumerate(TILES):
                    last = turn(out[:, t0:t0 + n], xn[0:n, t, k * P:(k + 1) * P], n)
                full(last, ("hT", k))

            w = weights("win", 1)
            pe.wait_ge(S["h_ready"], KT)
            for t, (t0, n) in enumerate(TILES):
                out = claim(("v", t))
                for k in range(KT):
                    last = mm(out[0:n, :], hT[:, k, t0:t0 + n], w[:, k, :], start=(k == 0), stop=(k == KT - 1))
                full(last, ("v", t))

            def columns(j, names):
                w = weights("win", j)
                for c, name in enumerate(names):
                    out = claim(name)
                    for k in range(KT):
                        last = mm(out[:, 0:TOK], w[:, k, c * P:(c + 1) * P], hT[:, k, :], start=(k == 0), stop=(k == KT - 1))
                    full(last, name)

            def state(name, made_of, src, at, n):
                await_freed(pe, made_of)
                out = claim(name)
                for c in range(CT):
                    last = turn(out[0:n, c * P:(c + 1) * P], src[:, c, at:at + n], P)
                full(last, name)

            for j in (7, 6, 3, 4, 5, 2, 0):
                columns(j, [("z", j, c) for c in range(CT)])
                if j == 6:
                    state("st_conf", ("z", 6, CT - 1), gluP, SEQ, HF + NS)
                if j == 4:
                    state("st_conv", ("z", 4, CT - 1), cgP, SEQ, HC + NS)
                if j == 5:
                    state("st_pool", ("z", 5, CT - 1), zcP, SEQ, HP + NS)
            pe.wait_ge(S["v_ready"], 1)
            pe.wait_ge(S["ws_ready"], 1)
            for c in range(CT):
                out = claim(("sg", c))
                for t in range(2):
                    mm(out[:, t * P:(t + 1) * P], v_sb[:, t, c * P:(c + 1) * P], wsT[:, c, :], start=True, stop=True)
                last = mm(out[:, SEQ:TOK], v_sb[0:NS, 2, c * P:(c + 1) * P], wdiag[:, c, :], start=True, stop=True)
                full(last, ("sg", c))
            pe.wait_ge(S["ld_param"], NPARAM * 16)
            pe.wait_ge(S["pooled_ready"], CT)
            for c in range(CT):
                out = claim(("pw", c))
                full(mm(out[:, 0:TOK], poolw[:, c, :], ybr[:, 2, c, :], start=True, stop=True), ("pw", c))
            for j in range(4, 12):
                ada(j)
                if j % 2:
                    i = (j - 5) // 2
                    await_freed(pe, ("ada", j))
                    if i == 2:
                        pe.wait_ge(S["g2_rows"], 1)
                    for h in range(2):
                        out = claim(("bc", i, h))
                        at = i * D + h * BLK
                        full(mm(out, sel8[:, :], mod[:, at:at + BLK], start=True, stop=True), ("bc", i, h))
            for n, k in enumerate(BR_ORDER):
                if k == 0:
                    pe.wait_ge(S["dconv_ready"], 1)
                    out = claim("cmean")
                    for c in range(CT):
                        last = mm(out[:, 0:TOK], cmean[:, :], dcv[:, c, :], start=(c == 0), stop=(c == CT - 1))
                    full(last, "cmean")
                if k == 3:
                    pe.wait_ge(S["sq_ready"], 1)
                    out = claim("cvar")
                    for c in range(CT):
                        last = mm(out[:, 0:TOK], cmean[:, :], tmpT[:, c, :], start=(c == 0), stop=(c == CT - 1))
                    full(last, "cvar")
                for half in range(2):
                    columns(8 + 2 * k + half, [("zg", k, 4 * half + c) for c in range(CT)])
                w = weights("br", k)
                if k == 2:
                    await_freed(pe, ("pw", CT - 1))
                elif k == 1:
                    await_freed(pe, ("z", 2, CT - 1))
                else:
                    pe.wait_ge(S["ya_ready" if k == 0 else "yd_ready"], CT)
                for d in range(KT):
                    out = claim(("pr", k, d))
                    for c in range(CT):
                        last = mm(out[:, 0:TOK], w[:, c, d * P:(d + 1) * P], ybr[:, k, c, :], start=(c == 0), stop=(c == CT - 1))
                    full(last, ("pr", k, d))
            pe.wait_ge(S["mrg_ready"], KT)
            w_out_sb = [weights("out", j) for j in range(2)]

            def turn_h(t):
                t0, n = TILES[t]
                pe.wait_ge(S["h2_ready"], MIX_ORDER.index(t) + 1)
                for h in range(2):
                    out = claim(("h2T", t, h))
                    for k in range(4 * h, 4 * h + 4):
                        last = turn(out[:, (k % 4) * n:(k % 4 + 1) * n], xn[0:n, t, k:D:KT], n)
                    full(last, ("h2T", t, h))

            for m, t in enumerate(MIX_ORDER):
                t0, n = TILES[t]
                for j in range(2):
                    out = claim(("mix", t, j))
                    for k in range(KT):
                        last = mm(out[0:n, :], mT[:, k, t0:t0 + n], w_out_sb[j][:, k, :], start=(k == 0), stop=(k == KT - 1))
                    full(last, ("mix", t, j))
                if m:
                    turn_h(MIX_ORDER[m - 1])
            turn_h(MIX_ORDER[-1])
            for t in MIX_ORDER:
                await_freed(pe, ("h2T", t, 1))
            out = claim("logit")
            for t, (t0, n) in enumerate(TILES):
                for k in range(KT):
                    last = mm(out[0:n, t * NE:(t + 1) * NE], hT[:, k, t0:t0 + n], rtw[:, k, :], start=(k == 0), stop=(k == KT - 1))
            full(last, "logit")

            pe.wait_ge(S["sh_load"], 48)
            for j in range(2):
                for a, name in enumerate(("shared_gate", "shared_up")):
                    out = claim((name, j))
                    for k in range(KT):
                        last = mm(out[:, 0:TOK], w_gu[1][:, k, a, j:FE:2], hT[:, k, :], start=(k == 0), stop=(k == KT - 1))
                    full(last, (name, j))
            pe.wait_ge(S["sel_ready"], 1)
            out = claim("slot")
            for t in range(3):
                for u in range(t):
                    mm(out[:, t * NE:(t + 1) * NE], ones[:, :], sel[:, u, :], start=(u == 0), stop=False)
                mm(out[:, t * NE:(t + 1) * NE], lower[:, :], sel[:, t, :], start=(t == 0), stop=True)
            for t in range(3):
                last = mm(out[:, 3 * NE:4 * NE], ones[:, :], sel[:, t, :], start=(t == 0), stop=(t == 2))
            full(last, "slot")

            def token_list(i, j):
                e = UNROLL * i + j
                pe.wait_ge(S["oh_ready"], e + 1)
                need(pe, S["lst_ready"], e)
                for t in range(3):
                    rhs = tab[:, t, :, :].rearrange("p e c -> p (e c)")
                    rhs = rhs[:, 2 * e:2 * e + 2] if isinstance(e, int) else rhs[:, bass.ds(2 * e, 2)]
                    last = mm(psum[:, LIST_BANK, 0:2], oh[:, j % 2, t, :], rhs, start=(t == 0), stop=(t == 2))
                last.then_inc(S["list_done"], 1)

            claim("lists")
            token_list(0, 0)
            await_freed(pe, ("shared_up", 1))
            for m, (t, h) in enumerate([(t, h) for t in range(3) for h in range(2)]):
                t0, n = TILES[t]
                out = claim(("sy", t, h))
                for f in range(2):
                    last = mm(out[0:n, :], sh_actT[:, f, t0:t0 + n], w_dn[1][:, f, h * BLK:(h + 1) * BLK], start=(f == 0), stop=(f == 1))
                full(last, ("sy", t, h))
                if m < UNROLL - 1:
                    token_list(0, m + 1)

            for name in JOBS[-6:] + ["slot"]:
                await_freed(pe, name)

            def turn_rows(i, j):
                e = UNROLL * i + j
                pe.wait_ge(gathered[j], 16 * (i + 1))
                need(pe, S["xgt_act"], e)
                need(pe, S["xgt_dve"], e)
                for k in range(KT):
                    last = turn(psum[:, 5 + k // 4, (k % 4) * P:(k % 4 + 1) * P], xg[j][:, k:D:KT], P)
                last.then_inc(S["xt_done"], 1)

            def up(i, j, ks):
                e = UNROLL * i + j
                if ks[0] == 0:
                    pe.wait_ge(gu_full[j], 32 * (i + 1))
                    pe.wait_ge(S["xgt_act"], e + 1)
                    pe.wait_ge(S["xgt_dve"], e + 1)
                    need(pe, S["act_ready"], e - 1)
                for k in ks:
                    last = mm(psum[:, j % 2, :], xgT[:, j % 2, k, :], w_gu[j][:, k], start=(k == 0), stop=(k == KT - 1))
                if ks[-1] == KT - 1:
                    last.then_inc(S["gu_done"], 1)

            def turn_act(i, j):
                e = UNROLL * i + j
                pe.wait_ge(S["act_ready"], e + 1)
                need(pe, S["actT_ready"], e)
                for h in range(2):
                    last = turn(psum[:, 2, h * P:(h + 1) * P], act[:, j % 2, h:FE:2], P)
                last.then_inc(S["tact_done"], 1)

            def down(i, j):
                e = UNROLL * i + j
                pe.wait_ge(S["actT_ready"], e + 1)
                pe.wait_ge(down_full[j], 16 * (i + 1))
                need(pe, S["ys_act"], e)
                need(pe, S["ys_dve"], e)
                for h in range(2):
                    for f in range(2):
                        last = mm(psum[:, 3 + h, :], actT[:, j % 2, f, :], w_dn[j][:, f, h * BLK:(h + 1) * BLK],
                                  start=(f == 0), stop=(f == 1))
                last.then_inc(S["dn_done"], 1)

            def body(i, first=False, last=False):
                for j in range(UNROLL):
                    prev = not (first and j == 0)
                    pi, pj = (i if j else i - 1), (j - 1) % UNROLL
                    up(i, j, range(0, 4))
                    if prev:
                        turn_act(pi, pj)
                    up(i, j, range(4, KT))
                    if not (last and j == UNROLL - 1):
                        turn_rows(i if j < 3 else i + 1, (j + 1) % UNROLL)
                    if prev:
                        down(pi, pj)
                    if not last:
                        token_list(i + 1, j)

            turn_rows(0, 0)
            body(0, first=True)
            with pe.Fori(1, NE // UNROLL - 1) as i:
                body(i)
            body(NE // UNROLL - 1, last=True)
            turn_act(NE // UNROLL - 1, UNROLL - 1)
            down(NE // UNROLL - 1, UNROLL - 1)


            def extra(r, e, n):
                pe.wait_ge(S["x_oh"], n + 1)
                for t in range(3):
                    rhs = tab[:, t, :, :].rearrange("p e c -> p (e c)")[:, bass.ds(2 * e, 2)]
                    last = mm(psum[:, LIST_BANK, 0:2], oh[:, 0, t, :], rhs, start=(t == 0), stop=(t == 2))
                last.then_inc(S["x_list"], 1)
                pe.wait_ge(S["x_gat"], 16 * n + 16)
                for k in range(KT):
                    last = turn(psum[:, 5 + k // 4, (k % 4) * P:(k % 4 + 1) * P], xg[0][:, k:D:KT], P)
                last.then_inc(S["x_xt"], 1)
                pe.wait_ge(S["x_xgt"], n + 1)
                pe.wait_ge(S["x_w"], 48 * n + 48)
                for k in range(KT):
                    last = mm(psum[:, 0, :], xgT[:, 0, k, :], w_gu[0][:, k], start=(k == 0), stop=(k == KT - 1))
                last.then_inc(S["x_gu"], 1)
                pe.wait_ge(S["x_act"], n + 1)
                for h in range(2):
                    last = turn(psum[:, 2, h * P:(h + 1) * P], act[:, 0, h:FE:2], P)
                last.then_inc(S["x_tact"], 1)
                pe.wait_ge(S["x_actT"], n + 1)
                for h in range(2):
                    for f in range(2):
                        last = mm(psum[:, 3 + h, :], actT[:, 0, f, :], w_dn[0][:, f, h * BLK:(h + 1) * BLK], start=(f == 0), stop=(f == 1))
                last.then_inc(S["x_dn"], 1)

            extra_passes(pe, extra)

        @block.scalar
        def _(ac):
            n_chain = [0]

            def link(ins):
                n_chain[0] += 1
                ins.then_inc(S["act_chain"], 1)
                ac.wait_ge(S["act_chain"], n_chain[0])

            def load(dst, src, name):
                ac.dma_start(dst, src).then_inc(S[name], 16)

            F = nc.scalar.activation
            load(crow[0:NS], c_sample, "ld_c")
            load(crow[NS:NC_ROWS], c_prompt, "ld_c")
            load(x_sb[:, 0:2, :], x_prompt[0].rearrange("(t p) d -> p t d", p=P), "ld_x")
            load(x_sb[0:NS, 2, :], x_sample[:, 0, :], "ld_x")
            load(mod[:, 0:2 * D], ada_b[0:1, 0:2 * D].to_broadcast([NC_ROWS, 2 * D]), "ld_mod")
            load(prow[R_CONFW:R_CONFW + 31], conf_w[0], "ld_stage")
            load(prow[R_CONVW:R_CONVW + 3], conv_w[0], "ld_stage")
            for r, p in ((R_CONFB, conf_b), (R_CLNG, conf_ln_g), (R_CLNB, conf_ln_b), (R_PSC, pool_scale)):
                load(prow[r:r + 1], p, "ld_stage")
            load(prow[R_N1G:R_N1G + 2], norm1_g.rearrange("a (r c) -> (a r) c", r=2), "ld_stage")
            load(wsr, sgu_w[0].rearrange("g p q -> p g q"), "ld_stage")
            load(hist[0:NS * HC, 0, :], state_conv[0].rearrange("s h c -> (s h) c"), "ld_stage")
            load(hist[0:NS * HP, 1, :], state_pool[0].rearrange("s h c -> (s h) c"), "ld_stage")
            for a in range(2):
                load(hist[0:4 * HF, 2 + a, :], state_conf[0, 4 * a:4 * a + 4].rearrange("s h c -> (s h) c"), "ld_stage")
            load(lnv[:, 0, :], sgu_ln_g.to_broadcast([P, BR]), "ld_param")
            load(lnv[:, 1, :], sgu_ln_b.to_broadcast([P, BR]), "ld_param")
            load(sgub, sgu_b[0:1].rearrange("a g q -> a (g q)").to_broadcast([P, BR]).rearrange("p (g q) -> p g q", g=CT), "ld_param")
            with nc.allow_non_contiguous_dma(reason="one weight per group"):
                load(w00[:], sgu_w[0, :, 0, 0:1].rearrange("g a -> a g").to_broadcast([NS, CT]), "ld_param")
            load(poolw, pool_w[0].rearrange("g c d -> c g d"), "ld_param")
            load(rtw[:], router_w[0].rearrange("(p k) e -> p k e", k=KT), "ld_param")
            load(rtb[:], router_bias.to_broadcast([P, NE]), "ld_param")
            load(bc[0:NC_ROWS, 2, :], norm2_g.to_broadcast([NC_ROWS, D]), "ld_param")

            ac.wait_ge(S["ld_c"], 32)
            F(crow[:, :], crow[:, :], ACT.Silu).then_inc(S["c_silu"], 1)

            def row_norm(src_sem, value, done):
                ac.wait_ge(src_sem, value)
                for t, (t0, n) in enumerate(TILES):
                    last = F(xn[0:n, t, :], x_sb[0:n, t, :], ACT.Square, accum_out=st[0:n, t, 0:1])
                link(last)
                F(st[:, :, 1], st[:, :, 0], ACT.Sqrt, scale=1.0 / D, bias=epsc[:, 0:1]).then_inc(done, 1)

            ac.wait_ge(S["consts"], 2)
            row_norm(S["ld_x"], 32, S["x_sq"])
            for t, (t0, n) in enumerate(TILES):
                b = await_full(ac, ("v", t))
                free(F(v_sb[0:n, t, :], b[0:n, :], ACT.Gelu), ("v", t))
            ac.wait_ge(S["v_mean"], 1)
            F(st[:, :, 6], st[:, :, 5], ACT.Sqrt, bias=epsc[:, 0:1]).then_inc(S["v_std"], 1)

            def z_out(j, func, dst, reader):
                for c in range(CT):
                    b = await_full(ac, ("z", j, c))
                    if reader:
                        await_freed(ac, ("z", reader, c))
                    free(F(dst(c), b[:, 0:TOK], func), ("z", j, c))

            def state_rows(name, rows, n):
                b = await_full(ac, name)
                free(F(rows[0:n, :], b[0:n, :], ACT.Copy), name)

            z_out(7, ACT.Sigmoid, lambda c: tmpT[:, c, :], None)
            state_rows("st_conf", st_conf, HF + NS)
            z_out(3, ACT.Copy, lambda c: tmpT[:, c, :], 6)
            state_rows("st_conv", st_conv, HC + NS)
            for c in range(CT):
                b = await_full(ac, ("z", 5, c))
                free(F(zcP[:, c, HP:], b[:, 0:TOK], ACT.Copy), ("z", 5, c))
            state_rows("st_pool", st_pool, HP + NS)
            z_out(0, ACT.Gelu, lambda c: tmpT[:, c, :], 4)

            def spread_out(i):
                for h in range(2):
                    b = await_full(ac, ("bc", i, h))
                    if i in (1, 3):
                        ac.wait_ge(S["st_stored"], 6 * 16)
                    free(F(bc[:, i, h * BLK:(h + 1) * BLK], b[:, :], ACT.Copy), ("bc", i, h))

            for i in range(4):
                spread_out(i)
            for n, k in enumerate(BR_ORDER):
                if k == 0:
                    await_freed(ac, "cmean")
                    F(tmpT[:, :, :], dcv[:, :, :], ACT.Square).then_inc(S["sq_ready"], 1)
                if k == 3:
                    b = await_full(ac, "cvar")
                    free(F(stat[:, 0, :], b[:, 0:TOK], ACT.Sqrt, bias=epsc[:, 0:1]), "cvar")
                    ac.wait_ge(S["dn_ready"], 1)
                    for c in range(CT):
                        F(ybr[:, 3, c, :], dcv[:, c, :], ACT.Silu, scale=col(c, R_CLNG), bias=col(c, R_CLNB)).then_inc(S["yd_ready"], 1)
                for d in range(KT):
                    b = await_full(ac, ("zg", k, d))
                    if n:
                        await_freed(ac, ("pr", BR_ORDER[n - 1], d))
                    free(F(sg[:, d, :], b[:, 0:TOK], ACT.Sigmoid), ("zg", k, d))
            def h2_out(t):
                t0, n = TILES[t]
                for h in range(2):
                    b = await_full(ac, ("h2T", t, h))
                    free(F(hT[:, 4 * h:4 * h + 4, t0:t0 + n], b[:, 0:4 * n].rearrange("p (k c) -> p k c", k=4), ACT.Copy), ("h2T", t, h))

            for m, t in enumerate(MIX_ORDER):
                t0, n = TILES[t]
                ac.wait_ge(S["x2_ready"], 2 * m + 2)
                link(F(xn[0:n, t, :], x_sb[0:n, t, :], ACT.Square, accum_out=st[0:n, t, 0:1]))
                F(st[0:n, t, 1:2], st[0:n, t, 0:1], ACT.Sqrt, scale=1.0 / D, bias=epsc[0:n, 0:1]).then_inc(S["x2_sq"], 1)
                if m:
                    h2_out(MIX_ORDER[m - 1])
            h2_out(MIX_ORDER[-1])
            b = await_full(ac, "logit")
            for t, (t0, n) in enumerate(TILES):
                last = F(sc[0:n, t, :], b[0:n, t * NE:(t + 1) * NE], ACT.Sigmoid)
            free(last, "logit")

            for j in range(2):
                b = await_full(ac, ("shared_gate", j))
                free(F(sh_silu[:, j, :], b[:, 0:TOK], ACT.Silu), ("shared_gate", j))
            for t, (t0, n) in enumerate(TILES):
                for h in range(2):
                    b = await_full(ac, ("sy", t, h))
                    free(F(shared[0:n, t, h * BLK:(h + 1) * BLK], b[0:n, :], ACT.Copy), ("sy", t, h))

            def rows_out(i, j):
                e = UNROLL * i + j
                ac.wait_ge(S["xt_done"], e + 1)
                need(ac, S["gu_done"], e - 1)
                F(xgT[:, j % 2, 0:4, :], psum[:, 5, :].rearrange("p (k c) -> p k c", k=4), ACT.Copy).then_inc(S["xgt_act"], 1)

            def act_turned(i, j):
                e = UNROLL * i + j
                ac.wait_ge(S["tact_done"], e + 1)
                need(ac, S["dn_done"], e - 1)
                F(actT[:, j % 2], psum[:, 2, 0:2 * P].rearrange("p (h c) -> p h c", h=2), ACT.Copy).then_inc(S["actT_ready"], 1)

            def y_out(i, j):
                e = UNROLL * i + j
                ac.wait_ge(S["dn_done"], e + 1)
                need(ac, scattered[j % 2], 16 * (2 * i + j // 2))
                F(y_rows[:, j % 2, 0:BLK], psum[:, 3, :], ACT.Copy).then_inc(S["ys_act"], 1)

            def body(i, first=False, last=False):
                for j in range(UNROLL):
                    prev = not (first and j == 0)
                    pi, pj = (i if j else i - 1), (j - 1) % UNROLL
                    e = UNROLL * i + j
                    if prev:
                        act_turned(pi, pj)
                    ac.wait_ge(S["gu_done"], e + 1)
                    need(ac, S["act_ready"], e - 1)
                    F(silu[:, j % 2, :], psum[:, j % 2, 0:FE], ACT.Silu).then_inc(S["silu_ready"], 1)
                    if not (last and j == UNROLL - 1):
                        rows_out(i if j < 3 else i + 1, (j + 1) % UNROLL)
                    if prev:
                        y_out(pi, pj)

            rows_out(0, 0)
            body(0, first=True)
            with ac.Fori(1, NE // UNROLL - 1) as i:
                body(i)
            body(NE // UNROLL - 1, last=True)
            act_turned(NE // UNROLL - 1, UNROLL - 1)
            y_out(NE // UNROLL - 1, UNROLL - 1)

            def extra(r, e, n):
                ac.wait_ge(S["x_gu"], n + 1)
                F(silu[:, 0, :], psum[:, 0, 0:FE], ACT.Silu).then_inc(S["x_silu"], 1)
                ac.wait_ge(S["x_tact"], n + 1)
                F(actT[:, 0], psum[:, 2, 0:2 * P].rearrange("p (h c) -> p h c", h=2), ACT.Copy).then_inc(S["x_actT"], 1)

            extra_passes(ac, extra)
            for t, (t0, n) in enumerate(TILES):
                ac.wait_ge(S["fin_red"], t + 1)
                link(F(xn[0:n, t, :], x_sb[0:n, t, :], ACT.Square, accum_out=st[0:n, t, 0:1]))
                F(st[0:n, t, 1:2], st[0:n, t, 0:1], ACT.Sqrt, scale=1.0 / D, bias=epsc[0:n, 0:1]).then_inc(S["fin_sq"], 1)

        @block.vector
        def _(ve):
            n_chain = [0]
            V = nc.vector

            def mark(ins):
                n_chain[0] += 1
                ins.then_inc(S["dve_chain"], 1)
                return n_chain[0]

            def link(ins):
                ve.wait_ge(S["dve_chain"], mark(ins))

            ve.wait_ge(S["consts"], 2)
            V.tensor_copy(tokid[:], tokid_i[:])
            link(V.tensor_copy(iota_f[:], iota_i[:]))
            link(V.tensor_scalar(rc[:], iota_f[:, 0:16], 1.0, None, ALU.add))
            V.reciprocal(rc[:], rc[:])
            link(V.tensor_scalar(tokid[:], tokid[:], -BIG, None, ALU.add))
            V.tensor_copy(tab[:, :, :, 0], tokid[:].unsqueeze(2).to_broadcast([P, 3, NE]))
            ve.wait_ge(S["x_sq"], 1)
            link(V.reciprocal(st[:, :, 2], st[:, :, 1]))
            for t, (t0, n) in enumerate(TILES):
                V.tensor_scalar(xn[0:n, t, :], x_sb[0:n, t, :], st[0:n, t, 2:3], None, ALU.mult).then_inc(S["x_norm"], 1)
            b = await_full(ve, "cT")
            free(V.tensor_copy(cT[:].rearrange("p k r -> p (k r)"), b[:, 0:KT * NC_ROWS]), "cT")
            b = await_full(ve, "prow0")
            free(V.tensor_copy(prm[:].rearrange("p c r -> p (c r)"), b[:, 0:CT * NPROW]), "prow0")
            b = await_full(ve, "wsT")
            free(V.tensor_copy(wsT.rearrange("p g q -> p (g q)"), b[:, :]), "wsT")
            ve.wait_ge(S["ld_param"], NPARAM * 16)
            for c in range(CT):
                last = V.tensor_scalar(wdiag[:, c, :], ident[0:NS, 0:NS], w00[:, c:c + 1], None, ALU.mult)
            last.then_inc(S["ws_ready"], 1)
            for n, (dst, rows) in enumerate(((convH.rearrange("p c s h -> p c (s h)"), NS * HC),
                                             (poolH.rearrange("p c s h -> p c (s h)"), NS * HP),
                                             (confH[:, :, 0:4, :].rearrange("p c s h -> p c (s h)"), 4 * HF),
                                             (confH[:, :, 4:8, :].rearrange("p c s h -> p c (s h)"), 4 * HF))):
                b = await_full(ve, ("hist", n))
                free(V.tensor_copy(dst, b[:, 0:CT * rows].rearrange("p (c r) -> p c r", c=CT)), ("hist", n))

            def ada_out(j):
                b = await_full(ve, ("ada", j))
                at = (j % 4 if j < 4 else j - 4) * BLK
                ins = V.tensor_tensor(mod[:, at:at + BLK], b[0:NC_ROWS, :], mod[:, at:at + BLK], ALU.add)
                return ins

            ve.wait_ge(S["ld_mod"], 16)
            for j in range(4):
                free(ada_out(j), ("ada", j))
            b = await_full(ve, "modT")
            V.tensor_copy(S1[:].rearrange("p k r -> p (k r)"), b[:, 0:KT * NC_ROWS])
            free(V.tensor_scalar(G1[:].rearrange("p k r -> p (k r)"), b[:, KT * NC_ROWS:2 * KT * NC_ROWS], 1.0, None, ALU.add), "modT")
            await_freed(ve, "modT")
            await_freed(ve, "prow0")
            link(V.tensor_tensor(G1[:].rearrange("p (a c) r -> p a c r", a=2), G1[:].rearrange("p (a c) r -> p a c r", a=2),
                                 prm[:, :, R_N1G:R_N1G + 2].rearrange("p c a -> p a c").unsqueeze(3).to_broadcast([P, 2, CT, NC_ROWS]),
                                 ALU.mult))
            for k in range(KT):
                b = await_full(ve, ("hT", k))
                V.tensor_scalar(hT[:, k, 0:SEQ], b[:, 0:SEQ], G1[:, k, NS:NC_ROWS], S1[:, k, NS:NC_ROWS], ALU.mult, ALU.add)
                free(V.tensor_tensor(hT[:, k, SEQ:TOK], b[:, SEQ:TOK], G1[:, k, 0:NS], ALU.mult), ("hT", k))
                await_freed(ve, ("hT", k))
                V.tensor_tensor(hT[:, k, SEQ:TOK], hT[:, k, SEQ:TOK], S1[:, k, 0:NS], ALU.add).then_inc(S["h_ready"], 1)
            for t, (t0, n) in enumerate(TILES):
                await_freed(ve, ("v", t))
                link(V.bn_stats(bns[0:n, t, 0:6], v_sb[0:n, t, :]))
                last = V.bn_aggr(st[0:n, t, 4:6], bns[0:n, t, 0:6])
            last.then_inc(S["v_mean"], 1)
            ve.wait_ge(S["v_std"], 1)
            link(V.reciprocal(st[:, :, 7], st[:, :, 6]))
            for t, (t0, n) in enumerate(TILES):
                link(V.tensor_scalar(v_sb[0:n, t, :], v_sb[0:n, t, :], st[0:n, t, 4:5], st[0:n, t, 7:8], ALU.subtract, ALU.mult))
                link(V.tensor_tensor(v_sb[0:n, t, :], v_sb[0:n, t, :], lnv[0:n, 0, :], ALU.mult))
                last = V.tensor_tensor(v_sb[0:n, t, :], v_sb[0:n, t, :], lnv[0:n, 1, :], ALU.add)
            last.then_inc(S["v_ready"], 1)

            for c in range(CT):
                b = await_full(ve, ("z", 6, c))
                await_freed(ve, ("z", 7, c))
                free(V.tensor_tensor(gluP[:, c, HF:], b[:, 0:TOK], tmpT[:, c, :], ALU.mult), ("z", 6, c))
            for c in range(CT):
                b = await_full(ve, ("z", 4, c))
                await_freed(ve, ("z", 3, c))
                free(V.tensor_tensor(cgP[:, c, HC:], b[:, 0:TOK], tmpT[:, c, :], ALU.mult), ("z", 4, c))

            await_freed(ve, ("z", 4, CT - 1))
            taps = [0] * CT
            for h in range(HC + 1):
                for c in range(CT):
                    w = col(c, R_CONVW + h)
                    past = convH[:, c, :, h] if h < HC else cgP[:, c, HC + SEQ:]
                    if h == 0:
                        V.tensor_scalar(ybr[:, 1, c, 0:SEQ], cgP[:, c, 0:SEQ], w, None, ALU.mult)
                        taps[c] = mark(V.tensor_scalar(ybr[:, 1, c, SEQ:], past, w, None, ALU.mult))
                    else:
                        ve.wait_ge(S["dve_chain"], taps[c])
                        V.scalar_tensor_tensor(ybr[:, 1, c, 0:SEQ], cgP[:, c, h:h + SEQ], w, ybr[:, 1, c, 0:SEQ], ALU.mult, ALU.add)
                        taps[c] = mark(V.scalar_tensor_tensor(ybr[:, 1, c, SEQ:], past, w, ybr[:, 1, c, SEQ:], ALU.mult, ALU.add))

            for c in range(CT):
                win = 2 << c
                await_freed(ve, ("z", 5, c))
                src = zcP[:, c, :]
                for r in range(c + 1):
                    d = 1 << r
                    dst = sums[:, r % 2, :]
                    link(V.tensor_tensor(dst[:, 2 * d - 1:HP + SEQ], src[:, 2 * d - 1:HP + SEQ], src[:, d - 1:HP + SEQ - d], ALU.add))
                    src = dst
                own = zcP[:, c, HP:HP + SEQ]
                V.scalar_tensor_tensor(ybr[:, 2, c, win - 1:SEQ], src[:, HP + win - 1:HP + SEQ], 1.0 / win, own[:, win - 1:], ALU.mult, ALU.subtract)
                link(V.tensor_tensor(src[:, HP:HP + win - 1], src[:, HP:HP + win - 1], rc[:, 0:win - 1], ALU.mult))
                V.tensor_tensor(ybr[:, 2, c, 0:win - 1], src[:, HP:HP + win - 1], own[:, 0:win - 1], ALU.subtract)
                new = zcP[:, c, HP + SEQ:]
                part = prod[:, :, 0]
                if win > 2:
                    link(V.tensor_reduce(part, poolH[:, c, :, HP - win + 1:HP], AX.X, ALU.add))
                else:
                    link(V.tensor_copy(part, poolH[:, c, :, HP - 1]))
                link(V.tensor_tensor(part, part, new, ALU.add))
                V.scalar_tensor_tensor(ybr[:, 2, c, SEQ:], part, 1.0 / win, new, ALU.mult, ALU.subtract).then_inc(S["pooled_ready"], 1)

            for c in range(CT):
                b = await_full(ve, ("z", 2, c))
                free(V.tensor_tensor(ybr[:, 1, c, :], b[:, 0:TOK], ybr[:, 1, c, :], ALU.mult), ("z", 2, c))
            for c in range(CT):
                b = await_full(ve, ("sg", c))
                V.tensor_tensor(ybr[:, 0, c, 0:SEQ].rearrange("p (t q) -> p t q", t=2), b[:, 0:SEQ].rearrange("p (t q) -> p t q", t=2),
                                sgub[:, c:c + 1, :].to_broadcast([P, 2, P]), ALU.add)
                free(V.tensor_scalar(ybr[:, 0, c, SEQ:], b[:, SEQ:TOK], sgub[:, c, 0:1], None, ALU.add), ("sg", c))
                await_freed(ve, ("sg", c))
                await_freed(ve, ("z", 0, c))
                V.tensor_tensor(ybr[:, 0, c, :], ybr[:, 0, c, :], tmpT[:, c, :], ALU.mult).then_inc(S["ya_ready"], 1)
            for c in range(CT):
                b = await_full(ve, ("pw", c))
                free(V.tensor_scalar(ybr[:, 2, c, :], b[:, 0:TOK], col(c, R_PSC), None, ALU.mult), ("pw", c))

            taps = [0] * CT

            def conf_taps(h0, h1):
                for h in range(h0, h1):
                    for c in range(CT):
                        w = col(c, R_CONFW + h)
                        if h == 0:
                            taps[c] = mark(V.tensor_scalar(dcv[:, c, 0:SEQ], gluP[:, c, 0:SEQ], w, col(c, R_CONFB), ALU.mult, ALU.add))
                        else:
                            ve.wait_ge(S["dve_chain"], taps[c])
                            taps[c] = mark(V.scalar_tensor_tensor(dcv[:, c, 0:SEQ], gluP[:, c, h:h + SEQ], w, dcv[:, c, 0:SEQ], ALU.mult, ALU.add))

            for j in range(4, 12):
                if j == 4:
                    ve.wait_ge(S["ld_mod2"], 16)
                free(ada_out(j), ("ada", j))
                if j == 9:
                    await_freed(ve, ("ada", 9))
                    V.scalar_tensor_tensor(mod[:, 2 * D:3 * D], mod[:, 2 * D:3 * D], 1.0, bc[0:NC_ROWS, 2, :], ALU.add, ALU.mult).then_inc(S["g2_rows"], 1)
                conf_taps(4 * (j - 4), min(4 * (j - 3), HF + 1))
            for c in range(CT):
                w = prm[:, c, R_CONFW:R_CONFW + HF].unsqueeze(1).to_broadcast([P, NS, HF])
                link(V.tensor_tensor(prod, confH[:, c, :, :], w, ALU.mult))
                link(V.tensor_reduce(dcv[:, c, SEQ:], prod, AX.X, ALU.add))
                link(V.scalar_tensor_tensor(dcv[:, c, SEQ:], gluP[:, c, HF + SEQ:], col(c, R_CONFW + HF), dcv[:, c, SEQ:], ALU.mult, ALU.add))
                last = V.tensor_scalar(dcv[:, c, SEQ:], dcv[:, c, SEQ:], col(c, R_CONFB), None, ALU.add)
            last.then_inc(S["dconv_ready"], 1)

            for n, k in enumerate(BR_ORDER):
                if k == 0:
                    b = await_full(ve, "cmean")
                    ve.wait_ge(S["dconv_ready"], 1)
                    free(V.tensor_tensor(dcv[:, :, :], dcv[:, :, :], b[:, 0:TOK].unsqueeze(1).to_broadcast([P, CT, TOK]), ALU.subtract), "cmean")
                if k == 3:
                    await_freed(ve, "cvar")
                    link(V.reciprocal(stat[:, 1, :], stat[:, 0, :]))
                    V.tensor_tensor(dcv[:, :, :], dcv[:, :, :], stat[:, 1:2, :].to_broadcast([P, CT, TOK]), ALU.mult).then_inc(S["dn_ready"], 1)
                for d in range(KT):
                    b = await_full(ve, ("pr", k, d))
                    await_freed(ve, ("zg", k, d))
                    if n == 0:
                        free(V.tensor_tensor(mT[:, d, :], b[:, 0:TOK], sg[:, d, :], ALU.mult), ("pr", k, d))
                    else:
                        free(V.tensor_tensor(sg[:, d, :], b[:, 0:TOK], sg[:, d, :], ALU.mult), ("pr", k, d))
                        await_freed(ve, ("pr", k, d))
                        ins = V.tensor_tensor(mT[:, d, :], mT[:, d, :], sg[:, d, :], ALU.add)
                        if n == 3:
                            ins.then_inc(S["mrg_ready"], 1)
                        else:
                            ins.then_inc(S["sg_used"], 1)
                if 0 < n < 3:
                    ve.wait_ge(S["sg_used"], n * KT)

            def rows_of(i, t, n, a, b):
                return mod[0:n, i * D + a:i * D + b] if t == 2 else bc[0:n, i, a:b]

            await_freed(ve, ("bc", 0, 1))
            await_freed(ve, ("bc", 2, 1))
            for m, t in enumerate(MIX_ORDER):
                t0, n = TILES[t]
                for j in range(2):
                    b = await_full(ve, ("mix", t, j))
                    a = slice(j * BLK, (j + 1) * BLK)
                    free(V.tensor_tensor(xn[0:n, t, a], b[0:n, :], rows_of(0, t, n, a.start, a.stop), ALU.mult), ("mix", t, j))
                    await_freed(ve, ("mix", t, j))
                    V.tensor_tensor(x_sb[0:n, t, a], x_sb[0:n, t, a], xn[0:n, t, a], ALU.add).then_inc(S["x2_ready"], 1)
                ve.wait_ge(S["x2_sq"], m + 1)
                link(V.reciprocal(st[0:n, t, 2:3], st[0:n, t, 1:2]))
                link(V.scalar_tensor_tensor(xn[0:n, t, :], x_sb[0:n, t, :], st[0:n, t, 2:3], rows_of(2, t, n, 0, D), ALU.mult, ALU.mult))
                V.tensor_tensor(xn[0:n, t, :], xn[0:n, t, :], rows_of(1, t, n, 0, D), ALU.add).then_inc(S["h2_ready"], 1)

            await_freed(ve, "logit")
            link(V.tensor_tensor(bsd[:], sc[:], rtb[:].unsqueeze(1).to_broadcast([P, 3, NE]), ALU.add))
            for t in range(3):
                for q in range(NG):
                    last = V.max(gm[:, t, q, :], bsd[:, t, q * 8:(q + 1) * 8])
            link(last)
            link(V.tensor_tensor(gs[:], gm[:, :, :, 0], gm[:, :, :, 1], ALU.add))
            for t in range(3):
                mine = gs[:, t, :].unsqueeze(2).to_broadcast([P, NG, NG])
                other = gs[:, t, :].unsqueeze(1).to_broadcast([P, NG, NG])
                V.tensor_tensor(cmp_[:, t], other, mine, ALU.is_gt)
                last = V.tensor_tensor(cmp2[:, t], other, mine, ALU.is_equal)
            link(last)
            link(V.tensor_tensor(cmp2[:], cmp2[:], trig[:].unsqueeze(1).to_broadcast([P, 3, NG, NG]), ALU.mult))
            link(V.tensor_tensor(cmp_[:], cmp_[:], cmp2[:], ALU.add))
            link(V.tensor_reduce(gs[:], cmp_[:], AX.X, ALU.add))
            link(V.tensor_scalar(gs[:], gs[:], float(TOPG), None, ALU.is_lt))
            link(V.tensor_scalar(gm[:, :, :, 0], gs[:], -1.0, 1e30, ALU.add, ALU.mult))
            sel_g = gs[:].unsqueeze(3).to_broadcast([P, 3, NG, 8])
            pen_g = gm[:, :, :, 0:1].to_broadcast([P, 3, NG, 8])
            link(V.tensor_tensor(msk[:].rearrange("p t (g e) -> p t g e", g=NG), bsd[:].rearrange("p t (g e) -> p t g e", g=NG), sel_g, ALU.mult))
            link(V.tensor_tensor(msk[:].rearrange("p t (g e) -> p t g e", g=NG), msk[:].rearrange("p t (g e) -> p t g e", g=NG), pen_g, ALU.add))
            for t in range(3):
                last = V.max(gm[:, t, 0, :], msk[:, t, :])
            link(last)
            for t in range(3):
                last = V.match_replace(sel[:, t, :], gm[:, t, 0, :], msk[:, t, :], -3e30)
            link(last)
            link(V.tensor_tensor(sel[:], sel[:], msk[:], ALU.not_equal))
            V.tensor_tensor(sel[:], sel[:], valid[:].unsqueeze(2).to_broadcast([P, 3, NE]), ALU.mult).then_inc(S["sel_ready"], 1)
            ve.wait_ge(S["sel_ready"], 1)

            link(V.tensor_tensor(msk[:], sc[:], sel[:], ALU.mult))
            link(V.tensor_reduce(st[:, :, 3], msk[:], AX.X, ALU.add))
            link(V.tensor_scalar(st[:, :, 3], st[:, :, 3], 1e-38, None, ALU.max))
            link(V.reciprocal(st[:, :, 3], st[:, :, 3]))
            for t in range(3):
                V.tensor_scalar(tab[:, t, :, 1], msk[:, t, :], st[:, t, 3:4], ROUTED_SCALE, ALU.mult, ALU.mult)
            b = await_full(ve, "slot")
            link(V.tensor_scalar(posm[:], sel[:], -1.0, 1e6, ALU.add, ALU.mult))
            V.tensor_reduce(cnt_f[:], b[:, 3 * NE:4 * NE], AX.X, ALU.max)
            free(V.tensor_tensor(posm[:].rearrange("p t e -> p (t e)"), b[:, 0:3 * NE], posm[:].rearrange("p t e -> p (t e)"), ALU.add), "slot")
            await_freed(ve, "slot")
            V.tensor_copy(cnt_i[:], cnt_f[:]).then_inc(S["cnt_ready"], 1)

            def one_hot(i, j):
                e = UNROLL * i + j
                need(ve, S["list_done"], e - 1)
                for t in range(3):
                    p = posm[:, t, e:e + 1] if isinstance(e, int) else posm[:, t, bass.ds(e, 1)]
                    last = V.tensor_scalar(oh[:, j % 2, t, :], iota_f[:], p, None, ALU.is_equal)
                last.then_inc(S["oh_ready"], 1)

            def list_out(i, j):
                e = UNROLL * i + j
                ve.wait_ge(S["list_done"], e + 1)
                need(ve, S["scatter_row_ready"], e - 3)
                need(ve, S["act_ready"], e - 3)
                V.tensor_scalar(idx[:, j, :], psum[:, LIST_BANK, 0:1], BIG, None, ALU.add)
                V.tensor_copy(gcol[:, j, :], psum[:, LIST_BANK, 1:2]).then_inc(S["lst_ready"], 1)

            def keep_scatter_row(i, j):
                e = UNROLL * i + j
                ve.wait_ge(S["lst_ready"], e + 1)
                need(ve, scattered[j % 2], 16 * (2 * i + j // 2 - 1))
                V.tensor_copy(scatter_row[:, j, :], idx[:, j, :]).then_inc(S["scatter_row_ready"], 1)

            def rows_out(i, j):
                e = UNROLL * i + j
                ve.wait_ge(S["xt_done"], e + 1)
                need(ve, S["gu_done"], e - 1)
                V.tensor_copy(xgT[:, j % 2, 4:8, :], psum[:, 6, :].rearrange("p (k c) -> p k c", k=4)).then_inc(S["xgt_dve"], 1)

            def gated(i, j):
                e = UNROLL * i + j
                ve.wait_ge(S["silu_ready"], e + 1)
                need(ve, S["tact_done"], e - 1)
                V.scalar_tensor_tensor(act[:, j % 2, :], psum[:, j % 2, FE:2 * FE], gcol[:, j, :], silu[:, j % 2, :],
                                       ALU.mult, ALU.mult).then_inc(S["act_ready"], 1)

            def y_out(i, j):
                e = UNROLL * i + j
                ve.wait_ge(S["dn_done"], e + 1)
                need(ve, scattered[j % 2], 16 * (2 * i + j // 2))
                V.tensor_copy(y_rows[:, j % 2, BLK:2 * BLK], psum[:, 4, :]).then_inc(S["ys_dve"], 1)

            def body(i, first=False, last=False):
                for j in range(UNROLL):
                    prev = not (first and j == 0)
                    pi, pj = (i if j else i - 1), (j - 1) % UNROLL
                    if not last:
                        one_hot(i + 1, j)
                    keep_scatter_row(i, j)
                    gated(i, j)
                    if not (last and j == UNROLL - 1):
                        rows_out(i if j < 3 else i + 1, (j + 1) % UNROLL)
                    if prev:
                        y_out(pi, pj)
                    if not last:
                        list_out(i + 1, j)
                    if first and j < 3:
                        t, n = j, TILES[j][1]
                        await_freed(ve, ("sy", t, 1))
                        await_freed(ve, ("bc", 3, 1))
                        link(V.tensor_tensor(shared[0:n, t, :], shared[0:n, t, :], rows_of(3, t, n, 0, D), ALU.mult))
                        V.tensor_tensor(x_sb[0:n, t, :], x_sb[0:n, t, :], shared[0:n, t, :], ALU.add)

            one_hot(0, 0)
            for j in range(2):
                b = await_full(ve, ("shared_up", j))
                await_freed(ve, ("shared_gate", j))
                free(V.tensor_tensor(sh_actT[:, j, :], b[:, 0:TOK], sh_silu[:, j, :], ALU.mult), ("shared_up", j))
            one_hot(0, 1)
            for j in range(UNROLL):
                list_out(0, j)
                if j < 2:
                    one_hot(0, j + 2)
            rows_out(0, 0)
            body(0, first=True)
            with ve.Fori(1, NE // UNROLL - 1) as i:
                body(i)
            body(NE // UNROLL - 1, last=True)
            y_out(NE // UNROLL - 1, UNROLL - 1)

            def extra(r, e, n):
                for t in range(3):
                    last = V.tensor_scalar(oh[:, 0, t, :], iota_f[:], posm[:, t, bass.ds(e, 1)], float(-CAP * r), ALU.subtract, ALU.is_equal)
                last.then_inc(S["x_oh"], 1)
                ve.wait_ge(S["x_list"], n + 1)
                V.tensor_scalar(idx[:, 0, :], psum[:, LIST_BANK, 0:1], BIG, None, ALU.add)
                V.tensor_copy(gcol[:, 0, :], psum[:, LIST_BANK, 1:2]).then_inc(S["x_idx"], 1)
                ve.wait_ge(S["x_xt"], n + 1)
                V.tensor_copy(xgT[:, 0, :, :], psum[:, 5:7, :].rearrange("p b (k c) -> p (b k) c", k=4)).then_inc(S["x_xgt"], 1)
                ve.wait_ge(S["x_silu"], n + 1)
                V.scalar_tensor_tensor(act[:, 0, :], psum[:, 0, FE:2 * FE], gcol[:, 0, :], silu[:, 0, :], ALU.mult, ALU.mult).then_inc(S["x_act"], 1)
                ve.wait_ge(S["x_dn"], n + 1)
                V.tensor_copy(y_rows[:, 0, :].rearrange("p (b n) -> p b n", b=2), psum[:, 3:5, :]).then_inc(S["x_y"], 1)
                ve.wait_ge(S["x_sc"], 16 * n + 16)

            extra_passes(ve, extra)
            for t, (t0, n) in enumerate(TILES):
                if t == 0:
                    ve.wait_ge(fin_ld[t], 2 * 16)
                    link(V.tensor_tensor(fin_y[0:n, t, 0], fin_y[0:n, t, 0], fin_y[0:n, t, 1], ALU.add))
                else:
                    ve.wait_ge(S["fin_sum"], t)
                link(V.tensor_tensor(fin_y[0:n, t, 0], fin_y[0:n, t, 0], rows_of(3, t, n, 0, D), ALU.mult))
                V.tensor_tensor(x_sb[0:n, t, :], x_sb[0:n, t, :], fin_y[0:n, t, 0], ALU.add).then_inc(S["fin_red"], 1)
            ve.wait_ge(S["ld_fin"], 16)
            for t, (t0, n) in enumerate(TILES):
                ve.wait_ge(S["fin_sq"], t + 1)
                link(V.reciprocal(st[0:n, t, 2:3], st[0:n, t, 1:2]))
                V.scalar_tensor_tensor(x_sb[0:n, t, :], x_sb[0:n, t, :], st[0:n, t, 2:3], fing[0:n, :], ALU.mult, ALU.mult).then_inc(S["fin_ready"], 1)


_INS = ["x_prompt", "x_sample", "state_conv", "state_pool", "state_conf", "c_prompt", "c_sample",
        "ada_w", "ada_b", "norm1_g", "norm2_g", "w_in", "sgu_ln_g", "sgu_ln_b", "sgu_w", "sgu_b",
        "conv_w", "pool_w", "pool_scale", "conf_w", "conf_b", "conf_ln_g", "conf_ln_b",
        "w_branch", "w_out", "router_w", "router_bias", "e_gate", "e_up", "e_down",
        "s_gate", "s_up", "s_down", "final_g"]
_OUTS = [(1, SEQ, D), (NS, 1, D), (1, 1, HC, BR), (1, 1, HP, BR), (1, 1, HF, BR),
         (1, NS, HC, BR), (1, NS, HP, BR), (1, NS, HF, BR), (1, NS, 1, BR)]


def kernel(**inputs):
    import concourse.bacc as _bacc
    from concourse.bass_utils import run_bass_kernel_spmd as _run

    nc = _bacc.Bacc("TRN2", target_bir_lowering=False, num_devices=1)
    arrays, args = {}, []
    for name in _INS:
        a = np.ascontiguousarray(inputs[name])
        arrays[f"in_{name}"] = a
        args.append(nc.dram_tensor(f"in_{name}", a.shape, F32, kind="ExternalInput").ap())
    for i, shape in enumerate(_OUTS):
        args.append(nc.dram_tensor(f"out_{i}", shape, F32, kind="ExternalOutput").ap())
    args.append(nc.dram_tensor("h_table", (TOK, D), F32, kind="Internal").ap())
    args.append(nc.dram_tensor("y_even", (TOK, D), F32, kind="Internal").ap())
    args.append(nc.dram_tensor("y_odd", (TOK, D), F32, kind="Internal").ap())
    bass_decoder_step(nc, *args)
    r = _run(nc, [arrays], core_ids=[0])
    return tuple(r.results[0][f"out_{i}"] for i in range(len(_OUTS)))
```

```python
from contextlib import ExitStack

import numpy as np

import concourse.bass as bass
from concourse import mybir

F32 = mybir.dt.float32
F32R = mybir.dt.float32r
I32 = mybir.dt.int32
ALU = mybir.AluOpType
ACT = mybir.ActivationFunctionType
AX = mybir.AxisListType

P = 128
D = 1024
KT = D // P
BR = D // 2
CT = BR // P
SEQ = 256
NS = 8
TOK = SEQ + NS
TILES = [(0, P), (P, P), (2 * P, NS)]
NC_ROWS = NS + 1
HC, HP, HF = 2, 15, 30
NE = 64
NG = 8
TOPG = 4
FE = D // 4
EPS = 1e-6
ROUTED_SCALE = 2.5
BLK = 512
UNIT = BLK // 2
RING = 4
NBANK = 8

R_CONFW, R_CONVW, R_CONFB, R_CLNG, R_CLNB, R_PSC, R_N1G = 0, 31, 34, 35, 36, 37, 38
NPROW = 40

BLOCKS = ([("ada", j) for j in range(4)]
          + [("win", j) for j in (1, 7, 6, 3, 4, 5, 2, 0)]
          + [("ada", j) for j in range(4, 12)]
          + [x for k in (2, 1, 0, 3) for x in (("win", 8 + 2 * k), ("win", 9 + 2 * k), ("br", k))]
          + [("out", 0), ("out", 1)])
UNITS = [(kind, j, h) for kind, j in BLOCKS for h in range(2)]
UNIT_AT = {u: i for i, u in enumerate(UNITS)}
SPLIT = [u for u in UNITS if u[0] != "ada"]
SPLIT_AT = {u: i for i, u in enumerate(SPLIT)}
AHEAD = 4
BR_ORDER = (2, 1, 0, 3)
MIX_ORDER = (2, 0, 1)
LIST_BANK = 7


def jobs_of_mixer():
    out = ["cT"]
    for kind, j in BLOCKS:
        if kind == "ada":
            out += [("ada", j, h) for h in range(2)]
            if j == 2:
                out += ["prow0", "wsT"] + [("hist", n) for n in range(4)]
            if j == 3:
                out.append("modT")
                out += [("hT", k) for k in range(KT)]
            if j in (5, 7, 9, 11):
                out += [("bc", (j - 4) // 2, h) for h in range(2)]
        elif kind == "win" and j == 1:
            out += [("v", h, t) for h in range(2) for t in range(3)]
        elif kind == "win" and j < 8:
            out += [("z", j, c) for c in range(CT)]
            if j == 6:
                out.append("st_conf")
            if j == 4:
                out.append("st_conv")
            if j == 5:
                out.append("st_pool")
            if j == 0:
                out += [("sg", g) for g in range(CT)]
                out += [("pw", g) for g in range(CT)]
        elif kind == "win":
            k, half = (j - 8) // 2, (j - 8) % 2
            if half == 0:
                out += {0: ["cmean"], 3: ["cvar"]}.get(k, [])
            out += [("zg", k, 4 * half + c) for c in range(CT)]
        elif kind == "br":
            out += [("pr", j, d) for d in range(KT)]
    for n, t in enumerate(MIX_ORDER):
        out += [("mix", t, 0), ("mix", t, 1)]
        if n:
            out += [("h2T", MIX_ORDER[n - 1], h) for h in range(2)]
    out += [("h2T", MIX_ORDER[-1], h) for h in range(2)]
    out += ["logit", ("shared_gate", 0), ("shared_up", 0), "slot", ("shared_gate", 1), ("shared_up", 1), "lists"]
    return out


JOBS = jobs_of_mixer()
JOB = {name: i for i, name in enumerate(JOBS)}
FIRST_BANK = (LIST_BANK - JOB["lists"]) % NBANK


def bank_of(name):
    return (JOB[name] + FIRST_BANK) % NBANK, JOB[name] // NBANK


def last_job(u, q):
    kind, j, h = u
    if kind == "ada":
        return "ada", j, h
    if kind == "br":
        return "pr", j, 4 * h + 2 * q + 1
    if kind == "out":
        return "mix", MIX_ORDER[-1], j
    if j == 1:
        return "v", h, 2
    if j < 8:
        return "z", j, 2 * h + q
    return "zg", (j - 8) // 2, 4 * (j % 2) + 2 * h + q


BIG = 4096.0
CAP = P
ROUNDS = -(-TOK // CAP)
UNROLL = 4
NPARAM = 8
PIECE = 2 * 2 * FE
SLOTF = 2 * KT * FE + 2 * D


def bass_decoder_step(nc, x_prompt, x_sample, state_conv, state_pool, state_conf, c_prompt, c_sample,
                      ada_w, ada_b, norm1_g, norm2_g, w_in, sgu_ln_g, sgu_ln_b, sgu_w, sgu_b,
                      conv_w, pool_w, pool_scale, conf_w, conf_b, conf_ln_g, conf_ln_b,
                      w_branch, w_out, router_w, router_bias, e_gate, e_up, e_down,
                      s_gate, s_up, s_down, final_g,
                      y_prompt, y_sample, conv_p, pool_p, conf_p, conv_s, pool_s, conf_s, chunk_v_s,
                      h_table, y_even, y_odd):
    with ExitStack() as ctx:
        def sb(name, shape, dt=F32):
            return ctx.enter_context(nc.sbuf_tensor(name, shape, dt))

        twins = {}

        def sb_twin(name, shape):
            t = sb(name, shape)
            at = nc.sbuf_base - 4 * int(np.prod(shape[1:]))
            twins[name] = nc.alloc_sbuf_tensor_at(name + "_r", shape, F32R, offset=at)
            return t

        def as_r(ap):
            return bass.AP(tensor=twins[ap.tensor.name], offset=ap.offset, ap=ap.ap)

        def sem(name):
            return ctx.enter_context(nc.semaphore(name))

        psum = ctx.enter_context(nc.psum_tensor("psum", [P, NBANK, 512], F32))

        wexp = sb_twin("wexp", [P, UNROLL, SLOTF])
        ring_room = wexp[:, 2:4, :].rearrange("p a n -> p (a n)").rearrange("p (s n) -> p s n", s=RING + 2)
        early = wexp[:, 0:2, :].rearrange("p a n -> p (a n)")
        used = [0]

        def take(n):
            at = used[0]
            used[0] += n
            assert used[0] <= 2 * SLOTF
            return early[:, at:at + n]

        sg = take(KT * TOK).rearrange("p (k t) -> p k t", k=KT)
        AT_YBR1 = used[0] + CT * TOK
        ybr = take(4 * CT * TOK).rearrange("p (b c t) -> p b c t", b=4, c=CT)
        tmpT = take(CT * TOK).rearrange("p (c t) -> p c t", c=CT)
        AT_GLUP = used[0]
        gluP = take(CT * (HF + TOK)).rearrange("p (c t) -> p c t", c=CT)
        zcP = take(CT * (HP + TOK)).rearrange("p (c t) -> p c t", c=CT)
        AT_CGP = used[0]
        cgP = take(CT * (HC + TOK)).rearrange("p (c t) -> p c t", c=CT)
        convH = take(CT * NS * HC).rearrange("p (c s h) -> p c s h", c=CT, h=HC)
        poolH = take(CT * NS * HP).rearrange("p (c s h) -> p c s h", c=CT, h=HP)
        confH = take(CT * NS * HF).rearrange("p (c s h) -> p c s h", c=CT, h=HF)

        x_sb = sb("x_sb", [P, 3, D])
        xn = sb_twin("xn", [P, 3, D])
        hT = sb_twin("hT", [P, KT, TOK])
        mod = sb("mod", [NC_ROWS, 4 * D])
        bc = sb("bc", [P, 4, D])
        mT = sb_twin("mT", [P, KT, TOK])
        mid = sb_twin("mid", [P, 5 * D + 64])
        AT_V = CT * TOK
        AT_LN, AT_SGU = AT_V + 3 * BR, AT_V + 5 * BR
        dcv = mid[:, 0:CT * TOK].rearrange("p (c t) -> p c t", c=CT)
        v_sb = mid[:, AT_V:AT_LN].rearrange("p (t c) -> p t c", t=3)
        lnv = mid[:, AT_LN:AT_SGU].rearrange("p (a c) -> p a c", a=2)
        sgub, poolw, wsT = [mid[:, AT_SGU + n * BR:AT_SGU + (n + 1) * BR].rearrange("p (g q) -> p g q", g=CT) for n in range(3)]
        crow = mid[0:NC_ROWS, 0:D]
        sh_gu = mid[:, CT * TOK:CT * TOK + 2 * KT * FE].rearrange("p (a k f) -> p k a f", a=2, k=KT)
        piece_rooms = [mid[:, n * PIECE:(n + 1) * PIECE] for n in range(3)]
        xgT_hi = mid[:, 3 * D:4 * D].rearrange("p (k c) -> p k c", k=KT)
        xgT_lo = mid[:, 4 * D:5 * D].rearrange("p (k c) -> p k c", k=KT)
        w00 = sb("w00", [NS, CT])
        wdiag = sb("wdiag", [NS, CT, NS])
        rtw = sb("rtw", [P, KT, NE])
        rtb = sb("rtb", [P, NE])
        cT = sb("cT", [P, KT, NC_ROWS])
        prm = sb("prm", [P, CT, NPROW])
        S1 = sb("S1", [P, KT, NC_ROWS])
        G1 = sb("G1", [P, KT, NC_ROWS])
        ident = sb("ident", [P, P])
        lower = sb("lower", [P, P])
        iota_i = sb("iota_i", [P, P], I32)
        iota_f = sb("iota_f", [P, P])
        ones = sb("ones", [P, P])
        cmean = sb("cmean", [P, P])
        sel8 = sb("sel8", [NC_ROWS, P])
        rc = sb("rc", [P, 16])
        st = sb("st", [P, 3, 8])
        bns = sb("bns", [P, 3, 8])
        sc = sb("sc", [P, 3, NE])
        bsd = sb("bsd", [P, 3, NE])
        msk = sb("msk", [P, 3, NE])
        sel = sb("sel", [P, 3, NE])
        posm = sb("posm", [P, 3, NE])
        tab = sb("tab", [P, 3, NE, 2])
        cmp2 = sb("cmp2", [P, 3, NG, NG])
        epsc = sb("epsc", [P, 1])
        sqrt_first = sb("sqrt_first", [P, 1])
        gm = sb("gm", [P, 3, NG, 8])
        gs = sb("gs", [P, 3, NG])
        cmp_ = sb("cmp_", [P, 3, NG, NG])
        trig = sb("trig", [P, NG, NG])
        tokid = sb("tokid", [P, 3])
        valid = sb("valid", [P, 3])
        zeros = sb("zeros", [P, P])
        cnt_f = sb("cnt_f", [P, 1])
        cnt_i = sb("cnt_i", [P, 1], I32)
        tokid_i = sb("tokid_i", [P, 3], I32)
        idx = sb("idx", [P, UNROLL, 1], I32)
        scatter_row = sb("scatter_row", [P, UNROLL, 1], I32)
        gcol = sb("gcol", [P, UNROLL, 1])
        hist = mT[:, :, :].rearrange("p k t -> p (k t)")[:, 0:4 * BR].rearrange("p (n c) -> p n c", n=4)
        hTf = hT[:, :, :].rearrange("p k t -> p (k t)")
        prow = hTf[0:NPROW, 0:BR]
        wsr = hTf[:, BR:2 * BR].rearrange("p (g q) -> p g q", g=CT)
        st_rows = bc[:, 3, :].rearrange("p (a c) -> p a c", a=2)
        st_conf, st_conv, st_pool = st_rows[:, 0, :], st_rows[:, 1, :], bc[:, 1, 0:BR]
        y_rows = mT[:, :, :].rearrange("p k t -> p (k t)")[:, 0:2 * D].rearrange("p (b d) -> p b d", b=2)
        xg = [xn[:, 0, :], xn[:, 1, :], xn[:, 2, :], bc[:, 2, :]]
        xnf = xn[:, :, :].rearrange("p t d -> p (t d)")
        sums = xnf[:, 0:544].rearrange("p (a n) -> p a n", a=2)
        prod = xnf[:, 544:784].rearrange("p (s h) -> p s h", s=NS)
        stat = xnf[:, 0:2 * TOK].rearrange("p (a t) -> p a t", a=2)
        hT_hi = xnf[:, 784:784 + KT * TOK].rearrange("p (k t) -> p k t", k=KT)
        y_hi = early[:, AT_CGP:AT_CGP + CT * TOK].rearrange("p (c t) -> p c t", c=CT)
        m_hi = sg
        squares = early[:, AT_CGP:AT_CGP + D]
        spare_hi = [early[:, AT_GLUP:AT_GLUP + KT * UNIT], early[:, AT_YBR1:AT_YBR1 + KT * UNIT]]
        silu = hTf[:, 0:512].rearrange("p (b f) -> p b f", b=2)
        act = hTf[:, 512:1024].rearrange("p (b f) -> p b f", b=2)
        actT_hi = hTf[:, 1024:1536].rearrange("p (b j c) -> p b j c", b=2, j=2)
        actT_lo = hTf[:, 1536:2048].rearrange("p (b j c) -> p b j c", b=2, j=2)
        mTf = mT[:, :, :].rearrange("p k t -> p (k t)")
        sh_silu = mTf[:, 0:2 * TOK].rearrange("p (j t) -> p j t", j=2)
        sh_actT = mTf[:, 2 * TOK:4 * TOK].rearrange("p (j t) -> p j t", j=2)
        sh_part = mTf[:, 1056:1056 + D].rearrange("p (h n) -> p h n", h=2)
        fing = bc[:, 0, :]
        oh = bc[:, 1, 0:6 * P].rearrange("p (b t c) -> p b t c", b=2, t=3)

        bank_full = [sem(f"bank_full{b}") for b in range(NBANK)]
        bank_free = [sem(f"bank_free{b}") for b in range(NBANK)]
        ring_full = [sem(f"ring_full{s}") for s in range(RING)]
        names = """cnt_ready ld_c ya_ready v_stored sh_load ld_mod2 consts tables_zero x2_sq
                   sh_down_load h2_stored up_done down_done shared_done x_xt x_w even_load moe_done
                   fin_ready out_done pool_chain ld_stage wg_masked states_done w_hi w_lo h2_ready
                   lst_ready xt_done dma_may_go scatter_row_ready ys_act ys_dve down_hi down_lo_pool x2_ready
                   ld_fin x_idx x_gat x_y x_sc even_taken fin_samples st_stored c_silu
                   x_norm h_split v_ready ws_ready ld_param pooled_ready g2_rows dconv_ready sq_ready
                   y_split m_split sel_ready oh_ready list_done shared_taken xgt_lo act_ready up_lo
                   actT_ready tact_done x_oh x_list x_xgt x_gu x_act x_tact x_actT
                   x_dn act_chain ld_x x_sq g1_ready h_prompt h_ready h_hi v_mean
                   v_std y_hi_ready dn_ready yd_ready mrg_ready m_hi_ready up_hi xgt_hi actT_hi_ready
                   silu_ready x_silu fin_red fin_sq dve_chain ld_mod sg_used down_lo_dve""".split()
        S = {n: sem(n) for n in names}
        fin_ld = [sem(f"fin_ld{t}") for t in range(3)]
        gathered = [sem(f"gathered{b}") for b in range(UNROLL)]
        scattered = [sem(f"scattered{b}") for b in range(2)]
        gu_full = [sem(f"gu_full{s}") for s in range(UNROLL)]
        down_full = [sem(f"down_full{s}") for s in range(UNROLL)]

        def col(c, r, n=P):
            return prm[0:n, c, r:r + 1]

        def await_full(eng, name):
            b, before = bank_of(name)
            eng.wait_ge(bank_full[b], before + 1)
            return psum[:, b, :]

        def free(ins, name):
            return ins.then_inc(bank_free[bank_of(name)[0]], 1)

        def await_freed(eng, name):
            b, before = bank_of(name)
            eng.wait_ge(bank_free[b], before + 1)

        def rows_of(i, t, n, a, b):
            return mod[0:n, i * D + a:i * D + b] if t == 2 else bc[0:n, i, a:b]

        def need(eng, sem_, value):
            if not isinstance(value, int) or value > 0:
                eng.wait_ge(sem_, value)

        def unit_source(kind, j, h):
            if kind == "br":
                return w_branch[0, j, :, h * BLK:(h + 1) * BLK].rearrange("(k p) n -> p k n", p=P)
            w = {"ada": ada_w, "win": w_in, "out": w_out}[kind]
            at = j * BLK + h * UNIT
            return w[0, :, at:at + UNIT].rearrange("(k p) n -> p k n", p=P)

        def unit_view(u):
            return ring_room[:, UNIT_AT[u] % RING, :].rearrange("p (k n) -> p k n", k=CT if u[0] == "br" else KT)

        def low(u, q):
            view = unit_view(u)
            n = view.shape[2] // 2
            return view[:, :, q * n:(q + 1) * n]

        def high_room(u):
            c = SPLIT_AT[u]
            spare = c - len(SPLIT) + 4
            return spare_hi[spare] if spare in (0, 1) else ring_room[:, RING + c % 2, :]

        def high(u, q):
            n = KT * UNIT // 2
            return high_room(u)[:, q * n:(q + 1) * n].rearrange("p (k n) -> p k n", k=CT if u[0] == "br" else KT)

        def await_unit(eng, u):
            i = UNIT_AT[u]
            eng.wait_ge(ring_full[i % RING], 16 * (i // RING + 1))

        w_gu = [wexp[:, s, 0:4096].rearrange("p (a k f) -> p k a f", a=2, k=KT) for s in range(UNROLL)]
        w_dn = [wexp[:, s, 4096:6144].rearrange("p (j n) -> p j n", j=2) for s in range(UNROLL)]

        def piece(j, n):
            return w_gu[j][:, 2 * n:2 * n + 2] if n < 4 else w_dn[j][:, :, (n - 4) * BLK:(n - 3) * BLK]

        def piece_hi(e_is, n):
            if n < 4:
                room = piece_rooms[(n if e_is == "first" else n + 1) % 3]
                return room.rearrange("p (k a f) -> p k a f", k=2, a=2)
            room = piece_rooms[(n - 3 if e_is == "last" else n + 1) % 3]
            return room.rearrange("p (j n) -> p j n", j=2)

        def place(e):
            return "first" if isinstance(e, int) and e == 0 else "last" if isinstance(e, int) and e == NE - 1 else None

        gate_v = e_gate[0].rearrange("e (p k) f -> e p (k f)", k=KT)
        up_v = e_up[0].rearrange("e (p k) f -> e p (k f)", k=KT)
        down_v = e_down[0].rearrange("e (p j) n -> e p (j n)", j=2)
        fin_y = wexp[:, 1, :].rearrange("p (a t d) -> p a t d", a=2, t=3)

        def extra_passes(eng, step):
            eng.wait_ge(S["cnt_ready"], 1)
            longest = eng.value_load(cnt_i[0:1, 0:1], min_val=0, max_val=TOK)
            with eng.If(longest > CAP):
                for r in range(1, ROUNDS):
                    with eng.Fori(0, NE) as e:
                        step(r, e, NE * (r - 1) + e)

        block = ctx.enter_context(nc.Block())

        @block.sync
        def _(sp):
            sp.dma_start(crow[0:NS], c_sample).then_inc(S["ld_c"], 16)
            sp.dma_start(crow[NS:NC_ROWS], c_prompt).then_inc(S["ld_c"], 16)
            for i, u in enumerate(UNITS):
                if i >= RING:
                    await_full(sp, last_job(UNITS[i - RING], 1))
                sp.dma_start(unit_view(u), unit_source(*u)).then_inc(ring_full[i % RING], 16)
                if u == ("ada", 11, 1):
                    await_freed(sp, ("pw", CT - 1))
                    sp.wait_ge(S["ya_ready"], CT)
                    sp.wait_ge(S["v_stored"], 16)
                    for a, w in enumerate((s_gate, s_up)):
                        sp.dma_start(sh_gu[:, :, a, :], w[0].rearrange("(p k) f -> p k f", k=KT)).then_inc(S["sh_load"], 16)
                if u == ("ada", 5, 1):
                    await_full(sp, "modT")
                    sp.dma_start(mod[:, :], ada_b[0:1, 2 * D:].to_broadcast([NC_ROWS, 4 * D])).then_inc(S["ld_mod2"], 16)
            sp.wait_ge(S["consts"], 2)
            for table in (y_even, y_odd):
                for t0, p, a in ((0, P, 2), (SEQ, NS, 1)):
                    sp.dma_start(table[t0:t0 + p * a].rearrange("(p a) (b c) -> p (a b) c", p=p, c=P),
                                 zeros[0:p, :].unsqueeze(1).to_broadcast([p, a * KT, P])).then_inc(S["tables_zero"], 16)
            await_full(sp, ("mix", MIX_ORDER[-1], 1))
            sp.wait_ge(S["x2_sq"], 3)
            sp.dma_start(wexp[:, 1, 4096:6144], s_down[0].rearrange("(p j) n -> p (j n)", j=2)).then_inc(S["sh_down_load"], 16)

            def rows_of_expert(view, e):
                return view[e] if isinstance(e, int) else view[bass.ds(e, 1)].rearrange("e p n -> (e p) n")

            def load_gate_up(e, s):
                sp.dma_start(wexp[:, s, 0:2048], rows_of_expert(gate_v, e)).then_inc(gu_full[s], 16)
                sp.dma_start(wexp[:, s, 2048:4096], rows_of_expert(up_v, e)).then_inc(gu_full[s], 16)

            def load_down(e, s):
                sp.dma_start(wexp[:, s, 4096:6144], rows_of_expert(down_v, e)).then_inc(down_full[s], 16)

            sp.wait_ge(S["h2_stored"], 3 * 16)
            load_gate_up(0, 0)
            load_down(0, 0)
            load_gate_up(1, 1)
            load_gate_up(2, 2)
            load_down(2, 2)
            sp.wait_ge(gathered[0], 16)
            load_gate_up(3, 3)
            load_down(3, 3)
            def reload(i, s, down_too=True):
                e = UNROLL * i + s
                sp.wait_ge(S["up_done"], 4 * (e - 3))
                load_gate_up(e, s)
                if down_too:
                    sp.wait_ge(S["down_done"], 2 * (e - 4))
                    load_down(e - 1, (s - 1) % UNROLL)

            reload(1, 0, down_too=False)
            sp.wait_ge(S["shared_done"], 6)
            load_down(1, 1)
            for s in range(1, UNROLL):
                reload(1, s)
            with sp.Fori(2, NE // UNROLL) as i:
                for s in range(UNROLL):
                    reload(i, s)
            sp.wait_ge(S["down_done"], 2 * (NE - 4))
            load_down(NE - 1, UNROLL - 1)

            def extra(r, e, n):
                sp.wait_ge(S["x_xt"], n + 1)
                for at, view in ((0, gate_v), (2048, up_v), (4096, down_v)):
                    sp.dma_start(wexp[:, 0, at:at + 2048], view[bass.ds(e, 1)].rearrange("e p n -> (e p) n")).then_inc(S["x_w"], 16)

            sp.wait_ge(S["down_done"], 2 * (NE - 2))
            sp.wait_ge(scattered[0], 16 * (NE // 2))
            for t, (t0, n) in enumerate(TILES):
                sp.dma_start(fin_y[0:n, 0, t], y_even[t0:t0 + n]).then_inc(S["even_load"], 16)
            sp.wait_ge(S["down_done"], 2 * NE)
            extra_passes(sp, extra)
            sp.wait_ge(S["moe_done"], 1)
            for t in (2, 0, 1):
                t0, n = TILES[t]
                sp.dma_start(fin_y[0:n, 1, t], y_odd[t0:t0 + n]).then_inc(fin_ld[t], 16)
            for t, (t0, n) in enumerate(TILES):
                sp.wait_ge(S["fin_ready"], t + 1)
                dst = y_sample[:, 0, :] if t == 2 else y_prompt[0, t0:t0 + n, :]
                sp.dma_start(dst, x_sb[0:n, t, :]).then_inc(S["out_done"], 16)
            sp.wait_ge(S["out_done"], 3 * 16)

        @block.gpsimd
        def _(pool):
            n_chain = [0]

            def link(ins):
                n_chain[0] += 1
                ins.then_inc(S["pool_chain"], 1)
                pool.wait_ge(S["pool_chain"], n_chain[0])

            g = nc.gpsimd
            link(g.memset(ident[:], 0.0))
            g.affine_select(out=ident[:], in_=ident[:], compare_op=ALU.not_equal, fill=1.0, base=0,
                            pattern=[[-1, P]], channel_multiplier=1).then_inc(S["consts"], 1)
            g.memset(xn[:, 2, :], 0.0)
            g.memset(zeros[:], 0.0)
            g.memset(sel8[:], 0.0)
            g.memset(ones[:], 1.0)
            g.memset(cmean[:], 1.0 / BR)
            g.memset(lower[:], 1.0)
            g.memset(trig[:], 1.0)
            link(g.memset(valid[:], 1.0))
            g.affine_select(out=sel8[:], in_=sel8[:], compare_op=ALU.not_equal, fill=1.0, base=-NS,
                            pattern=[[0, P]], channel_multiplier=1)
            g.affine_select(out=lower[:], in_=lower[:], compare_op=ALU.is_ge, fill=0.0, base=-1,
                            pattern=[[1, P]], channel_multiplier=-1)
            g.affine_select(out=trig[:], in_=trig[:], compare_op=ALU.is_ge, fill=0.0, base=-1,
                            pattern=[[1, NG], [-1, NG]], channel_multiplier=0)
            g.affine_select(out=valid[:], in_=valid[:], compare_op=ALU.is_ge, fill=0.0, base=TOK - 1,
                            pattern=[[-P, 3]], channel_multiplier=-1)
            g.iota(iota_i[:], pattern=[[1, P]], base=0, channel_multiplier=0)
            g.iota(tokid_i[:], pattern=[[P, 3]], base=0, channel_multiplier=1)
            g.memset(gluP[:, :, 0:HF], 0.0)
            g.memset(zcP[:, :, 0:HP], 0.0)
            g.memset(cgP[:, :, 0:HC], 0.0)
            g.memset(st[:], 1.0)
            g.memset(bns[:], 1.0)
            g.memset(epsc[:], EPS)
            g.memset(sc[:], 0.0).then_inc(S["consts"], 1)
            pool.wait_ge(S["ld_stage"], 12 * 16)
            g.affine_select(out=wsr, in_=wsr, compare_op=ALU.is_ge, fill=0.0, base=0,
                            pattern=[[0, CT], [-1, P]], channel_multiplier=1).then_inc(S["wg_masked"], 1)
            with nc.allow_non_contiguous_dma(reason="history rows"):
                g.dma_start(conv_s[0, :, 0:HC - 1, :], state_conv[0, :, 1:HC, :]).then_inc(S["states_done"], 16)
                g.dma_start(pool_s[0, :, 0:HP - 1, :], state_pool[0, :, 1:HP, :]).then_inc(S["states_done"], 16)
                g.dma_start(conf_s[0, :, 0:HF - 1, :], state_conf[0, :, 1:HF, :]).then_inc(S["states_done"], 16)
            for c, u in enumerate(SPLIT):
                for q in range(2):
                    pool.wait_ge(S["w_hi"], 2 * c + q + 1)
                    g.tensor_tensor(out=as_r(low(u, q)), in0=low(u, q), in1=as_r(high(u, q)).bitcast(F32),
                                    op=ALU.subtract).then_inc(S["w_lo"], 1)
            for m, t in enumerate(MIX_ORDER):
                t0, n = TILES[t]
                pool.wait_ge(S["h2_ready"], m + 1)
                g.dma_start(h_table[t0:t0 + n], xn[0:n, t, :]).then_inc(S["h2_stored"], 16)
            pool.wait_ge(S["h2_stored"], 3 * 16)
            pool.wait_ge(S["tables_zero"], 4 * 16)

            last_token = pool.alloc_register("last_token")
            pool.reg_mov(last_token, TOK - 1)

            def gather(i, j):
                e = UNROLL * i + j
                pool.wait_ge(S["lst_ready"], e + 1)
                need(pool, S["xt_done"], e - 3)
                pool.sem_inc(S["dma_may_go"], 1)
                g.indirect_dma_start(out=xg[j], out_offset=None, in_=h_table,
                                     in_offset=bass.IndirectOffsetOnAxis(ap=idx[:, j, 0:1].bitcast(mybir.dt.uint32), axis=0),
                                     bounds_check=last_token, oob_is_err=False).then_inc(gathered[j], 16)

            def scatter(i, j):
                e = UNROLL * i + j
                pool.wait_ge(S["scatter_row_ready"], e + 1)
                need(pool, scattered[j % 2], 16 * (2 * i + j // 2))
                pool.wait_ge(S["ys_act"], e + 1)
                pool.wait_ge(S["ys_dve"], e + 1)
                pool.sem_inc(S["dma_may_go"], 1)
                g.indirect_dma_start(out=(y_even, y_odd)[j % 2], out_offset=bass.IndirectOffsetOnAxis(ap=scatter_row[:, j, :].bitcast(mybir.dt.uint32), axis=0),
                                     in_=y_rows[:, j % 2, :], in_offset=None,
                                     bounds_check=last_token, oob_is_err=False, compute_op=ALU.add).then_inc(scattered[j % 2], 16)

            def down_low(i, j):
                e = UNROLL * i + j
                hi, lo = piece_hi(place(e), 5), piece(j, 5)
                pool.wait_ge(S["down_hi"], 2 * e + 2)
                g.tensor_tensor(out=as_r(lo), in0=lo, in1=as_r(hi).bitcast(F32), op=ALU.subtract).then_inc(S["down_lo_pool"], 1)

            await_full(pool, ("h2T", MIX_ORDER[-1], 1))
            for j in range(UNROLL):
                gather(0, j)
            pool.wait_ge(S["x2_ready"], 6)
            g.dma_start(fing, final_g.rearrange("(a d) -> a d", a=1).to_broadcast([P, D])).then_inc(S["ld_fin"], 16)

            def body(i, first=False, last=False):
                for j in range(UNROLL):
                    if not (first and j == 0):
                        down_low(i if j else i - 1, (j - 1) % UNROLL)
                        scatter(i if j else i - 1, (j - 1) % UNROLL)
                    if not last:
                        gather(i + 1, j)

            body(0, first=True)
            with pool.Fori(1, NE // UNROLL - 1) as i:
                body(i)
            body(NE // UNROLL - 1, last=True)
            down_low(NE // UNROLL - 1, UNROLL - 1)
            scatter(NE // UNROLL - 1, UNROLL - 1)
            pool.wait_ge(scattered[0], 16 * (NE // 2))
            pool.wait_ge(scattered[1], 16 * (NE // 2))

            def extra(r, e, n):
                pool.wait_ge(S["x_idx"], n + 1)
                pool.sem_inc(S["dma_may_go"], 1)
                g.indirect_dma_start(out=xg[0], out_offset=None, in_=h_table,
                                     in_offset=bass.IndirectOffsetOnAxis(ap=idx[:, 0, 0:1].bitcast(mybir.dt.uint32), axis=0),
                                     bounds_check=last_token, oob_is_err=False).then_inc(S["x_gat"], 16)
                pool.wait_ge(S["x_y"], n + 1)
                pool.sem_inc(S["dma_may_go"], 1)
                g.indirect_dma_start(out=y_odd, out_offset=bass.IndirectOffsetOnAxis(ap=idx[:, 0, 0:1].bitcast(mybir.dt.uint32), axis=0),
                                     in_=y_rows[:, 0, :], in_offset=None,
                                     bounds_check=last_token, oob_is_err=False, compute_op=ALU.add).then_inc(S["x_sc"], 16)
                pool.wait_ge(S["x_sc"], 16 * n + 16)

            extra_passes(pool, extra)
            pool.sem_inc(S["moe_done"], 1)
            t, n = 2, NS
            pool.wait_ge(fin_ld[t], 16)
            link(g.tensor_tensor(out=fin_y[0:n, 1, t], in0=fin_y[0:n, 1, t], in1=rows_of(3, t, n, 0, D), op=ALU.mult))
            pool.wait_ge(S["even_taken"], 3)
            g.tensor_tensor(out=x_sb[0:n, t, :], in0=x_sb[0:n, t, :], in1=fin_y[0:n, 1, t], op=ALU.add).then_inc(S["fin_samples"], 1)
            pool.wait_ge(S["states_done"], 3 * 16)
            pool.wait_ge(S["v_stored"], 16)
            pool.wait_ge(S["st_stored"], 6 * 16)

        @block.tensor
        def _(pe):
            mm = nc.tensor.matmul

            def claim(name):
                b, before = bank_of(name)
                need(pe, bank_free[b], before)
                return psum[:, b, :]

            def full(ins, name):
                ins.then_inc(bank_full[bank_of(name)[0]], 1)

            def parts(kind, j, h, q=None):
                u = kind, j, h
                pe.wait_ge(S["w_lo"], 2 * SPLIT_AT[u] + (2 if q is None else q + 1))
                if q is not None:
                    return as_r(high(u, q)), as_r(low(u, q))
                return (as_r(high_room(u).rearrange("p (q k n) -> p k q n", q=2, k=KT)),
                        as_r(unit_view(u).rearrange("p k (q n) -> p k q n", q=2)))

            def mm3(out, a, b, start, stop):
                for x, y in ((0, 0), (0, 1), (1, 0)):
                    last = mm(out, a[x], b[y], start=start and x == y == 0, stop=stop and x == 1)
                return last

            def turn(out, src, rows):
                return nc.tensor.transpose(out, src, ident[0:rows, 0:rows])

            pe.wait_ge(S["consts"], 1)
            pe.wait_ge(S["c_silu"], 1)
            out = claim("cT")
            for k in range(KT):
                last = turn(out[:, k * NC_ROWS:(k + 1) * NC_ROWS], crow[:, k * P:(k + 1) * P], NC_ROWS)
            full(last, "cT")
            def ada(j):
                await_freed(pe, "cT")
                for h in range(2):
                    await_unit(pe, ("ada", j, h))
                    w = unit_view(("ada", j, h))
                    out = claim(("ada", j, h))
                    for k in range(KT):
                        last = mm(out[0:NC_ROWS, 0:UNIT], cT[:, k, :], w[:, k, :], start=(k == 0), stop=(k == KT - 1))
                    full(last, ("ada", j, h))

            for j in range(3):
                ada(j)
            pe.wait_ge(S["consts"], 2)
            pe.wait_ge(S["ld_stage"], 12 * 16)
            out = claim("prow0")
            for c in range(CT):
                last = turn(out[:, c * NPROW:(c + 1) * NPROW], prow[:, c * P:(c + 1) * P], NPROW)
            full(last, "prow0")
            pe.wait_ge(S["wg_masked"], 1)
            out = claim("wsT")
            for c in range(CT):
                last = turn(out[:, c * P:(c + 1) * P], wsr[:, c, :], P)
            full(last, "wsT")
            for n, rows in enumerate((NS * HC, NS * HP, 4 * HF, 4 * HF)):
                out = claim(("hist", n))
                for c in range(CT):
                    last = turn(out[:, c * rows:(c + 1) * rows], hist[0:rows, n, c * P:(c + 1) * P], rows)
                full(last, ("hist", n))

            ada(3)
            out = claim("modT")
            await_freed(pe, ("ada", 3, 1))
            for k in range(2 * KT):
                last = turn(out[:, k * NC_ROWS:(k + 1) * NC_ROWS], mod[:, k * P:(k + 1) * P], NC_ROWS)
            full(last, "modT")
            pe.wait_ge(S["x_norm"], 3)
            for k in range(KT):
                out = claim(("hT", k))
                for t, (t0, n) in enumerate(TILES):
                    last = turn(out[:, t0:t0 + n], xn[0:n, t, k * P:(k + 1) * P], n)
                full(last, ("hT", k))

            for half in range(2):
                w = parts("win", 1, half)
                for t, (t0, n) in enumerate(TILES):
                    out = claim(("v", half, t))
                    for k in range(KT):
                        if half == t == 0:
                            pe.wait_ge(S["h_split"], k + 1)
                        h = [as_r(hT_hi[:, k, t0:t0 + n]), as_r(hT[:, k, t0:t0 + n])]
                        last = mm3(out[0:n, 0:UNIT].rearrange("p (q n) -> p q n", q=2), h, [x[:, k] for x in w], start=(k == 0), stop=(k == KT - 1))
                    full(last, ("v", half, t))

            def columns(j, names):
                for c, name in enumerate(names):
                    w = parts("win", j, c // 2, c % 2)
                    out = claim(name)
                    for k in range(KT):
                        last = mm3(out[:, 0:TOK], [x[:, k, :] for x in w], [as_r(hT_hi[:, k, :]), as_r(hT[:, k, :])],
                                   start=(k == 0), stop=(k == KT - 1))
                    full(last, name)

            def state(name, made_of, src, at, n):
                await_freed(pe, made_of)
                out = claim(name)
                for c in range(CT):
                    last = turn(out[0:n, c * P:(c + 1) * P], src[:, c, at:at + n], P)
                full(last, name)

            for j in (7, 6, 3, 4, 5, 2, 0):
                columns(j, [("z", j, c) for c in range(CT)])
                if j == 6:
                    state("st_conf", ("z", 6, CT - 1), gluP, SEQ, HF + NS)
                if j == 4:
                    state("st_conv", ("z", 4, CT - 1), cgP, SEQ, HC + NS)
                if j == 5:
                    state("st_pool", ("z", 5, CT - 1), zcP, SEQ, HP + NS)
            pe.wait_ge(S["v_ready"], 1)
            pe.wait_ge(S["ws_ready"], 1)
            for c in range(CT):
                out = claim(("sg", c))
                for t in range(2):
                    mm(out[:, t * P:(t + 1) * P], v_sb[:, t, c * P:(c + 1) * P], wsT[:, c, :], start=True, stop=True)
                last = mm(out[:, SEQ:TOK], v_sb[0:NS, 2, c * P:(c + 1) * P], wdiag[:, c, :], start=True, stop=True)
                full(last, ("sg", c))
            pe.wait_ge(S["ld_param"], NPARAM * 16)
            pe.wait_ge(S["pooled_ready"], CT)
            for c in range(CT):
                out = claim(("pw", c))
                full(mm(out[:, 0:TOK], poolw[:, c, :], ybr[:, 2, c, :], start=True, stop=True), ("pw", c))
            for j in range(4, 12):
                ada(j)
                if j % 2:
                    i = (j - 5) // 2
                    await_freed(pe, ("ada", j, 1))
                    if i == 2:
                        pe.wait_ge(S["g2_rows"], 1)
                    for h in range(2):
                        out = claim(("bc", i, h))
                        at = i * D + h * BLK
                        full(mm(out, sel8[:, :], mod[:, at:at + BLK], start=True, stop=True), ("bc", i, h))
            for n, k in enumerate(BR_ORDER):
                if k == 0:
                    pe.wait_ge(S["dconv_ready"], 1)
                    out = claim("cmean")
                    for c in range(CT):
                        last = mm(out[:, 0:TOK], cmean[:, :], dcv[:, c, :], start=(c == 0), stop=(c == CT - 1))
                    full(last, "cmean")
                if k == 3:
                    pe.wait_ge(S["sq_ready"], 1)
                    out = claim("cvar")
                    for c in range(CT):
                        last = mm(out[:, 0:TOK], cmean[:, :], tmpT[:, c, :], start=(c == 0), stop=(c == CT - 1))
                    full(last, "cvar")
                for half in range(2):
                    columns(8 + 2 * k + half, [("zg", k, 4 * half + c) for c in range(CT)])
                pe.wait_ge(S["y_split"], n + 1)
                for d in range(KT):
                    w = parts("br", k, d // 4, d // 2 % 2)
                    out = claim(("pr", k, d))
                    at = d % 2 * P
                    for c in range(CT):
                        last = mm3(out[:, 0:TOK], [x[:, c, at:at + P] for x in w], [as_r(y_hi[:, c, :]), as_r(ybr[:, k, c, :])],
                                   start=(c == 0), stop=(c == CT - 1))
                    full(last, ("pr", k, d))
            pe.wait_ge(S["m_split"], KT)

            def turn_h(t):
                t0, n = TILES[t]
                pe.wait_ge(S["h2_ready"], MIX_ORDER.index(t) + 1)
                for h in range(2):
                    out = claim(("h2T", t, h))
                    for k in range(4 * h, 4 * h + 4):
                        last = turn(out[:, (k % 4) * n:(k % 4 + 1) * n], xn[0:n, t, k:D:KT], n)
                    full(last, ("h2T", t, h))

            for m, t in enumerate(MIX_ORDER):
                t0, n = TILES[t]
                for j in range(2):
                    out = claim(("mix", t, j))
                    for h in range(2):
                        w = parts("out", j, h)
                        for k in range(KT):
                            last = mm3(out[0:n, h * UNIT:(h + 1) * UNIT].rearrange("p (q n) -> p q n", q=2), [as_r(m_hi[:, k, t0:t0 + n]), as_r(mT[:, k, t0:t0 + n])],
                                       [x[:, k] for x in w], start=(k == 0), stop=(k == KT - 1))
                    full(last, ("mix", t, j))
                if m:
                    turn_h(MIX_ORDER[m - 1])
            turn_h(MIX_ORDER[-1])
            for t in MIX_ORDER:
                await_freed(pe, ("h2T", t, 1))
            out = claim("logit")
            for t, (t0, n) in enumerate(TILES):
                for k in range(KT):
                    last = mm(out[0:n, t * NE:(t + 1) * NE], hT[:, k, t0:t0 + n], rtw[:, k, :], start=(k == 0), stop=(k == KT - 1))
            full(last, "logit")

            def shared_product(name, a, j):
                out = claim((name, j))
                for k in range(KT):
                    last = mm(out[:, 0:TOK], sh_gu[:, k, a, j:FE:2], hT[:, k, :], start=(k == 0), stop=(k == KT - 1))
                full(last, (name, j))

            pe.wait_ge(S["sh_load"], 32)
            shared_product("shared_gate", 0, 0)
            shared_product("shared_up", 1, 0)
            pe.wait_ge(S["sel_ready"], 1)
            out = claim("slot")
            for t in range(3):
                for u in range(t):
                    mm(out[:, t * NE:(t + 1) * NE], ones[:, :], sel[:, u, :], start=(u == 0), stop=False)
                mm(out[:, t * NE:(t + 1) * NE], lower[:, :], sel[:, t, :], start=(t == 0), stop=True)
            for t in range(3):
                last = mm(out[:, 3 * NE:4 * NE], ones[:, :], sel[:, t, :], start=(t == 0), stop=(t == 2))
            full(last, "slot")

            def token_list(i, j):
                e = UNROLL * i + j
                pe.wait_ge(S["oh_ready"], e + 1)
                need(pe, S["lst_ready"], e)
                for t in range(3):
                    rhs = tab[:, t, :, :].rearrange("p e c -> p (e c)")
                    rhs = rhs[:, 2 * e:2 * e + 2] if isinstance(e, int) else rhs[:, bass.ds(2 * e, 2)]
                    last = mm(psum[:, LIST_BANK, 0:2], oh[:, j % 2, t, :], rhs, start=(t == 0), stop=(t == 2))
                last.then_inc(S["list_done"], 1)

            claim("lists")
            token_list(0, 0)
            shared_product("shared_gate", 0, 1)
            token_list(0, 1)
            shared_product("shared_up", 1, 1)
            token_list(0, 2)
            token_list(0, 3)

            def shared_down():
                await_freed(pe, ("shared_up", 1))
                pe.wait_ge(S["sh_down_load"], 16)
                for t, (t0, n) in enumerate(TILES):
                    for h in range(2):
                        need(pe, S["shared_taken"], 2 * t + h - 1)
                        for f in range(2):
                            last = mm(psum[0:n, 3 + h, :], sh_actT[:, f, t0:t0 + n], w_dn[1][:, f, h * BLK:(h + 1) * BLK],
                                      start=(f == 0), stop=(f == 1))
                        last.then_inc(S["shared_done"], 1)

            for b in range(NBANK - 1):
                uses = len([1 for name in JOBS if bank_of(name)[0] == b])
                pe.wait_ge(bank_free[b], uses)

            def turn_rows(i, j):
                e = UNROLL * i + j
                pe.wait_ge(gathered[j], 16 * (i + 1))
                need(pe, S["xgt_lo"], e)
                for k in range(KT):
                    last = turn(psum[:, 5 + k // 4, (k % 4) * P:(k % 4 + 1) * P], xg[j][:, k:D:KT], P)
                last.then_inc(S["xt_done"], 1)

            def up(i, j, pieces):
                e = UNROLL * i + j
                if pieces[0] == 0:
                    pe.wait_ge(S["xgt_lo"], e + 1)
                    need(pe, S["act_ready"], e - 1)
                for n in pieces:
                    pe.wait_ge(S["up_lo"], 4 * e + n + 1)
                    hi, lo = as_r(piece_hi(place(e), n)), as_r(piece(j, n))
                    for kk in range(2):
                        k = 2 * n + kk
                        last = mm3(psum[:, j % 2, :].rearrange("p (a f) -> p a f", a=2), [as_r(xgT_hi[:, k, :]), as_r(xgT_lo[:, k, :])],
                                   [hi[:, kk], lo[:, kk]], start=(k == 0), stop=(k == KT - 1))
                    last.then_inc(S["up_done"], 1)

            def turn_act(i, j):
                e = UNROLL * i + j
                pe.wait_ge(S["act_ready"], e + 1)
                need(pe, S["actT_ready"], e)
                for h in range(2):
                    last = turn(psum[:, 2, h * P:(h + 1) * P], act[:, j % 2, h:FE:2], P)
                last.then_inc(S["tact_done"], 1)

            def down(i, j):
                e = UNROLL * i + j
                pe.wait_ge(S["actT_ready"], e + 1)
                for h in range(2):
                    pe.wait_ge(S["down_lo_pool" if h else "down_lo_dve"], e + 1)
                    if place(e) == "first":
                        pe.wait_ge(S["shared_taken"], 6)
                    need(pe, S["ys_dve" if h else "ys_act"], e)
                    hi, lo = as_r(piece_hi(place(e), 4 + h)), as_r(piece(j, 4 + h))
                    for f in range(2):
                        last = mm3(psum[:, 3 + h, :], [as_r(actT_hi[:, j % 2, f, :]), as_r(actT_lo[:, j % 2, f, :])],
                                   [hi[:, f, :], lo[:, f, :]], start=(f == 0), stop=(f == 1))
                    last.then_inc(S["down_done"], 1)

            def body(i, first=False, last=False):
                for j in range(UNROLL):
                    prev = not (first and j == 0)
                    pi, pj = (i if j else i - 1), (j - 1) % UNROLL
                    up(i, j, (0, 1))
                    if prev:
                        turn_act(pi, pj)
                    up(i, j, (2, 3))
                    if not (last and j == UNROLL - 1):
                        turn_rows(i if j < 3 else i + 1, (j + 1) % UNROLL)
                    if prev:
                        down(pi, pj)
                    else:
                        shared_down()
                    if not last:
                        token_list(i + 1, j)

            turn_rows(0, 0)
            body(0, first=True)
            with pe.Fori(1, NE // UNROLL - 1) as i:
                body(i)
            body(NE // UNROLL - 1, last=True)
            turn_act(NE // UNROLL - 1, UNROLL - 1)
            down(NE // UNROLL - 1, UNROLL - 1)


            def extra(r, e, n):
                pe.wait_ge(S["x_oh"], n + 1)
                for t in range(3):
                    rhs = tab[:, t, :, :].rearrange("p e c -> p (e c)")[:, bass.ds(2 * e, 2)]
                    last = mm(psum[:, LIST_BANK, 0:2], oh[:, 0, t, :], rhs, start=(t == 0), stop=(t == 2))
                last.then_inc(S["x_list"], 1)
                pe.wait_ge(S["x_gat"], 16 * n + 16)
                for k in range(KT):
                    last = turn(psum[:, 5 + k // 4, (k % 4) * P:(k % 4 + 1) * P], xg[0][:, k:D:KT], P)
                last.then_inc(S["x_xt"], 1)
                pe.wait_ge(S["x_xgt"], n + 1)
                pe.wait_ge(S["x_w"], 48 * n + 48)
                for k in range(KT):
                    last = mm(psum[:, 0, :], xgT_hi[:, k, :], w_gu[0][:, k], start=(k == 0), stop=(k == KT - 1))
                last.then_inc(S["x_gu"], 1)
                pe.wait_ge(S["x_act"], n + 1)
                for h in range(2):
                    last = turn(psum[:, 2, h * P:(h + 1) * P], act[:, 0, h:FE:2], P)
                last.then_inc(S["x_tact"], 1)
                pe.wait_ge(S["x_actT"], n + 1)
                for h in range(2):
                    for f in range(2):
                        last = mm(psum[:, 3 + h, :], actT_hi[:, 0, f, :], w_dn[0][:, f, h * BLK:(h + 1) * BLK], start=(f == 0), stop=(f == 1))
                last.then_inc(S["x_dn"], 1)

            extra_passes(pe, extra)

        @block.scalar
        def _(ac):
            n_chain = [0]

            def link(ins):
                n_chain[0] += 1
                ins.then_inc(S["act_chain"], 1)
                ac.wait_ge(S["act_chain"], n_chain[0])

            def load(dst, src, name):
                ac.dma_start(dst, src).then_inc(S[name], 16)

            F = nc.scalar.activation
            load(x_sb[:, 0:2, :], x_prompt[0].rearrange("(t p) d -> p t d", p=P), "ld_x")
            load(x_sb[0:NS, 2, :], x_sample[:, 0, :], "ld_x")
            load(mod[:, 0:2 * D], ada_b[0:1, 0:2 * D].to_broadcast([NC_ROWS, 2 * D]), "ld_mod")
            ac.wait_ge(S["ld_c"], 32)
            F(crow[:, :], crow[:, :], ACT.Silu).then_inc(S["c_silu"], 1)
            load(prow[R_CONFW:R_CONFW + 31], conf_w[0], "ld_stage")
            load(prow[R_CONVW:R_CONVW + 3], conv_w[0], "ld_stage")
            for r, p in ((R_CONFB, conf_b), (R_CLNG, conf_ln_g), (R_CLNB, conf_ln_b), (R_PSC, pool_scale)):
                load(prow[r:r + 1], p, "ld_stage")
            load(prow[R_N1G:R_N1G + 2], norm1_g.rearrange("a (r c) -> (a r) c", r=2), "ld_stage")
            load(wsr, sgu_w[0].rearrange("g p q -> p g q"), "ld_stage")
            load(hist[0:NS * HC, 0, :], state_conv[0].rearrange("s h c -> (s h) c"), "ld_stage")
            load(hist[0:NS * HP, 1, :], state_pool[0].rearrange("s h c -> (s h) c"), "ld_stage")
            for a in range(2):
                load(hist[0:4 * HF, 2 + a, :], state_conf[0, 4 * a:4 * a + 4].rearrange("s h c -> (s h) c"), "ld_stage")
            load(lnv[:, 0, :], sgu_ln_g.to_broadcast([P, BR]), "ld_param")
            load(lnv[:, 1, :], sgu_ln_b.to_broadcast([P, BR]), "ld_param")
            load(sgub, sgu_b[0:1].rearrange("a g q -> a (g q)").to_broadcast([P, BR]).rearrange("p (g q) -> p g q", g=CT), "ld_param")
            with nc.allow_non_contiguous_dma(reason="one weight per group"):
                load(w00[:], sgu_w[0, :, 0, 0:1].rearrange("g a -> a g").to_broadcast([NS, CT]), "ld_param")
            load(poolw, pool_w[0].rearrange("g c d -> c g d"), "ld_param")
            load(rtw[:], router_w[0].rearrange("(p k) e -> p k e", k=KT), "ld_param")
            load(rtb[:], router_bias.to_broadcast([P, NE]), "ld_param")
            load(bc[0:NC_ROWS, 2, :], norm2_g.to_broadcast([NC_ROWS, D]), "ld_param")


            def row_norm(src_sem, value, done):
                ac.wait_ge(src_sem, value)
                for t, (t0, n) in enumerate(TILES):
                    last = F(xn[0:n, t, :], x_sb[0:n, t, :], ACT.Square, accum_out=st[0:n, t, 0:1])
                link(last)
                F(st[:, :, 1], st[:, :, 0], ACT.Sqrt, scale=1.0 / D, bias=epsc[:, 0:1]).then_inc(done, 1)

            ac.wait_ge(S["consts"], 2)
            row_norm(S["ld_x"], 32, S["x_sq"])

            n_split = [0]
            before_ada = 2 * SPLIT_AT["win", 12, 0]

            def split_until(end):
                for m in range(n_split[0], min(end, 2 * len(SPLIT))):
                    u, q = SPLIT[m // 2], m % 2
                    if q == 0:
                        await_unit(ac, u)
                    if u == ("out", 0, 0):
                        ac.wait_ge(S["dconv_ready"], 1)
                    elif u == ("out", 0, 1):
                        await_full(ac, ("pr", 1, KT - 1))
                    elif m >= AHEAD:
                        held = SPLIT[m // 2 - (4 if u[0] == "out" else 2)]
                        await_full(ac, last_job(held, q))
                    F(as_r(high(u, q)), low(u, q), ACT.Copy).then_inc(S["w_hi"], 1)
                n_split[0] = max(n_split[0], end)

            def while_pe_on(kind, j, h, q):
                m = 2 * SPLIT_AT[kind, j, h] + q
                split_until(min(m + AHEAD, before_ada) if m < before_ada else m + AHEAD)

            split_until(AHEAD)
            ac.wait_ge(S["g1_ready"], 1)
            for k in range(KT + 1):
                if k < KT:
                    b = await_full(ac, ("hT", k))
                    F(hT[:, k, 0:SEQ], b[:, 0:SEQ], ACT.Identity, scale=G1[:, k, NS:NC_ROWS], bias=S1[:, k, NS:NC_ROWS]).then_inc(S["h_prompt"], 1)
                if k == 1:
                    await_full(ac, ("hT", KT - 1))
                if k:
                    ac.wait_ge(S["h_prompt"], k)
                    ac.wait_ge(S["h_ready"], k)
                    F(as_r(hT_hi[:, k - 1, :]), hT[:, k - 1, :], ACT.Copy).then_inc(S["h_hi"], 1)
            for half in range(2):
                while_pe_on("win", 1, half, 0)
                for t, (t0, n) in enumerate(TILES):
                    b = await_full(ac, ("v", half, t))
                    free(F(v_sb[0:n, t, half * UNIT:(half + 1) * UNIT], b[0:n, 0:UNIT], ACT.Gelu), ("v", half, t))
            ac.wait_ge(S["v_mean"], 1)
            F(st[:, :, 6], st[:, :, 5], ACT.Sqrt, bias=epsc[:, 0:1]).then_inc(S["v_std"], 1)

            def z_out(j, func, dst, reader):
                for c in range(CT):
                    while_pe_on("win", j, c // 2, c % 2)
                    b = await_full(ac, ("z", j, c))
                    if reader:
                        await_freed(ac, ("z", reader, c))
                    free(F(dst(c), b[:, 0:TOK], func), ("z", j, c))

            def state_rows(name, rows, h, prompt, sample):
                b = await_full(ac, name)
                free(F(rows[0:h + NS, :], b[0:h + NS, :], ACT.Copy), name)
                await_freed(ac, name)
                ac.dma_start(prompt[0, 0], rows[0:h, :]).then_inc(S["st_stored"], 16)
                ac.dma_start(sample[0, :, h - 1, :], rows[h:h + NS, :]).then_inc(S["st_stored"], 16)

            z_out(7, ACT.Sigmoid, lambda c: tmpT[:, c, :], None)
            ac.wait_ge(S["v_ready"], 1)
            ac.dma_start(chunk_v_s[0, :, 0, :], v_sb[0:NS, 2, :]).then_inc(S["v_stored"], 16)
            for c in range(CT):
                while_pe_on("win", 6, c // 2, c % 2)
            state_rows("st_conf", st_conf, HF, conf_p, conf_s)
            z_out(3, ACT.Copy, lambda c: tmpT[:, c, :], 6)
            for c in range(CT):
                while_pe_on("win", 4, c // 2, c % 2)
            state_rows("st_conv", st_conv, HC, conv_p, conv_s)
            z_out(5, ACT.Copy, lambda c: zcP[:, c, HP:], None)
            for c in range(CT):
                while_pe_on("win", 2, c // 2, c % 2)
            state_rows("st_pool", st_pool, HP, pool_p, pool_s)
            z_out(0, ACT.Gelu, lambda c: tmpT[:, c, :], 4)

            def spread_out(i):
                for h in range(2):
                    b = await_full(ac, ("bc", i, h))
                    if i in (1, 3):
                        ac.wait_ge(S["st_stored"], 6 * 16)
                    free(F(bc[:, i, h * BLK:(h + 1) * BLK], b[:, :], ACT.Copy), ("bc", i, h))

            for i in range(3):
                spread_out(i)
            split_until(before_ada + AHEAD)
            spread_out(3)

            def split_y(n, k):
                if n == 0:
                    await_freed(ac, ("pw", CT - 1))
                else:
                    await_full(ac, ("pr", BR_ORDER[n - 1], KT - 1))
                if k == 1:
                    await_freed(ac, ("z", 2, CT - 1))
                elif k != 2:
                    ac.wait_ge(S["ya_ready" if k == 0 else "yd_ready"], CT)
                F(as_r(y_hi), ybr[:, k], ACT.Copy).then_inc(S["y_hi_ready"], 1)

            for n, k in enumerate(BR_ORDER):
                if k == 0:
                    await_freed(ac, "cmean")
                    F(tmpT[:, :, :], dcv[:, :, :], ACT.Square).then_inc(S["sq_ready"], 1)
                if k == 3:
                    b = await_full(ac, "cvar")
                    free(F(stat[:, 0, :], b[:, 0:TOK], ACT.Sqrt, bias=epsc[:, 0:1]), "cvar")
                    ac.wait_ge(S["dn_ready"], 1)
                    for c in range(CT):
                        F(ybr[:, 3, c, :], dcv[:, c, :], ACT.Silu, scale=col(c, R_CLNG), bias=col(c, R_CLNB)).then_inc(S["yd_ready"], 1)
                split_y(n, k)
                for d in range(KT):
                    while_pe_on("win", 8 + 2 * k + d // 4, d // 2 % 2, d % 2)
                    b = await_full(ac, ("zg", k, d))
                    if n:
                        await_freed(ac, ("pr", BR_ORDER[n - 1], d))
                    free(F(sg[:, d, :], b[:, 0:TOK], ACT.Sigmoid), ("zg", k, d))
                for q in range(4):
                    while_pe_on("br", k, q // 2, q % 2)
            split_until(2 * SPLIT_AT["out", 1, 0])
            for half in range(2):
                for d in range(4 * half, 4 * half + 4):
                    ac.wait_ge(S["mrg_ready"], d + 1)
                    F(as_r(m_hi[:, d, :]), mT[:, d, :], ACT.Copy).then_inc(S["m_hi_ready"], 1)
                split_until(2 * SPLIT_AT["out", 1, half] + 2)
            def h2_out(t):
                t0, n = TILES[t]
                for h in range(2):
                    b = await_full(ac, ("h2T", t, h))
                    free(F(hT[:, 4 * h:4 * h + 4, t0:t0 + n], b[:, 0:4 * n].rearrange("p (k c) -> p k c", k=4), ACT.Copy), ("h2T", t, h))

            for m, t in enumerate(MIX_ORDER):
                t0, n = TILES[t]
                ac.wait_ge(S["x2_ready"], 2 * m + 2)
                link(F(squares[0:n, :], x_sb[0:n, t, :], ACT.Square, accum_out=st[0:n, t, 0:1]))
                F(st[0:n, t, 1:2], st[0:n, t, 0:1], ACT.Sqrt, scale=1.0 / D, bias=epsc[0:n, 0:1]).then_inc(S["x2_sq"], 1)
                if m:
                    h2_out(MIX_ORDER[m - 1])
            h2_out(MIX_ORDER[-1])
            b = await_full(ac, "logit")
            for t, (t0, n) in enumerate(TILES):
                last = F(sc[0:n, t, :], b[0:n, t * NE:(t + 1) * NE], ACT.Sigmoid)
            free(last, "logit")

            for j in range(2):
                b = await_full(ac, ("shared_gate", j))
                free(F(sh_silu[:, j, :], b[:, 0:TOK], ACT.Silu), ("shared_gate", j))
            def up_high(i, j, n):
                e = UNROLL * i + j
                if n == 0:
                    ac.wait_ge(gu_full[j], 32 * (i + 1))
                if n in (0, 3):
                    need(ac, S["up_done"], 4 * e + n // 3)
                else:
                    need(ac, S["down_done"], 2 * e + n - 4)
                F(as_r(piece_hi(place(e), n)), piece(j, n), ACT.Copy).then_inc(S["up_hi"], 1)

            def down_high(i, j, f):
                e = UNROLL * i + j
                if f == 0:
                    ac.wait_ge(down_full[j], 16 * (i + 1))
                if place(e) != "last":
                    ac.wait_ge(S["up_done"], 4 * e + 6 + f)
                elif f == 0:
                    ac.wait_ge(S["up_done"], 4 * e + 4)
                else:
                    ac.wait_ge(S["down_done"], 2 * e - 1)
                F(as_r(piece_hi(place(e), 4 + f)), piece(j, 4 + f), ACT.Copy).then_inc(S["down_hi"], 1)

            def rows_high(i, j):
                e = UNROLL * i + j
                ac.wait_ge(S["xt_done"], e + 1)
                need(ac, S["up_done"], 4 * e)
                F(as_r(xgT_hi), psum[:, 5:7, :].rearrange("p b (k c) -> p (b k) c", k=4), ACT.Copy).then_inc(S["xgt_hi"], 1)

            def act_high(i, j):
                e = UNROLL * i + j
                ac.wait_ge(S["tact_done"], e + 1)
                need(ac, S["down_done"], 2 * e - 2)
                F(as_r(actT_hi[:, j % 2]), psum[:, 2, 0:2 * P].rearrange("p (h c) -> p h c", h=2), ACT.Copy).then_inc(S["actT_hi_ready"], 1)

            def y_out(i, j):
                e = UNROLL * i + j
                ac.wait_ge(S["down_done"], 2 * e + 1)
                need(ac, scattered[j % 2], 16 * (2 * i + j // 2))
                F(y_rows[:, j % 2, 0:BLK], psum[:, 3, :], ACT.Copy).then_inc(S["ys_act"], 1)

            def body(i, first=False, last=False):
                for j in range(UNROLL):
                    prev = not (first and j == 0)
                    more = not (last and j == UNROLL - 1)
                    pi, pj = (i if j else i - 1), (j - 1) % UNROLL
                    ni, nj = (i if j < 3 else i + 1), (j + 1) % UNROLL
                    e = UNROLL * i + j
                    up_high(i, j, 3)
                    if prev:
                        down_high(pi, pj, 0)
                        act_high(pi, pj)
                        down_high(pi, pj, 1)
                    ac.wait_ge(S["up_done"], 4 * e + 4)
                    need(ac, S["act_ready"], e - 1)
                    F(silu[:, j % 2, :], psum[:, j % 2, 0:FE], ACT.Silu).then_inc(S["silu_ready"], 1)
                    if more:
                        up_high(ni, nj, 0)
                        rows_high(ni, nj)
                        up_high(ni, nj, 1)
                        up_high(ni, nj, 2)
                    if prev:
                        y_out(pi, pj)

            up_high(0, 0, 0)
            await_full(ac, ("shared_up", 1))
            up_high(0, 0, 1)
            up_high(0, 0, 2)
            rows_high(0, 0)
            body(0, first=True)
            with ac.Fori(1, NE // UNROLL - 1) as i:
                body(i)
            body(NE // UNROLL - 1, last=True)
            down_high(NE // UNROLL - 1, UNROLL - 1, 0)
            act_high(NE // UNROLL - 1, UNROLL - 1)
            down_high(NE // UNROLL - 1, UNROLL - 1, 1)
            y_out(NE // UNROLL - 1, UNROLL - 1)

            def extra(r, e, n):
                ac.wait_ge(S["x_gu"], n + 1)
                F(silu[:, 0, :], psum[:, 0, 0:FE], ACT.Silu).then_inc(S["x_silu"], 1)
                ac.wait_ge(S["x_tact"], n + 1)
                F(actT_hi[:, 0], psum[:, 2, 0:2 * P].rearrange("p (h c) -> p h c", h=2), ACT.Copy).then_inc(S["x_actT"], 1)

            F(sqrt_first[:], epsc[:], ACT.Sqrt)
            extra_passes(ac, extra)
            for t, (t0, n) in enumerate(TILES):
                if t == 2:
                    ac.wait_ge(S["fin_samples"], 1)
                else:
                    ac.wait_ge(S["fin_red"], t + 1)
                link(F(xn[0:n, t, :], x_sb[0:n, t, :], ACT.Square, accum_out=st[0:n, t, 0:1]))
                F(st[0:n, t, 1:2], st[0:n, t, 0:1], ACT.Sqrt, scale=1.0 / D, bias=epsc[0:n, 0:1]).then_inc(S["fin_sq"], 1)

        @block.vector
        def _(ve):
            n_chain = [0]
            V = nc.vector

            def mark(ins):
                n_chain[0] += 1
                ins.then_inc(S["dve_chain"], 1)
                return n_chain[0]

            def link(ins):
                ve.wait_ge(S["dve_chain"], mark(ins))

            ve.wait_ge(S["consts"], 2)
            V.tensor_copy(tokid[:], tokid_i[:])
            link(V.tensor_copy(iota_f[:], iota_i[:]))
            link(V.tensor_scalar(rc[:], iota_f[:, 0:16], 1.0, None, ALU.add))
            V.reciprocal(rc[:], rc[:])
            link(V.tensor_scalar(tokid[:], tokid[:], -BIG, None, ALU.add))
            V.tensor_copy(tab[:, :, :, 0], tokid[:].unsqueeze(2).to_broadcast([P, 3, NE]))
            b = await_full(ve, "cT")
            free(V.tensor_copy(cT[:].rearrange("p k r -> p (k r)"), b[:, 0:KT * NC_ROWS]), "cT")
            def ada_out(j):
                for h in range(2):
                    b = await_full(ve, ("ada", j, h))
                    at = (j if j < 4 else j - 4) * BLK + h * UNIT
                    free(V.tensor_tensor(mod[:, at:at + UNIT], b[0:NC_ROWS, 0:UNIT], mod[:, at:at + UNIT], ALU.add), ("ada", j, h))

            ve.wait_ge(S["ld_mod"], 16)
            ada_out(0)
            ada_out(1)
            ve.wait_ge(S["x_sq"], 1)
            link(V.reciprocal(st[:, :, 2], st[:, :, 1]))
            for t, (t0, n) in enumerate(TILES):
                V.tensor_scalar(xn[0:n, t, :], x_sb[0:n, t, :], st[0:n, t, 2:3], None, ALU.mult).then_inc(S["x_norm"], 1)
            ada_out(2)
            b = await_full(ve, "prow0")
            free(V.tensor_copy(prm[:].rearrange("p c r -> p (c r)"), b[:, 0:CT * NPROW]), "prow0")
            b = await_full(ve, "wsT")
            free(V.tensor_copy(wsT.rearrange("p g q -> p (g q)"), b[:, :]), "wsT")
            ve.wait_ge(S["ld_param"], NPARAM * 16)
            for c in range(CT):
                last = V.tensor_scalar(wdiag[:, c, :], ident[0:NS, 0:NS], w00[:, c:c + 1], None, ALU.mult)
            last.then_inc(S["ws_ready"], 1)
            for n, (dst, rows) in enumerate(((convH.rearrange("p c s h -> p c (s h)"), NS * HC),
                                             (poolH.rearrange("p c s h -> p c (s h)"), NS * HP),
                                             (confH[:, :, 0:4, :].rearrange("p c s h -> p c (s h)"), 4 * HF),
                                             (confH[:, :, 4:8, :].rearrange("p c s h -> p c (s h)"), 4 * HF))):
                b = await_full(ve, ("hist", n))
                free(V.tensor_copy(dst, b[:, 0:CT * rows].rearrange("p (c r) -> p c r", c=CT)), ("hist", n))

            ada_out(3)
            b = await_full(ve, "modT")
            V.tensor_copy(S1[:].rearrange("p k r -> p (k r)"), b[:, 0:KT * NC_ROWS])
            free(V.tensor_scalar(G1[:].rearrange("p k r -> p (k r)"), b[:, KT * NC_ROWS:2 * KT * NC_ROWS], 1.0, None, ALU.add), "modT")
            await_freed(ve, "modT")
            await_freed(ve, "prow0")
            V.tensor_tensor(G1[:].rearrange("p (a c) r -> p a c r", a=2), G1[:].rearrange("p (a c) r -> p a c r", a=2),
                            prm[:, :, R_N1G:R_N1G + 2].rearrange("p c a -> p a c").unsqueeze(3).to_broadcast([P, 2, CT, NC_ROWS]),
                            ALU.mult).then_inc(S["g1_ready"], 1)
            ve.wait_ge(S["g1_ready"], 1)

            def h_low(k):
                ve.wait_ge(S["h_hi"], k + 1)
                V.tensor_tensor(as_r(hT[:, k, :]), hT[:, k, :], as_r(hT_hi[:, k, :]).bitcast(F32), ALU.subtract).then_inc(S["h_split"], 1)

            for k in range(KT):
                ve.wait_ge(S["h_prompt"], k + 1)
                b = await_full(ve, ("hT", k))
                free(V.tensor_tensor(hT[:, k, SEQ:TOK], b[:, SEQ:TOK], G1[:, k, 0:NS], ALU.mult), ("hT", k))
                await_freed(ve, ("hT", k))
                V.tensor_tensor(hT[:, k, SEQ:TOK], hT[:, k, SEQ:TOK], S1[:, k, 0:NS], ALU.add).then_inc(S["h_ready"], 1)
                if k:
                    h_low(k - 1)
            h_low(KT - 1)
            for t, (t0, n) in enumerate(TILES):
                await_freed(ve, ("v", 0, t))
                await_freed(ve, ("v", 1, t))
                link(V.bn_stats(bns[0:n, t, 0:6], v_sb[0:n, t, :]))
                last = V.bn_aggr(st[0:n, t, 4:6], bns[0:n, t, 0:6])
            last.then_inc(S["v_mean"], 1)
            ve.wait_ge(S["v_std"], 1)
            link(V.reciprocal(st[:, :, 7], st[:, :, 6]))
            for t, (t0, n) in enumerate(TILES):
                link(V.tensor_scalar(v_sb[0:n, t, :], v_sb[0:n, t, :], st[0:n, t, 4:5], st[0:n, t, 7:8], ALU.subtract, ALU.mult))
                link(V.tensor_tensor(v_sb[0:n, t, :], v_sb[0:n, t, :], lnv[0:n, 0, :], ALU.mult))
                last = V.tensor_tensor(v_sb[0:n, t, :], v_sb[0:n, t, :], lnv[0:n, 1, :], ALU.add)
            last.then_inc(S["v_ready"], 1)

            for c in range(CT):
                b = await_full(ve, ("z", 6, c))
                await_freed(ve, ("z", 7, c))
                free(V.tensor_tensor(gluP[:, c, HF:], b[:, 0:TOK], tmpT[:, c, :], ALU.mult), ("z", 6, c))
            for c in range(CT):
                b = await_full(ve, ("z", 4, c))
                await_freed(ve, ("z", 3, c))
                free(V.tensor_tensor(cgP[:, c, HC:], b[:, 0:TOK], tmpT[:, c, :], ALU.mult), ("z", 4, c))

            await_freed(ve, ("z", 4, CT - 1))
            taps = [0] * CT
            for h in range(HC + 1):
                for c in range(CT):
                    w = col(c, R_CONVW + h)
                    past = convH[:, c, :, h] if h < HC else cgP[:, c, HC + SEQ:]
                    if h == 0:
                        V.tensor_scalar(ybr[:, 1, c, 0:SEQ], cgP[:, c, 0:SEQ], w, None, ALU.mult)
                        taps[c] = mark(V.tensor_scalar(ybr[:, 1, c, SEQ:], past, w, None, ALU.mult))
                    else:
                        ve.wait_ge(S["dve_chain"], taps[c])
                        V.scalar_tensor_tensor(ybr[:, 1, c, 0:SEQ], cgP[:, c, h:h + SEQ], w, ybr[:, 1, c, 0:SEQ], ALU.mult, ALU.add)
                        taps[c] = mark(V.scalar_tensor_tensor(ybr[:, 1, c, SEQ:], past, w, ybr[:, 1, c, SEQ:], ALU.mult, ALU.add))

            for c in range(CT):
                win = 2 << c
                await_freed(ve, ("z", 5, c))
                src = zcP[:, c, :]
                for r in range(c + 1):
                    d = 1 << r
                    dst = sums[:, r % 2, :]
                    link(V.tensor_tensor(dst[:, 2 * d - 1:HP + SEQ], src[:, 2 * d - 1:HP + SEQ], src[:, d - 1:HP + SEQ - d], ALU.add))
                    src = dst
                own = zcP[:, c, HP:HP + SEQ]
                V.scalar_tensor_tensor(ybr[:, 2, c, win - 1:SEQ], src[:, HP + win - 1:HP + SEQ], 1.0 / win, own[:, win - 1:], ALU.mult, ALU.subtract)
                link(V.tensor_tensor(src[:, HP:HP + win - 1], src[:, HP:HP + win - 1], rc[:, 0:win - 1], ALU.mult))
                V.tensor_tensor(ybr[:, 2, c, 0:win - 1], src[:, HP:HP + win - 1], own[:, 0:win - 1], ALU.subtract)
                new = zcP[:, c, HP + SEQ:]
                part = prod[:, :, 0]
                if win > 2:
                    link(V.tensor_reduce(part, poolH[:, c, :, HP - win + 1:HP], AX.X, ALU.add))
                else:
                    link(V.tensor_copy(part, poolH[:, c, :, HP - 1]))
                link(V.tensor_tensor(part, part, new, ALU.add))
                V.scalar_tensor_tensor(ybr[:, 2, c, SEQ:], part, 1.0 / win, new, ALU.mult, ALU.subtract).then_inc(S["pooled_ready"], 1)

            for c in range(CT):
                b = await_full(ve, ("z", 2, c))
                free(V.tensor_tensor(ybr[:, 1, c, :], b[:, 0:TOK], ybr[:, 1, c, :], ALU.mult), ("z", 2, c))
            for c in range(CT):
                b = await_full(ve, ("sg", c))
                V.tensor_tensor(ybr[:, 0, c, 0:SEQ].rearrange("p (t q) -> p t q", t=2), b[:, 0:SEQ].rearrange("p (t q) -> p t q", t=2),
                                sgub[:, c:c + 1, :].to_broadcast([P, 2, P]), ALU.add)
                free(V.tensor_scalar(ybr[:, 0, c, SEQ:], b[:, SEQ:TOK], sgub[:, c, 0:1], None, ALU.add), ("sg", c))
                await_freed(ve, ("sg", c))
                await_freed(ve, ("z", 0, c))
                V.tensor_tensor(ybr[:, 0, c, :], ybr[:, 0, c, :], tmpT[:, c, :], ALU.mult).then_inc(S["ya_ready"], 1)
            for c in range(CT):
                b = await_full(ve, ("pw", c))
                free(V.tensor_scalar(ybr[:, 2, c, :], b[:, 0:TOK], col(c, R_PSC), None, ALU.mult), ("pw", c))

            taps = [0] * CT

            def conf_taps(h0, h1):
                for h in range(h0, h1):
                    for c in range(CT):
                        w = col(c, R_CONFW + h)
                        if h == 0:
                            taps[c] = mark(V.tensor_scalar(dcv[:, c, 0:SEQ], gluP[:, c, 0:SEQ], w, col(c, R_CONFB), ALU.mult, ALU.add))
                        else:
                            ve.wait_ge(S["dve_chain"], taps[c])
                            taps[c] = mark(V.scalar_tensor_tensor(dcv[:, c, 0:SEQ], gluP[:, c, h:h + SEQ], w, dcv[:, c, 0:SEQ], ALU.mult, ALU.add))

            for j in range(4, 12):
                if j == 4:
                    ve.wait_ge(S["ld_mod2"], 16)
                ada_out(j)
                if j == 9:
                    await_freed(ve, ("ada", 9, 1))
                    V.scalar_tensor_tensor(mod[:, 2 * D:3 * D], mod[:, 2 * D:3 * D], 1.0, bc[0:NC_ROWS, 2, :], ALU.add, ALU.mult).then_inc(S["g2_rows"], 1)
                conf_taps(4 * (j - 4), min(4 * (j - 3), HF + 1))
            for c in range(CT):
                w = prm[:, c, R_CONFW:R_CONFW + HF].unsqueeze(1).to_broadcast([P, NS, HF])
                link(V.tensor_tensor(prod, confH[:, c, :, :], w, ALU.mult))
                link(V.tensor_reduce(dcv[:, c, SEQ:], prod, AX.X, ALU.add))
                link(V.scalar_tensor_tensor(dcv[:, c, SEQ:], gluP[:, c, HF + SEQ:], col(c, R_CONFW + HF), dcv[:, c, SEQ:], ALU.mult, ALU.add))
                last = V.tensor_scalar(dcv[:, c, SEQ:], dcv[:, c, SEQ:], col(c, R_CONFB), None, ALU.add)
            last.then_inc(S["dconv_ready"], 1)

            for n, k in enumerate(BR_ORDER):
                if k == 0:
                    b = await_full(ve, "cmean")
                    ve.wait_ge(S["dconv_ready"], 1)
                    free(V.tensor_tensor(dcv[:, :, :], dcv[:, :, :], b[:, 0:TOK].unsqueeze(1).to_broadcast([P, CT, TOK]), ALU.subtract), "cmean")
                if k == 3:
                    await_freed(ve, "cvar")
                    link(V.reciprocal(stat[:, 1, :], stat[:, 0, :]))
                    V.tensor_tensor(dcv[:, :, :], dcv[:, :, :], stat[:, 1:2, :].to_broadcast([P, CT, TOK]), ALU.mult).then_inc(S["dn_ready"], 1)
                ve.wait_ge(S["y_hi_ready"], n + 1)
                V.tensor_tensor(as_r(ybr[:, k]), ybr[:, k], as_r(y_hi).bitcast(F32), ALU.subtract).then_inc(S["y_split"], 1)
                for d in range(KT):
                    b = await_full(ve, ("pr", k, d))
                    await_freed(ve, ("zg", k, d))
                    if n == 0:
                        free(V.tensor_tensor(mT[:, d, :], b[:, 0:TOK], sg[:, d, :], ALU.mult), ("pr", k, d))
                    else:
                        free(V.tensor_tensor(sg[:, d, :], b[:, 0:TOK], sg[:, d, :], ALU.mult), ("pr", k, d))
                        await_freed(ve, ("pr", k, d))
                        ins = V.tensor_tensor(mT[:, d, :], mT[:, d, :], sg[:, d, :], ALU.add)
                        if n == 3:
                            ins.then_inc(S["mrg_ready"], 1)
                        else:
                            ins.then_inc(S["sg_used"], 1)
                if 0 < n < 3:
                    ve.wait_ge(S["sg_used"], n * KT)
            for d in range(KT):
                ve.wait_ge(S["m_hi_ready"], d + 1)
                V.tensor_tensor(as_r(mT[:, d, :]), mT[:, d, :], as_r(m_hi[:, d, :]).bitcast(F32), ALU.subtract).then_inc(S["m_split"], 1)

            await_freed(ve, ("bc", 0, 1))
            await_freed(ve, ("bc", 2, 1))
            for m, t in enumerate(MIX_ORDER):
                t0, n = TILES[t]
                for j in range(2):
                    b = await_full(ve, ("mix", t, j))
                    a = slice(j * BLK, (j + 1) * BLK)
                    free(V.tensor_tensor(xn[0:n, t, a], b[0:n, :], rows_of(0, t, n, a.start, a.stop), ALU.mult), ("mix", t, j))
                    await_freed(ve, ("mix", t, j))
                    V.tensor_tensor(x_sb[0:n, t, a], x_sb[0:n, t, a], xn[0:n, t, a], ALU.add).then_inc(S["x2_ready"], 1)
                ve.wait_ge(S["x2_ready"], 2 * m + 2)
                mark(V.tensor_tensor(xn[0:n, t, :], x_sb[0:n, t, :], rows_of(2, t, n, 0, D), ALU.mult))
                ve.wait_ge(S["x2_sq"], m + 1)
                link(V.reciprocal(st[0:n, t, 2:3], st[0:n, t, 1:2]))
                V.scalar_tensor_tensor(xn[0:n, t, :], xn[0:n, t, :], st[0:n, t, 2:3], rows_of(1, t, n, 0, D), ALU.mult, ALU.add).then_inc(S["h2_ready"], 1)

            await_freed(ve, "logit")
            link(V.tensor_tensor(bsd[:], sc[:], rtb[:].unsqueeze(1).to_broadcast([P, 3, NE]), ALU.add))
            for t in range(3):
                for q in range(NG):
                    last = V.max(gm[:, t, q, :], bsd[:, t, q * 8:(q + 1) * 8])
            link(last)
            link(V.tensor_tensor(gs[:], gm[:, :, :, 0], gm[:, :, :, 1], ALU.add))
            for t in range(3):
                mine = gs[:, t, :].unsqueeze(2).to_broadcast([P, NG, NG])
                other = gs[:, t, :].unsqueeze(1).to_broadcast([P, NG, NG])
                V.tensor_tensor(cmp_[:, t], other, mine, ALU.is_gt)
                last = V.tensor_tensor(cmp2[:, t], other, mine, ALU.is_equal)
            link(last)
            link(V.tensor_tensor(cmp2[:], cmp2[:], trig[:].unsqueeze(1).to_broadcast([P, 3, NG, NG]), ALU.mult))
            link(V.tensor_tensor(cmp_[:], cmp_[:], cmp2[:], ALU.add))
            link(V.tensor_reduce(gs[:], cmp_[:], AX.X, ALU.add))
            link(V.tensor_scalar(gs[:], gs[:], float(TOPG), None, ALU.is_lt))
            link(V.tensor_scalar(gm[:, :, :, 0], gs[:], -1.0, 1e30, ALU.add, ALU.mult))
            sel_g = gs[:].unsqueeze(3).to_broadcast([P, 3, NG, 8])
            pen_g = gm[:, :, :, 0:1].to_broadcast([P, 3, NG, 8])
            link(V.tensor_tensor(msk[:].rearrange("p t (g e) -> p t g e", g=NG), bsd[:].rearrange("p t (g e) -> p t g e", g=NG), sel_g, ALU.mult))
            link(V.tensor_tensor(msk[:].rearrange("p t (g e) -> p t g e", g=NG), msk[:].rearrange("p t (g e) -> p t g e", g=NG), pen_g, ALU.add))
            for t in range(3):
                last = V.max(gm[:, t, 0, :], msk[:, t, :])
            link(last)
            for t in range(3):
                last = V.match_replace(sel[:, t, :], gm[:, t, 0, :], msk[:, t, :], -3e30)
            link(last)
            link(V.tensor_tensor(sel[:], sel[:], msk[:], ALU.not_equal))
            V.tensor_tensor(sel[:], sel[:], valid[:].unsqueeze(2).to_broadcast([P, 3, NE]), ALU.mult).then_inc(S["sel_ready"], 1)
            ve.wait_ge(S["sel_ready"], 1)

            link(V.tensor_tensor(msk[:], sc[:], sel[:], ALU.mult))
            link(V.tensor_reduce(st[:, :, 3], msk[:], AX.X, ALU.add))
            link(V.tensor_scalar(st[:, :, 3], st[:, :, 3], 1e-38, None, ALU.max))
            link(V.reciprocal(st[:, :, 3], st[:, :, 3]))
            for t in range(3):
                V.tensor_scalar(tab[:, t, :, 1], msk[:, t, :], st[:, t, 3:4], ROUTED_SCALE, ALU.mult, ALU.mult)
            b = await_full(ve, "slot")
            link(V.tensor_scalar(posm[:], sel[:], -1.0, 1e6, ALU.add, ALU.mult))
            V.tensor_reduce(cnt_f[:], b[:, 3 * NE:4 * NE], AX.X, ALU.max)
            free(V.tensor_tensor(posm[:].rearrange("p t e -> p (t e)"), b[:, 0:3 * NE], posm[:].rearrange("p t e -> p (t e)"), ALU.add), "slot")
            await_freed(ve, "slot")
            V.tensor_copy(cnt_i[:], cnt_f[:]).then_inc(S["cnt_ready"], 1)

            def one_hot(i, j):
                e = UNROLL * i + j
                need(ve, S["list_done"], e - 1)
                for t in range(3):
                    p = posm[:, t, e:e + 1] if isinstance(e, int) else posm[:, t, bass.ds(e, 1)]
                    last = V.tensor_scalar(oh[:, j % 2, t, :], iota_f[:], p, None, ALU.is_equal)
                last.then_inc(S["oh_ready"], 1)

            def list_out(i, j):
                e = UNROLL * i + j
                ve.wait_ge(S["list_done"], e + 1)
                need(ve, S["scatter_row_ready"], e - 3)
                need(ve, S["act_ready"], e - 3)
                V.tensor_scalar(idx[:, j, :], psum[:, LIST_BANK, 0:1], BIG, None, ALU.add)
                V.tensor_copy(gcol[:, j, :], psum[:, LIST_BANK, 1:2]).then_inc(S["lst_ready"], 1)

            def keep_scatter_row(i, j):
                e = UNROLL * i + j
                ve.wait_ge(S["lst_ready"], e + 1)
                need(ve, scattered[j % 2], 16 * (2 * i + j // 2 - 1))
                V.tensor_copy(scatter_row[:, j, :], idx[:, j, :]).then_inc(S["scatter_row_ready"], 1)

            def up_low(i, j, n):
                e = UNROLL * i + j
                hi, lo = piece_hi(place(e), n), piece(j, n)
                ve.wait_ge(S["up_hi"], 4 * e + n + 1)
                V.tensor_tensor(as_r(lo), lo, as_r(hi).bitcast(F32), ALU.subtract).then_inc(S["up_lo"], 1)

            def down_low(i, j):
                e = UNROLL * i + j
                hi, lo = piece_hi(place(e), 4), piece(j, 4)
                ve.wait_ge(S["down_hi"], 2 * e + 1)
                V.tensor_tensor(as_r(lo), lo, as_r(hi).bitcast(F32), ALU.subtract).then_inc(S["down_lo_dve"], 1)

            def rows_low(i, j):
                e = UNROLL * i + j
                ve.wait_ge(S["xgt_hi"], e + 1)
                V.tensor_tensor(as_r(xgT_lo), psum[:, 5:7, :].rearrange("p b (k c) -> p (b k) c", k=4), as_r(xgT_hi).bitcast(F32),
                                ALU.subtract).then_inc(S["xgt_lo"], 1)

            def act_low(i, j):
                e = UNROLL * i + j
                ve.wait_ge(S["actT_hi_ready"], e + 1)
                V.tensor_tensor(as_r(actT_lo[:, j % 2]), psum[:, 2, 0:2 * P].rearrange("p (h c) -> p h c", h=2),
                                as_r(actT_hi[:, j % 2]).bitcast(F32), ALU.subtract).then_inc(S["actT_ready"], 1)

            def gated(i, j):
                e = UNROLL * i + j
                ve.wait_ge(S["silu_ready"], e + 1)
                need(ve, S["tact_done"], e - 1)
                V.scalar_tensor_tensor(act[:, j % 2, :], psum[:, j % 2, FE:2 * FE], gcol[:, j, :], silu[:, j % 2, :],
                                       ALU.mult, ALU.mult).then_inc(S["act_ready"], 1)

            def y_out(i, j):
                e = UNROLL * i + j
                ve.wait_ge(S["down_done"], 2 * e + 2)
                need(ve, scattered[j % 2], 16 * (2 * i + j // 2))
                V.tensor_copy(y_rows[:, j % 2, BLK:2 * BLK], psum[:, 4, :]).then_inc(S["ys_dve"], 1)

            def body(i, first=False, last=False):
                for j in range(UNROLL):
                    prev = not (first and j == 0)
                    pi, pj = (i if j else i - 1), (j - 1) % UNROLL
                    ni, nj = (i if j < 3 else i + 1), (j + 1) % UNROLL
                    up_low(i, j, 2)
                    if not last:
                        one_hot(i + 1, j)
                    up_low(i, j, 3)
                    if prev:
                        down_low(pi, pj)
                        act_low(pi, pj)
                    keep_scatter_row(i, j)
                    gated(i, j)
                    if not (last and j == UNROLL - 1):
                        up_low(ni, nj, 0)
                        rows_low(ni, nj)
                        up_low(ni, nj, 1)
                    if prev:
                        y_out(pi, pj)
                    else:
                        take_shared()
                    if not last:
                        list_out(i + 1, j)

            def take_shared():
                await_freed(ve, ("bc", 3, 1))
                for t, (t0, n) in enumerate(TILES):
                    for h in range(2):
                        a = slice(h * BLK, (h + 1) * BLK)
                        ve.wait_ge(S["shared_done"], 2 * t + h + 1)
                        V.tensor_tensor(sh_part[0:n, h, :], psum[0:n, 3 + h, :], rows_of(3, t, n, a.start, a.stop), ALU.mult).then_inc(S["shared_taken"], 1)
                        ve.wait_ge(S["shared_taken"], 2 * t + h + 1)
                        mark(V.tensor_tensor(x_sb[0:n, t, a], x_sb[0:n, t, a], sh_part[0:n, h, :], ALU.add))
                        if h:
                            ve.wait_ge(S["dve_chain"], n_chain[0])

            def shared_act(j):
                b = await_full(ve, ("shared_up", j))
                await_freed(ve, ("shared_gate", j))
                free(V.tensor_tensor(sh_actT[:, j, :], b[:, 0:TOK], sh_silu[:, j, :], ALU.mult), ("shared_up", j))

            one_hot(0, 0)
            one_hot(0, 1)
            list_out(0, 0)
            shared_act(0)
            one_hot(0, 2)
            list_out(0, 1)
            one_hot(0, 3)
            list_out(0, 2)
            shared_act(1)
            list_out(0, 3)
            up_low(0, 0, 0)
            rows_low(0, 0)
            up_low(0, 0, 1)
            body(0, first=True)
            with ve.Fori(1, NE // UNROLL - 1) as i:
                body(i)
            body(NE // UNROLL - 1, last=True)
            down_low(NE // UNROLL - 1, UNROLL - 1)
            act_low(NE // UNROLL - 1, UNROLL - 1)
            y_out(NE // UNROLL - 1, UNROLL - 1)

            def extra(r, e, n):
                for t in range(3):
                    last = V.tensor_scalar(oh[:, 0, t, :], iota_f[:], posm[:, t, bass.ds(e, 1)], float(-CAP * r), ALU.subtract, ALU.is_equal)
                last.then_inc(S["x_oh"], 1)
                ve.wait_ge(S["x_list"], n + 1)
                V.tensor_scalar(idx[:, 0, :], psum[:, LIST_BANK, 0:1], BIG, None, ALU.add)
                V.tensor_copy(gcol[:, 0, :], psum[:, LIST_BANK, 1:2]).then_inc(S["x_idx"], 1)
                ve.wait_ge(S["x_xt"], n + 1)
                V.tensor_copy(xgT_hi[:, :, :], psum[:, 5:7, :].rearrange("p b (k c) -> p (b k) c", k=4)).then_inc(S["x_xgt"], 1)
                ve.wait_ge(S["x_silu"], n + 1)
                V.scalar_tensor_tensor(act[:, 0, :], psum[:, 0, FE:2 * FE], gcol[:, 0, :], silu[:, 0, :], ALU.mult, ALU.mult).then_inc(S["x_act"], 1)
                ve.wait_ge(S["x_dn"], n + 1)
                V.tensor_copy(y_rows[:, 0, :].rearrange("p (b n) -> p b n", b=2), psum[:, 3:5, :]).then_inc(S["x_y"], 1)
                ve.wait_ge(S["x_sc"], 16 * n + 16)

            ve.wait_ge(S["even_load"], 3 * 16)
            for t, (t0, n) in enumerate(TILES):
                link(V.tensor_tensor(fin_y[0:n, 0, t], fin_y[0:n, 0, t], rows_of(3, t, n, 0, D), ALU.mult))
                V.tensor_tensor(x_sb[0:n, t, :], x_sb[0:n, t, :], fin_y[0:n, 0, t], ALU.add).then_inc(S["even_taken"], 1)
            extra_passes(ve, extra)
            for t in range(2):
                n = TILES[t][1]
                ve.wait_ge(fin_ld[t], 16)
                link(V.tensor_tensor(fin_y[0:n, 1, t], fin_y[0:n, 1, t], rows_of(3, t, n, 0, D), ALU.mult))
                ve.wait_ge(S["even_taken"], t + 1)
                V.tensor_tensor(x_sb[0:n, t, :], x_sb[0:n, t, :], fin_y[0:n, 1, t], ALU.add).then_inc(S["fin_red"], 1)
            ve.wait_ge(S["ld_fin"], 16)
            for t, (t0, n) in enumerate(TILES):
                ve.wait_ge(S["fin_sq"], t + 1)
                link(V.reciprocal(st[0:n, t, 2:3], st[0:n, t, 1:2]))
                V.scalar_tensor_tensor(x_sb[0:n, t, :], x_sb[0:n, t, :], st[0:n, t, 2:3], fing[0:n, :], ALU.mult, ALU.mult).then_inc(S["fin_ready"], 1)


_INS = ["x_prompt", "x_sample", "state_conv", "state_pool", "state_conf", "c_prompt", "c_sample",
        "ada_w", "ada_b", "norm1_g", "norm2_g", "w_in", "sgu_ln_g", "sgu_ln_b", "sgu_w", "sgu_b",
        "conv_w", "pool_w", "pool_scale", "conf_w", "conf_b", "conf_ln_g", "conf_ln_b",
        "w_branch", "w_out", "router_w", "router_bias", "e_gate", "e_up", "e_down",
        "s_gate", "s_up", "s_down", "final_g"]
_OUTS = [(1, SEQ, D), (NS, 1, D), (1, 1, HC, BR), (1, 1, HP, BR), (1, 1, HF, BR),
         (1, NS, HC, BR), (1, NS, HP, BR), (1, NS, HF, BR), (1, NS, 1, BR)]


def kernel(**inputs):
    import concourse.bacc as _bacc
    from concourse.bass_utils import run_bass_kernel_spmd as _run

    nc = _bacc.Bacc("TRN2", target_bir_lowering=False, num_devices=1)
    arrays, args = {}, []
    for name in _INS:
        a = np.ascontiguousarray(inputs[name])
        arrays[f"in_{name}"] = a
        args.append(nc.dram_tensor(f"in_{name}", a.shape, F32, kind="ExternalInput").ap())
    for i, shape in enumerate(_OUTS):
        args.append(nc.dram_tensor(f"out_{i}", shape, F32, kind="ExternalOutput").ap())
    args.append(nc.dram_tensor("h_table", (TOK, D), F32, kind="Internal").ap())
    args.append(nc.dram_tensor("y_even", (TOK, D), F32, kind="Internal").ap())
    args.append(nc.dram_tensor("y_odd", (TOK, D), F32, kind="Internal").ap())
    bass_decoder_step(nc, *args)
    r = _run(nc, [arrays], core_ids=[0])
    return tuple(r.results[0][f"out_{i}"] for i in range(len(_OUTS)))
```
